# Optimizing a Trainium2 kernel written in Bass

```python
import functools
import jax, jax.numpy as jnp
from jax import lax
import numpy as np

D_MODEL = 1024
BATCH = 1
SEQ = 512
DEPTH = 1
DEC_BATCH = 1
DEC_SEQ = 32
PAST_LEN = 1024

CHUNK = 64
D_MIX = D_MODEL
RET_HEADS = 4
RET_DK = 128
RET_DV = 128
SB_HEADS = 4
SB_DH = 128
SB_BLOCK = 128
ROPE_BASE = 10000.0
NORM_EPS = 1e-6
RET_W = RET_HEADS * RET_DK
RET_WV = RET_HEADS * RET_DV
SB_W = SB_HEADS * SB_DH
IN_COLS = 2 * RET_W + 2 * RET_WV + 3 * SB_W
PEER_HEADS = 8
PEER_NKEYS = 128
PEER_EXPERTS = PEER_NKEYS * PEER_NKEYS
PEER_DKEY = 256
PEER_TOPK = 16
PEER_TOKBLOCK = 256

kernel_name = 'hymba_retention_stickbreaking_peer_stream'

def rmsnorm(x, g):
    xf = x.astype(jnp.float32)
    y = xf * lax.rsqrt(jnp.mean(xf * xf, axis=-1, keepdims=True) + NORM_EPS)
    return (y * g.astype(jnp.float32)).astype(x.dtype)

def adaln(c, w_ada, b_ada):
    mod = jax.nn.silu(c) @ w_ada + b_ada
    return jnp.split(mod[:, None, :], 6, axis=-1)

def modulate(x, g, shift, scale):
    return rmsnorm(x, g) * (1 + scale) + shift

def rope(x, pos):
    half = x.shape[-1] // 2
    inv_freq = ROPE_BASE ** (-jnp.arange(half, dtype=jnp.float32) / half)
    ang = pos.astype(jnp.float32)[:, None] * inv_freq[None, :]
    cos = jnp.cos(ang)[None, :, None, :].astype(x.dtype)
    sin = jnp.sin(ang)[None, :, None, :].astype(x.dtype)
    x1, x2 = x[..., :half], x[..., half:]
    return jnp.concatenate([x1 * cos - x2 * sin, x1 * sin + x2 * cos], axis=-1)

def retention_log_decay():
    return jnp.log1p(-jnp.exp2(-5.0 - jnp.arange(RET_HEADS, dtype=jnp.float32)))

def split_heads(proj):
    B, L = proj.shape[:2]
    c0 = RET_W
    c1 = 2 * RET_W
    c2 = c1 + RET_WV
    c3 = c2 + RET_WV
    c4 = c3 + SB_W
    c5 = c4 + SB_W
    rq, rk, rv, rg, sq, sk, sv = jnp.split(proj, [c0, c1, c2, c3, c4, c5], axis=-1)
    return (rq.reshape(B, L, RET_HEADS, RET_DK), rk.reshape(B, L, RET_HEADS, RET_DK),
            rv.reshape(B, L, RET_HEADS, RET_DV), rg,
            sq.reshape(B, L, SB_HEADS, SB_DH), sk.reshape(B, L, SB_HEADS, SB_DH),
            sv.reshape(B, L, SB_HEADS, SB_DH))

def retention_chunk(S, q, k, v):
    L = q.shape[1]
    log_g = retention_log_decay()
    idx = jnp.arange(L, dtype=jnp.float32)
    diff = idx[:, None] - idx[None, :]
    causal = diff >= 0
    intra = jnp.where(causal[None], jnp.exp(jnp.where(causal, diff, 0.0)[None] * log_g[:, None, None]), 0.0)
    scores = jnp.einsum('bihd,bjhd->bhij', q, k) * intra.astype(q.dtype)[None]
    o = jnp.einsum('bhij,bjhe->bihe', scores, v)
    q_decay = jnp.exp((idx[:, None] + 1.0) * log_g[None, :]).astype(q.dtype)
    o = o + jnp.einsum('bihd,bhde->bihe', q, S) * q_decay[None, :, :, None]
    k_decay = jnp.exp((L - 1.0 - idx)[:, None] * log_g[None, :]).astype(k.dtype)
    S_new = (jnp.exp(L * log_g)[None, :, None, None].astype(S.dtype) * S
             + jnp.einsum('bjhd,bjhe->bhde', k * k_decay[None, :, :, None], v))
    return o, S_new

def retention_prompt(q, k, v):
    B, L, H, dk = q.shape
    dv = v.shape[-1]
    nc = L // CHUNK

    def to_chunks(t):
        return t.reshape(B, nc, CHUNK, H, t.shape[-1]).transpose(1, 0, 2, 3, 4)

    def step(S, qkv):
        qc, kc, vc = qkv
        o, S = retention_chunk(S, qc, kc, vc)
        return S, o

    S0 = jnp.zeros((B, H, dk, dv), q.dtype)
    S, o = lax.scan(step, S0, (to_chunks(q), to_chunks(k), to_chunks(v)))
    o = o.transpose(1, 0, 2, 3, 4).reshape(B, L, H, dv)
    return o, S

def stick_breaking_block(q, k, v, q_pos, k_pos):
    z = jnp.einsum('bqhd,bkhd->bhqk', q, k).astype(jnp.float32) * (SB_DH ** -0.5)
    mask = (k_pos[None, :] < q_pos[:, None])[None, None]
    log_beta = jax.nn.log_sigmoid(z)
    log_keep = jnp.where(mask, jax.nn.log_sigmoid(-z), 0.0)
    after = lax.cumsum(log_keep, axis=3, reverse=True) - log_keep
    A = jnp.where(mask, jnp.exp(log_beta + after), 0.0)
    return jnp.einsum('bhqk,bkhd->bqhd', A.astype(v.dtype), v)

def stick_breaking_prompt(q, k, v):
    L = q.shape[1]
    outs = []
    for i in range(L // SB_BLOCK):
        s, e = i * SB_BLOCK, (i + 1) * SB_BLOCK
        outs.append(stick_breaking_block(q[:, s:e], k[:, :e], v[:, :e], jnp.arange(s, e), jnp.arange(e)))
    return jnp.concatenate(outs, axis=1)

def mix_first_chunk(rq, rk, rv, sq, sk, sv):
    ro, s_ret = retention_prompt(rq, rk, rv)
    so = stick_breaking_prompt(sq, sk, sv)
    return ro, so, (s_ret, sk, sv)

def mix_later_chunk(s_prev, k_past, v_past, rq, rk, rv, sq, sk, sv):
    P = k_past.shape[1]
    Ls = sq.shape[1]
    ro, s_new = retention_chunk(s_prev, rq, rk, rv)
    k_all = jnp.concatenate([k_past, sk], axis=1)
    v_all = jnp.concatenate([v_past, sv], axis=1)
    so = stick_breaking_block(sq, k_all, v_all, P + jnp.arange(Ls), jnp.arange(P + Ls))
    return ro, so, (s_new, sk, sv)

def merge_groups(ro, rg, so, ret_norm_g, w_out):
    B, L = ro.shape[:2]
    of = ro.astype(jnp.float32)
    mu = jnp.mean(of, axis=-1, keepdims=True)
    cen = of - mu
    on = (cen * lax.rsqrt(jnp.mean(cen * cen, axis=-1, keepdims=True) + NORM_EPS)).astype(ro.dtype)
    ret = on.reshape(B, L, RET_WV) * ret_norm_g * jax.nn.silu(rg)
    return jnp.concatenate([ret, so.reshape(B, L, SB_W)], axis=-1) @ w_out

def peer_ffn(x, w_query, sub_keys, expert_u, expert_v):
    n = x.shape[0]
    pad = (-n) % PEER_TOKBLOCK
    blocks = jnp.pad(x, ((0, pad), (0, 0))).reshape(-1, PEER_TOKBLOCK, D_MODEL)

    def one(xb):
        T = xb.shape[0]
        q = (xb @ w_query).reshape(T, PEER_HEADS, 2, PEER_DKEY // 2)
        s = jnp.einsum('thpd,phkd->thpk', q, sub_keys).astype(jnp.float32)
        sv_, si = lax.top_k(s, PEER_TOPK)
        cand = (sv_[:, :, 0, :, None] + sv_[:, :, 1, None, :]).reshape(T, PEER_HEADS, PEER_TOPK * PEER_TOPK)
        cand_idx = (si[:, :, 0, :, None] * PEER_NKEYS + si[:, :, 1, None, :]).reshape(T, PEER_HEADS, PEER_TOPK * PEER_TOPK)
        top_s, pos = lax.top_k(cand, PEER_TOPK)
        idx = jnp.take_along_axis(cand_idx, pos, axis=-1)
        g = jax.nn.softmax(top_s, axis=-1)
        u = expert_u[idx]
        act = jax.nn.gelu(jnp.einsum('td,thkd->thk', xb, u).astype(jnp.float32))
        return jnp.einsum('thk,thkd->td', (g * act).astype(xb.dtype), expert_v[idx])

    return lax.map(one, blocks).reshape(-1, D_MODEL)[:n]

def trunk_layer(h, c, pos, token_mix, w_ada, b_ada, norm1_g, w_in, ret_norm_g, w_out,
                norm2_g, peer_w_query, peer_sub_keys, peer_u, peer_v):
    sh1, sc1, gt1, sh2, sc2, gt2 = adaln(c, w_ada, b_ada)
    a = modulate(h, norm1_g, sh1, sc1)
    rq, rk, rv, rg, sq, sk, sv = split_heads(a @ w_in)
    rq = rope(rq, pos) * (RET_DK ** -0.5)
    rk = rope(rk, pos)
    ro, so, new_state = token_mix(rq, rk, rv, sq, sk, sv)
    h = h + gt1 * merge_groups(ro, rg, so, ret_norm_g, w_out)
    b = modulate(h, norm2_g, sh2, sc2)
    B, L, D = b.shape
    h = h + gt2 * peer_ffn(b.reshape(B * L, D), peer_w_query, peer_sub_keys, peer_u, peer_v).reshape(B, L, D)
    return h, new_state

def setup_inputs(seed: int = 0) -> dict:
    key = jax.random.key(seed)
    ks = jax.random.split(key, 20)

    def nrm(k, shape, s):
        return jax.random.normal(k, shape, jnp.float32) * s

    return {
        'x_prompt': nrm(ks[0], (BATCH, SEQ, D_MODEL), 1.0),
        'x_sample': nrm(ks[1], (DEC_BATCH, DEC_SEQ, D_MODEL), 1.0),
        'c_prompt': nrm(ks[2], (BATCH, D_MODEL), 1.0),
        'c_sample': nrm(ks[3], (DEC_BATCH, D_MODEL), 1.0),
        'state_ret': nrm(ks[4], (DEPTH, DEC_BATCH, RET_HEADS, RET_DK, RET_DV), 1.0),
        'cache_sb_k': nrm(ks[5], (DEPTH, DEC_BATCH, PAST_LEN, SB_HEADS, SB_DH), 1.0),
        'cache_sb_v': nrm(ks[6], (DEPTH, DEC_BATCH, PAST_LEN, SB_HEADS, SB_DH), 1.0),
        'w_ada': nrm(ks[7], (DEPTH, D_MODEL, 6 * D_MODEL), 0.5 * D_MODEL ** -0.5),
        'b_ada': nrm(ks[8], (DEPTH, 6 * D_MODEL), 0.01),
        'norm1_g': 1.0 + nrm(ks[9], (DEPTH, D_MODEL), 0.02),
        'w_in': nrm(ks[10], (DEPTH, D_MODEL, IN_COLS), D_MODEL ** -0.5),
        'ret_norm_g': 1.0 + nrm(ks[11], (DEPTH, RET_WV), 0.02),
        'w_out': nrm(ks[12], (DEPTH, D_MIX, D_MODEL), D_MIX ** -0.5),
        'norm2_g': 1.0 + nrm(ks[13], (DEPTH, D_MODEL), 0.02),
        'peer_w_query': nrm(ks[14], (DEPTH, D_MODEL, PEER_HEADS * PEER_DKEY), D_MODEL ** -0.5),
        'peer_sub_keys': nrm(ks[15], (DEPTH, 2, PEER_HEADS, PEER_NKEYS, PEER_DKEY // 2), (PEER_DKEY // 2) ** -0.5),
        'peer_u': nrm(ks[16], (DEPTH, PEER_EXPERTS, D_MODEL), D_MODEL ** -0.5),
        'peer_v': nrm(ks[17], (DEPTH, PEER_EXPERTS, D_MODEL), 0.5),
        'final_norm_g': 1.0 + nrm(ks[18], (D_MODEL,), 0.02),
    }

def reference(x_prompt, x_sample, c_prompt, c_sample, state_ret, cache_sb_k, cache_sb_v,
              w_ada, b_ada, norm1_g, w_in, ret_norm_g, w_out, norm2_g,
              peer_w_query, peer_sub_keys, peer_u, peer_v, final_norm_g):
    hp, hs = x_prompt, x_sample
    pos_p = jnp.arange(x_prompt.shape[1])
    pos_s = cache_sb_k.shape[2] + jnp.arange(x_sample.shape[1])
    ret_p, k_p, v_p, ret_s, k_s, v_s = [], [], [], [], [], []
    for l in range(DEPTH):
        lp = (w_ada[l], b_ada[l], norm1_g[l], w_in[l], ret_norm_g[l], w_out[l], norm2_g[l],
              peer_w_query[l], peer_sub_keys[l], peer_u[l], peer_v[l])
        hp, (sp_, kp_, vp_) = trunk_layer(hp, c_prompt, pos_p, mix_first_chunk, *lp)
        mix_s = functools.partial(mix_later_chunk, state_ret[l], cache_sb_k[l], cache_sb_v[l])
        hs, (ss_, ks_, vs_) = trunk_layer(hs, c_sample, pos_s, mix_s, *lp)
        ret_p.append(sp_)
        k_p.append(kp_)
        v_p.append(vp_)
        ret_s.append(ss_)
        k_s.append(ks_)
        v_s.append(vs_)
    y_prompt = rmsnorm(hp, final_norm_g)
    y_sample = rmsnorm(hs, final_norm_g)
    return (y_prompt, y_sample,
            jnp.stack(ret_p), jnp.stack(k_p), jnp.stack(v_p),
            jnp.stack(ret_s), jnp.stack(k_s), jnp.stack(v_s))


_drawn_inputs = setup_inputs


def setup_inputs(seed=0):
    import zlib

    import numpy as np

    out = dict(_drawn_inputs(seed))
    spreads = {}
    factors = {'cache_sb_k': 3.719, 'ret_norm_g': 8.0, 'norm2_g': 4.443, 'final_norm_g': 2.889}
    for name, (base, spread) in spreads.items():
        noise = np.random.default_rng([zlib.crc32(name.encode()), seed]).standard_normal(out[name].shape)
        drawn = base * np.exp(spread * noise) if base else spread * noise
        out[name] = __import__('jax').numpy.asarray(drawn.astype(out[name].dtype))
    for name, factor in factors.items():
        out[name] = (out[name] * factor).astype(out[name].dtype)
    return out
```

```python
from contextlib import ExitStack

import numpy as np

import concourse.bass as bass
from concourse import mybir

F32 = mybir.dt.float32
F32R = mybir.dt.float32r
U32 = mybir.dt.uint32
ALU = mybir.AluOpType
ACT = mybir.ActivationFunctionType
AX_X = mybir.AxisListType.X

P = 128
D = 1024
KD = D // P
TP, TS = 512, 32
T = TP + TS
HT = T // 2
TILES = [(0, 128), (128, 128), (256, 128), (384, 128), (512, 32)]
NH = 4
PAST = 1024
NPB = PAST // P
QB = TP // P
EPS = 1e-6
NIN = 28
RQ, RK, RV, RG, SQ, SK, SV = (4 * n for n in range(7))
PH = 8
NK = 128
TOPK = 16
JB = 4
NJB = NK // JB
TB = 32
SCALE = P ** -0.5
NEG = -1.0e30
CREDIT = 2

C_ID, C_TRI, C_MASK, C_MIN, C_IOTA, C_KDEC = 0, 128, 256, 384, 512, 640
C_N = C_KDEC + NH * 5
M_DT, M_COS, M_SIN, M_QDEC = 0, NH * TP, NH * TP + T, NH * TP + 2 * T
M_N = M_QDEC + NH * TS
R_C, R_N1, R_N2, R_FG, R_RG, R_B, R_N = 0, 16, 24, 32, 40, 44, 92


def shape_constants():
    i = np.arange(P)
    small = np.zeros((P, C_N), np.float32)
    small[:, C_ID:C_ID + P] = np.eye(P)
    small[:, C_TRI:C_TRI + P] = -(i[:, None] >= i[None, :]).astype(np.float32)
    small[:, C_MASK:C_MASK + P] = (i[:, None] < i[None, :])
    small[:, C_MIN:C_MIN + P] = np.where(i[:, None] < i[None, :], 0.0, NEG)
    small[:, C_IOTA:C_IOTA + P] = i[None, :]
    log_g = np.log1p(-np.exp2(-5.0 - np.arange(NH)))
    for b, (t0, n) in enumerate(TILES):
        last = TP - 1 - t0 if t0 < TP else TS - 1
        for h in range(NH):
            left = last - i
            small[:, C_KDEC + b * NH + h] = np.where(left >= 0, np.exp(np.maximum(left, 0) * log_g[h]), 0.0)
    mix = np.zeros((P, M_N), np.float32)
    x = np.arange(TP)
    for h in range(NH):
        gap = x[None, :] - i[:, None]
        mix[:, M_DT + h * TP:M_DT + (h + 1) * TP] = np.where(gap >= 0, np.exp(np.maximum(gap, 0) * log_g[h]), 0.0)
        mix[:, M_QDEC + h * TS:M_QDEC + (h + 1) * TS] = SCALE * np.exp((np.arange(TS) + 1.0) * log_g[h])[None, :]
    half = P // 2
    inv = np.power(np.float32(10000.0), -np.arange(half, dtype=np.float32) / np.float32(half)).astype(np.float32)
    pos = np.concatenate([np.arange(TP), PAST + np.arange(TS)]).astype(np.float32)
    ang = (inv[:, None] * pos[None, :]).astype(np.float32)
    mix[:half, M_COS:M_COS + T] = mix[half:, M_COS:M_COS + T] = np.cos(ang)
    mix[:half, M_SIN:M_SIN + T] = -np.sin(ang)
    mix[half:, M_SIN:M_SIN + T] = np.sin(ang)
    return small, mix


def build(nc, x_prompt, x_sample, c_prompt, c_sample, state_ret, cache_sb_k, cache_sb_v, w_ada, b_ada, norm1_g, w_in,
          ret_norm_g, w_out, norm2_g, peer_w_query, peer_sub_keys, peer_u, peer_v, final_norm_g, small_c, mix_c,
          gate_dram, y_prompt, y_sample, st_prompt, k_prompt, v_prompt, st_sample, k_sample, v_sample):
    ctx = ExitStack()
    BASE = nc.sbuf_base + (-nc.sbuf_base) % 32

    def at(name, off, shape, dt=F32):
        return nc.alloc_sbuf_tensor_at(name, [P] + list(shape), dt, offset=BASE + off)

    cst = at("cst", 0, [C_N])
    o = 4 * C_N + 16
    ones = at("ones", o, [P])
    negones = at("negones", o + 512, [P])
    meanw = at("meanw", o + 1024, [P])
    o += 1536
    rowsT = at("rowsT", o, [R_N + 4])
    modT = at("modT", o + 384, [48, 2])
    coefA = at("coefA", o + 768, [2, KD, 2])
    siluT = at("siluT", o + 896, [KD, 2])
    epsc = at("epsc", o + 960, [8])
    assert o + 992 <= 6144
    hT = at("hT", 6144, [KD, T])
    XH = at("XH", 6144 + 17408, [KD, T], F32R)
    XL = at("XL", 6144 + 34816, [KD, T], F32R)
    R0 = 6144 + 52224

    wraw = at("wraw", R0, [2, KD, 512])
    whi = at("whi", R0 + 32768, [2, KD, P], F32R)
    wlo = at("wlo", R0 + 40960, [2, KD, P], F32R)
    RP = R0 + 49152
    projT = at("projT", RP, [NIN, T])
    adaR = at("adaR", RP + 16 * 4 * T, [12, 512])
    scr1 = at("scr1", RP, [KD, T])
    scr2 = at("scr2", RP + 8 * 4 * T, [KD, T])
    sqb = at("sqb", RP + 4 * 4 * T, [NH, T])
    rsb = at("rsb", RP + 8 * 4 * T, [NH, T])
    rs = at("rs", RP + 27 * 4 * T, [T])
    yT = at("yT", RP + 20 * 4 * T, [KD, T])
    RF = RP + NIN * 4 * T
    mixc = at("mixc", RF, [M_N])
    RT = RF + 13056
    rvt = at("rvt", RT, [5, 512])
    svt = at("svt", RT + 10240, [5, 512])
    rkd = at("rkd", RT + 20480, [5, 512])
    xin = at("xin", RT, [5, D])
    rows = at("rows", RT + 20480, [P])
    A0 = 6144 + 17408
    sw = at("sw", A0, [8, T])
    t1 = at("t1", A0 + 17408, [8, T])
    skt = at("skt", A0, [5, 512])
    lk = at("lk", A0 + 10240, [2, 1280])
    aw = at("aw", A0 + 20480, [1, 1280])
    pr = at("pr", A0 + 10240, [2, 1280])
    prs = at("prs", A0 + 25600, [NH, TS])
    qds = at("qds", A0 + 26112, [NH, TS])
    stO = at("stO", A0 + 26624, [NH, P])
    stS = at("stS", A0 + 28672, [NH, P])
    stN = at("stN", A0 + 30720, [NH, P])
    lks = at("lks", A0 + 10240, [NPB + 1, P])
    rsum = at("rsum", A0 + 14848, [NPB - 1, P])
    aws = at("aws", A0 + 20480, [NPB + 1, P])
    kraw = at("kraw", R0, [NPB, 512])
    vraw = at("vraw", R0 + 16384, [NPB, 512])
    kT = at("kT", R0 + 32768, [NH, PAST])

    qT = at("qT", RP, [16, T])
    skraw = at("skraw", RP + 34816, [16, P])
    skT = at("skT", RP + 43008, [16, P])
    isel = at("isel", RP + 51200, [5, P])
    jsel = at("jsel", RP + 53760, [5, P])
    gsel = at("gsel", RP + 56320, [5, P])
    S = at("S", RF, [16, P])
    S2 = at("S2", RF + 8192, [16, P])
    cand = at("cand", RF + 16384, [PH, 256])
    cand2 = at("cand2", RF + 24576, [PH, 256])
    eq = at("eq", RF + 32768, [PH * TOPK, TOPK])
    iT = at("iT", R0 + 32768, [T])
    jT = at("jT", R0 + 34944, [T])
    gT = at("gT", R0 + 37120, [T])
    gTl = at("gTl", R0 + 39296, [T])
    W1 = R0 + 41472
    val = at("val", W1, [16, TOPK])
    ind = at("ind", W1 + 1024, [16, TOPK], U32)
    indf = at("indf", W1 + 2048, [16, TOPK])
    tops = at("tops", W1 + 3072, [PH, TOPK])
    pos = at("pos", W1 + 3584, [PH, TOPK], U32)
    posa = at("posa", W1 + 4096, [PH, TOPK], U32)
    posf = at("posf", W1 + 4608, [2, PH, TOPK])
    ex = at("ex", W1 + 5632, [PH, TOPK])
    sm = at("sm", W1 + 6144, [2, PH])
    AS = 8
    ohA = at("ohA", RP, [AS, P], F32R)
    ohB = at("ohB", RP + 4096, [AS, P], F32R)
    ohC = at("ohC", RP + 8192, [AS, P], F32R)
    gst = at("gst", RP + 12288, [2, NJB, TB, JB])
    jcur = at("jcur", RP + 12288 + 32768 + 2176, [TB])
    gTh = at("gTh", RP + 12288 + 32768, [T], F32R)

    uraw = at("uraw", R0, [2, 2, D])
    vrw = at("vrw", R0 + 16384, [2, 2, D])
    uth = at("uth", R0 + 32768, [2, KD, P], F32R)
    utl = at("utl", R0 + 40960, [2, KD, P], F32R)
    vh = at("vh", R0 + 49152, [2, 2, D], F32R)
    vl = at("vl", R0 + 65536, [2, 2, D], F32R)
    wh = at("wh", R0 + 81920, [2, 2, T], F32R)
    wl = at("wl", R0 + 90624, [2, 2, T], F32R)
    G = at("G", R0 + 99328, [2, T, JB])
    acc = at("acc", R0 + 116736, [KD, T])
    gel = at("gel", R0 + 134144, [2, T])
    wv = at("wv", R0 + 138496, [2, T])
    ys = at("ys", R0, [2, D])

    PS = ctx.enter_context(nc.psum_tensor("PS", [P, 8, 512], F32))

    def sem(name):
        return ctx.enter_context(nc.semaphore(name))

    ident = cst[:, C_ID:C_ID + P]
    ntri = cst[:, C_TRI:C_TRI + P]
    mask = cst[:, C_MASK:C_MASK + P]
    mmin = cst[:, C_MIN:C_MIN + P]
    iota = cst[:, C_IOTA:C_IOTA + P]

    def kdec(b):
        return cst[:, C_KDEC + b * NH:C_KDEC + (b + 1) * NH]

    def bc(ap, axis, n):
        v = ap.unsqueeze(axis)
        shape = list(v.shape)
        shape[axis] = n
        return v.to_broadcast(shape)

    def pair(b):
        return PS[:, b:b + 2, 0:HT]

    def halves(ap):
        return ap.rearrange("p (b t) -> p b t", b=2)

    def f(ap):
        return ap.bitcast(F32)

    def groups_of(ap):
        return (ap[..., 0:TP], ap[..., TP:T])

    s_cst, s_mixc, s_rows, s_x = sem("s_cst"), sem("s_mixc"), sem("s_rows"), sem("s_x")
    s_init = sem("s_init")
    s_w = [sem("s_w0"), sem("s_w1")]
    s_rowsT_ps, s_rowsT = sem("s_rowsT_ps"), sem("s_rowsT")
    s_silu = sem("s_silu")
    s_xT, s_hT = sem("s_xT"), sem("s_hT")
    s_ada_mm, s_ada_row, s_mod_ps = sem("s_ada_mm"), sem("s_ada_row"), sem("s_mod_ps")
    s_dch = sem("s_dch")
    s_ach = sem("s_ach")
    s_coef = sem("s_coef")

    class Stage:
        pass

    norms, gemms = [], []
    for n in range(3):
        st = Stage()
        st.sq, st.ss, st.sd, st.rs, st.tmp, st.y, st.hi, st.lo = (
            sem(f"s_n{n}_{x}") for x in ("sq", "ss", "sd", "rs", "tmp", "y", "hi", "lo"))
        norms.append(st)
    for name, groups, arrived, first in (("in", 7, 6, 0), ("out", 2, 10, 0), ("qry", 4, 11, 0)):
        st = Stage()
        st.name, st.groups = name, groups
        st.hi, st.lo, st.mm, st.ev = (sem(f"s_{name}_{x}") for x in ("hi", "lo", "mm", "ev"))
        gemms.append(st)
    gemms[0].before = (6, 6)
    gemms[1].before = (10, 9)
    gemms[2].before = (11, 10)

    s_swap, s_rope, s_sqs = sem("s_swap"), sem("s_rope"), sem("s_sqs")
    s_tp, s_tm, s_rkd = sem("s_tp"), sem("s_tm"), sem("s_rkd")
    s_kc, s_vc, s_stS = sem("s_kc"), sem("s_vc"), sem("s_stS")
    s_rs_mm, s_rp, s_raux, s_rps, s_ro, s_ros, s_rev, s_rsn, s_qds = (
        sem(x) for x in ("s_rs_mm", "s_rp", "s_raux", "s_rps", "s_ro", "s_ros", "s_rev", "s_rsn", "s_qds"))
    s_bz, s_bln, s_blk, s_bc, s_bmin, s_ba, s_bo, s_bev = (
        sem(x) for x in ("s_bz", "s_bln", "s_blk", "s_bc", "s_bmin", "s_ba", "s_bo", "s_bev"))
    s_kt, s_kte, s_cz, s_cln, s_clk, s_cc, s_cmin, s_ca, s_co, s_cev = (
        sem(x) for x in ("s_kt", "s_kte", "s_cz", "s_cln", "s_clk", "s_cc", "s_cmin", "s_ca", "s_co", "s_cev"))
    s_gm, s_gcen, s_gsq, s_gv, s_gsd, s_gate, s_gy, s_ghi, s_glo = (
        sem(x) for x in ("s_gm", "s_gcen", "s_gsq", "s_gv", "s_gsd", "s_gate", "s_gy", "s_ghi", "s_glo"))
    s_h1, s_zero = sem("s_h1"), sem("s_zero")
    s_skl, s_skp, s_skT = sem("s_skl"), sem("s_skp"), sem("s_skT")
    s_sc, s_scev, s_cmpd, s_exd, s_exa, s_sel = (
        sem(x) for x in ("s_sc", "s_scev", "s_cmpd", "s_exd", "s_exa", "s_sel"))
    s_selT, s_selTe, s_gsplit = sem("s_selT"), sem("s_selTe"), sem("s_gsplit")
    s_oh, s_oha, s_gmm, s_gev = sem("s_oh"), sem("s_oha"), sem("s_gmm"), sem("s_gev")
    s_jc, s_pool = sem("s_jc"), sem("s_pool")
    s_gout = [sem("s_gout0"), sem("s_gout1")]
    s_u = [sem("s_u0"), sem("s_u1")]
    s_v = [sem("s_v0"), sem("s_v1")]
    s_g = [sem("s_g0"), sem("s_g1")]
    s_ut, s_uth, s_utl, s_up, s_gel, s_wv, s_wh, s_wl, s_vh, s_vl, s_om, s_add, s_acc0 = (
        sem(x) for x in ("s_ut", "s_uth", "s_utl", "s_up", "s_gel", "s_wv", "s_wh", "s_wl", "s_vh", "s_vl", "s_om",
                         "s_add", "s_acc0"))
    s_h2 = sem("s_h2")
    s_yt, s_ye = sem("s_yt"), sem("s_ye")
    s_yo = [sem("s_yo0"), sem("s_yo1")]
    s_out = sem("s_out")

    def w_view(w, g):
        return w[0].rearrange("(k p) n -> p k n", p=P)[:, :, bass.ds(g * 512, 512)]

    u_d = peer_u[0].rearrange("(j p) d -> p j d", p=P)
    v_d = peer_v[0].rearrange("(j p) d -> p j d", p=P)
    gate_v = gate_dram

    block = ctx.enter_context(nc.Block())

    @block.sync
    def _(sp):
        n_out = [0]

        def store(dst, src):
            sp.dma_start(dst, src).then_inc(s_out, 16)
            n_out[0] += 1

        sp.dma_start(rows[R_C:R_C + 8, :], c_prompt[0].rearrange("(k p) -> k p", p=P)).then_inc(s_rows, 16)
        sp.dma_start(rows[R_C + 8:R_C + 16, :], c_sample[0].rearrange("(k p) -> k p", p=P)).then_inc(s_rows, 16)
        sp.dma_start(rows[R_N1:R_N1 + 8, :], norm1_g[0].rearrange("(k p) -> k p", p=P)).then_inc(s_rows, 16)
        sp.dma_start(rows[R_N2:R_N2 + 8, :], norm2_g[0].rearrange("(k p) -> k p", p=P)).then_inc(s_rows, 16)
        sp.dma_start(rows[R_FG:R_FG + 8, :], final_norm_g.rearrange("(k p) -> k p", p=P)).then_inc(s_rows, 16)
        sp.dma_start(rows[R_RG:R_RG + 4, :], ret_norm_g[0].rearrange("(k p) -> k p", p=P)).then_inc(s_rows, 16)
        sp.dma_start(rows[R_B:R_B + 48, :], b_ada[0].rearrange("(k p) -> k p", p=P)).then_inc(s_rows, 16)
        sp.dma_start(cst[:], small_c).then_inc(s_cst, 16)

        def ada_load(g, slot):
            sp.dma_start(wraw[:, slot], w_view(w_ada, g)).then_inc(s_w[slot], 16)

        ada_load(0, 0)
        ada_load(1, 1)
        sp.dma_start(xin[:, 0:4, :], x_prompt[0].rearrange("(b p) d -> p b d", p=P)).then_inc(s_x, 16)
        sp.dma_start(xin[0:TS, 4, :], x_sample[0]).then_inc(s_x, 16)
        sp.dma_start(mixc[:], mix_c).then_inc(s_mixc, 16)
        with sp.Fori(1, 6) as i:
            for slot in range(2):
                sp.wait_ge(s_ada_mm, 2 * i + slot - 1)
                ada_load(2 * i + slot, slot)

        def gemm_loads(st, w, first_waits):
            for slot in range(2):
                for s, v in first_waits[slot]:
                    sp.wait_ge(s, v)
                sp.dma_start(wraw[:, slot], w_view(w, slot)).then_inc(s_w[slot], 16)
            if st.groups // 2 > 1:
                with sp.Fori(1, st.groups // 2) as i:
                    for slot in range(2):
                        g = 2 * i + slot
                        sp.wait_ge(st.lo, 4 * g - 4)
                        sp.dma_start(wraw[:, slot], w_view(w, g)).then_inc(s_w[slot], 16)
            if st.groups % 2:
                g = st.groups - 1
                sp.wait_ge(st.lo, 4 * g - 4)
                sp.dma_start(wraw[:, 0], w_view(w, g)).then_inc(s_w[0], 16)

        gemm_loads(gemms[0], w_in, (((s_ada_mm, 11),), ((s_ada_mm, 12),)))
        sp.wait_ge(gemms[0].lo, NIN)
        sp.dma_start(kraw[:], cache_sb_k[0, 0].rearrange("(b p) h d -> p b (h d)", p=P)).then_inc(s_kc, 16)
        sp.dma_start(vraw[:], cache_sb_v[0, 0].rearrange("(b p) h d -> p b (h d)", p=P)).then_inc(s_vc, 16)
        sp.wait_ge(s_rope, 3)
        sp.dma_start(stS[:], state_ret[0, 0].rearrange("h k v -> k h v")).then_inc(s_stS, 16)
        sp.wait_ge(s_tm, 10)
        store(v_prompt[0, 0].rearrange("(b p) h d -> p b (h d)", p=P), svt[:, 0:4, :])
        store(v_sample[0, 0].rearrange("p h d -> p (h d)"), svt[0:TS, 4, :])
        sp.wait_ge(s_tm, 15)
        store(k_prompt[0, 0].rearrange("(b p) h d -> p b (h d)", p=P), skt[:, 0:4, :])
        store(k_sample[0, 0].rearrange("p h d -> p (h d)"), skt[0:TS, 4, :])
        sp.wait_ge(s_rev, 3 * NH)
        store(st_prompt[0, 0].rearrange("h k v -> k h v"), stO[:])
        sp.wait_ge(s_rsn, NH)
        store(st_sample[0, 0].rearrange("h k v -> k h v"), stN[:])
        sp.wait_ge(s_out, 16 * n_out[0])

        gemm_loads(gemms[1], w_out, (((s_kt, NPB),), ((s_co, 1),)))
        gemm_loads(gemms[2], peer_w_query, (((gemms[1].lo, 4),), ((gemms[1].lo, 8),)))
        sp.wait_ge(gemms[1].ev, CREDIT + 8)
        sp.dma_start(skraw[:], peer_sub_keys[0].rearrange("a h k d -> k (a h) d")).then_inc(s_skl, 16)

        def u_load(pr_, slot):
            sp.dma_start(uraw[:, slot], u_d[:, bass.ds(2 * pr_, 2), :]).then_inc(s_u[slot], 16)

        def v_load(pr_, slot):
            sp.dma_start(vrw[:, slot], v_d[:, bass.ds(2 * pr_, 2), :]).then_inc(s_v[slot], 16)

        def g_load(b, slot):
            sp.dma_start(G[:, slot], gate_v[:, bass.ds(b, 1), :, :].rearrange("p a t j -> p (a t) j")
                         ).then_inc(s_g[slot], 16)

        sp.wait_ge(gemms[2].lo, 16)
        for slot in range(2):
            u_load(slot, slot)
            v_load(slot, slot)

        def g_store(b, slot):
            sp.wait_ge(s_gev, CREDIT + 8 * b + 8)
            sp.dma_start(gate_v[:, :, bass.ds(TB * b, TB), :], gst[:, slot]).then_inc(s_gout[slot], 16)

        with sp.Fori(0, 8) as i:
            for slot in range(2):
                g_store(2 * i + slot, slot)
        g_store(16, 0)
        sp.wait_ge(s_gout[0], 16 * 9)
        sp.wait_ge(s_gout[1], 16 * 8)
        g_load(0, 0)
        g_load(1, 1)

        def expert_loads(i, last):
            for q in range(4):
                pr_ = 4 * i + q
                if not (last and q >= 2):
                    sp.wait_ge(s_utl, 2 * pr_ + 2)
                    sp.wait_ge(s_ut, 2 * pr_ + 2)
                    u_load(pr_ + 2, q % 2)
                    sp.wait_ge(s_vl, 2 * pr_ + 2)
                    v_load(pr_ + 2, q % 2)
                if q % 2 and not last:
                    sp.wait_ge(s_wv, 2 * pr_ + 2)
                    g_load(2 * i + q // 2 + 2, q // 2)

        with sp.Fori(0, 15) as i:
            expert_loads(i, False)
        expert_loads(15, True)

        for n, (t0, w) in enumerate(TILES):
            sp.wait_ge(s_ye, n + 1)
            dst = y_prompt[0, t0:t0 + w, :] if t0 < TP else y_sample[0]
            sp.dma_start(dst, ys[0:w, n % 2, :]).then_inc(s_yo[n % 2], 16)
        sp.wait_ge(s_yo[0], 48)
        sp.wait_ge(s_yo[1], 32)
        sp.wait_ge(s_out, 16 * n_out[0])

    @block.tensor
    def _(pe):
        mm = nc.tensor.matmul

        def mm3(out, ah, al, bh, bl, start, stop):
            mm(out, ah, bh, start=start, stop=False)
            mm(out, ah, bl, start=False, stop=False)
            return mm(out, al, bh, start=False, stop=stop)

        def norm(st, squares):
            for k in range(KD):
                pe.wait_ge(st.sq, k + 1)
                for b in range(2):
                    last = mm(PS[:, b, 0:HT], ones[:], squares[:, k, b * HT:(b + 1) * HT], start=(k == 0),
                              stop=(k == KD - 1))
            last.then_inc(st.ss, 1)

        def gemm(st, pools):
            pe.sem_inc(st.mm, CREDIT)

            def group(g, slot):
                for cc in range(4):
                    c = 4 * g + cc
                    par = cc % 2
                    pe.wait_ge(st.lo, c + 1)
                    pe.wait_ge(st.ev, c + 1)
                    for b in range(2):
                        for k in range(KD):
                            last = mm3(PS[:, 2 * par + b, 0:HT], whi[:, par, k, :], wlo[:, par, k, :],
                                       XH[:, k, b * HT:(b + 1) * HT], XL[:, k, b * HT:(b + 1) * HT],
                                       k == 0, k == KD - 1)
                    last.then_inc(st.mm, 1)

            with pe.Fori(0, st.groups // 2) as i:
                for slot in range(2):
                    group(2 * i + slot, slot)
            if st.groups % 2:
                group(st.groups - 1, 0)

        pe.wait_ge(s_cst, 16)
        pe.wait_ge(s_rows, 16 * 7)
        nc.tensor.transpose(PS[:, 6, 0:R_N], rows[0:R_N, :], ident[0:R_N, 0:R_N]).then_inc(s_rowsT_ps, 1)
        pe.wait_ge(s_x, 32)
        for n, (t0, w) in enumerate(TILES):
            if n >= 2:
                pe.wait_ge(s_hT, n - 1)
            b = 2 + 2 * (n % 2)
            for k in range(KD):
                last = nc.tensor.transpose(PS[:, b + k // 4, (k % 4) * P:(k % 4) * P + w],
                                           xin[0:w, n, k * P:(k + 1) * P], ident[0:w, 0:w])
            last.then_inc(s_xT, 1)
        pe.wait_ge(s_silu, 1)
        with pe.Fori(0, 6) as i:
            for slot in range(2):
                g = 2 * i + slot
                pe.wait_ge(s_w[slot], 16 * i + 16)
                pe.wait_ge(s_ada_row, g + 1)
                for k in range(KD):
                    last = mm(PS[0:2, slot, :], siluT[:, k, :], wraw[:, slot, k, :], start=(k == 0),
                              stop=(k == KD - 1))
                last.then_inc(s_ada_mm, 1)
        pe.wait_ge(s_ada_row, CREDIT + 12)
        for n in range(48):
            last = nc.tensor.transpose(PS[:, 6, 2 * n:2 * n + 2], adaR[0:2, n // 4, (n % 4) * P:(n % 4) * P + P],
                                       ident[0:2, 0:2])
        last.then_inc(s_mod_ps, 1)
        pe.wait_ge(s_init, 1)
        norm(norms[0], scr1)
        pe.wait_ge(norms[0].lo, KD)
        pe.wait_ge(norms[0].hi, KD)
        pe.wait_ge(norms[0].sd, 1)
        gemm(gemms[0], None)

        pe.wait_ge(gemms[0].ev, CREDIT + NIN)
        n = 0
        for chunk in (RV, SV, SK, RK):
            if chunk == RK:
                pe.wait_ge(s_rope, 3)
            for t0, w in TILES:
                if n >= 4:
                    m = n - 4
                    if m < 15:
                        pe.wait_ge(s_tm, m + 1)
                    else:
                        pe.wait_ge(s_rkd, m - 14)
                for h in range(NH):
                    last = nc.tensor.transpose(PS[0:w, n % 4, h * P:(h + 1) * P], projT[:, chunk + h, t0:t0 + w], ident)
                last.then_inc(s_tp, 1)
                n += 1

        pe.wait_ge(s_rkd, 5)
        pe.wait_ge(s_tm, 15)
        pe.wait_ge(s_stS, 16)
        pe.wait_ge(s_qds, 2)
        for h in range(NH):
            hs = slice(h * P, (h + 1) * P)
            for kb in range(QB):
                if h >= 1:
                    pe.wait_ge(s_rp, QB * (h - 1) + kb + 1)
                mm(PS[:, kb, 0:TP - P * kb], projT[:, RK + h, kb * P:(kb + 1) * P], projT[:, RQ + h, kb * P:TP],
                   start=True, stop=True).then_inc(s_rs_mm, 1)
            if h >= 2:
                pe.wait_ge(s_rev, 3 * (h - 1))
                pe.wait_ge(s_rsn, h - 1)
                pe.wait_ge(s_rps, h - 1)
            aux = 6 + h % 2
            for kb in range(QB):
                mm(PS[:, aux, 0:P], rkd[:, kb, hs], rvt[:, kb, hs], start=(kb == 0), stop=(kb == QB - 1))
            mm(PS[0:TS, aux, P:P + TS], projT[:, RK + h, TP:T], projT[:, RQ + h, TP:T], start=True, stop=True)
            mm(PS[:, aux, 256:384], rkd[0:TS, 4, hs], rvt[0:TS, 4, hs], start=True, stop=True).then_inc(s_raux, 1)
            for kb in range(QB):
                pe.wait_ge(s_rp, QB * h + kb + 1)
                last = mm(PS[:, 4 + h % 2, kb * P:TP], rvt[:, kb, hs], pr[:, h % 2, pcol(kb):pcol(kb) + TP - P * kb],
                          start=(kb == 0), stop=(kb == QB - 1))
            last.then_inc(s_ro, 1)
            pe.wait_ge(s_rps, h + 1)
            pe.wait_ge(s_rsn, h + 1)
            mm(PS[:, aux, 384:384 + TS], stS[:, h, :], qds[:, h, :], start=True, stop=False)
            mm(PS[:, aux, 384:384 + TS], rvt[:, 4, hs], prs[:, h, :], start=False, stop=True).then_inc(s_ros, 1)

        pe.wait_ge(s_sqs, 1)
        pe.wait_ge(s_rev, 3 * NH)
        pe.wait_ge(s_rsn, NH)
        for h in range(NH):
            hs = slice(h * P, (h + 1) * P)
            for kb in range(QB):
                if h >= 1:
                    pe.wait_ge(s_ba, 7 * h)
                mm(PS[:, kb, 0:TP - P * kb], projT[:, SK + h, kb * P:(kb + 1) * P], projT[:, SQ + h, kb * P:TP],
                   start=True, stop=True).then_inc(s_bz, 1)
            pe.wait_ge(s_blk, QB * (h + 1))
            for kb in reversed(range(QB)):
                w = TP - P * kb
                last = mm(PS[:, kb, 0:w], ntri, lk[:, h % 2, pcol(kb):pcol(kb) + w], start=False, stop=(kb == QB - 1),
                          skip_group_check=True)
                for later in range(kb + 1, QB):
                    wl_ = TP - P * later
                    last = mm(PS[:, kb, w - wl_:w], negones[:], lk[:, h % 2, pcol(later):pcol(later) + wl_],
                              start=False, stop=(later == QB - 1), skip_group_check=True)
                last.then_inc(s_bc, 1)
            pe.wait_ge(s_ba, 7 * (h + 1))
            if h >= 2:
                pe.wait_ge(s_bev, h - 1)
            for kb in range(QB):
                last = mm(PS[:, 4 + h % 2, kb * P:TP], svt[:, kb, hs], aw[:, 0, pcol(kb):pcol(kb) + TP - P * kb],
                          start=(kb == 0), stop=(kb == QB - 1))
            last.then_inc(s_bo, 1)

        pe.wait_ge(s_kc, 16)
        for b in range(NPB):
            if b >= 2:
                pe.wait_ge(s_kte, b - 1)
            for h in range(NH):
                last = nc.tensor.transpose(PS[:, 6 + b % 2, h * P:(h + 1) * P], kraw[:, b, h * P:(h + 1) * P], ident)
            last.then_inc(s_kt, 1)
        pe.wait_ge(s_kte, NPB)
        for b in range(NPB):
            for h in range(NH):
                mm(PS[:, b // 4, (b % 4) * P + h * TS:(b % 4) * P + (h + 1) * TS], kT[:, h, b * P:(b + 1) * P],
                   projT[:, SQ + h, TP:T], start=(b % 4 == 0 and h == 0), stop=(b % 4 == 3 and h == NH - 1),
                   skip_group_check=True)
        for h in range(NH):
            last = mm(PS[0:TS, 2, h * TS:(h + 1) * TS], projT[:, SK + h, TP:T], projT[:, SQ + h, TP:T],
                      start=(h == 0), stop=(h == NH - 1), skip_group_check=True)
        last.then_inc(s_cz, 1)
        pe.wait_ge(s_clk, 1)
        for b in range(NPB):
            out = PS[:, b // 4, (b % 4) * P:(b % 4 + 1) * P]
            mm(out, ntri, lks[:, b, :], start=False, stop=False, skip_group_check=True)
            if b < NPB - 1:
                mm(out, negones[:], rsum[:, b, :], start=False, stop=False, skip_group_check=True)
            mm(out, negones[:], lks[:, NPB, :], start=False, stop=True, skip_group_check=True)
        mm(PS[0:TS, 2, 0:P], ntri[:, 0:TS], lks[:, NPB, :], start=False, stop=True,
           skip_group_check=True).then_inc(s_cc, 1)
        pe.wait_ge(s_ca, 2)
        pe.wait_ge(s_vc, 16)
        for h in range(NH):
            hs = slice(h * P, (h + 1) * P)
            for b in range(NPB + 1):
                lhs = vraw[:, b, hs] if b < NPB else svt[:, 4, hs]
                last = mm(PS[:, 3, h * TS:(h + 1) * TS], lhs, aws[:, b, h * TS:(h + 1) * TS], start=(b == 0),
                          stop=(b == NPB))
        last.then_inc(s_co, 1)

        pe.wait_ge(s_cev, 1)
        pe.wait_ge(s_bev, NH)
        for h in range(NH):
            for b in range(2):
                last = mm(PS[:, 2 * h + b, 0:HT], meanw[:], projT[:, h, b * HT:(b + 1) * HT], start=True, stop=True)
            last.then_inc(s_gm, 1)
        for h in range(NH):
            pe.wait_ge(s_gsq, h + 1)
            for b in range(2):
                last = mm(PS[:, 2 * h + b, 0:HT], meanw[:], sqb[:, h, b * HT:(b + 1) * HT], start=True, stop=True)
            last.then_inc(s_gv, 1)
        pe.wait_ge(s_gsd, NH)
        pe.wait_ge(s_ghi, 2)
        pe.wait_ge(s_glo, 2)
        gemm(gemms[1], None)
        pe.wait_ge(gemms[1].ev, CREDIT + 8)
        norm(norms[1], scr1)
        pe.wait_ge(norms[1].lo, KD)
        pe.wait_ge(norms[1].hi, KD)
        pe.wait_ge(norms[1].sd, 1)
        gemm(gemms[2], None)

        pe.wait_ge(s_skl, 16)
        for n in range(4):
            for m in range(4):
                last = nc.tensor.transpose(PS[:, 4 + n, m * P:(m + 1) * P], skraw[:, 4 * n + m, :], ident)
        last.then_inc(s_skp, 1)
        pe.wait_ge(s_skT, 1)
        pe.wait_ge(gemms[2].ev, CREDIT + 16)
        for n, (t0, w) in enumerate(TILES):
            for hp in range(16):
                if hp % 4 == 0 and n >= 1:
                    pe.wait_ge(s_scev, 4 * (n - 1) + hp // 4 + 1)
                last = mm(PS[0:w, hp // 4, (hp % 4) * P:(hp % 4 + 1) * P], qT[:, hp, t0:t0 + w],
                          skT[:, (hp % 2) * PH + hp // 2, :], start=True, stop=True)
                if hp % 4 == 3:
                    last.then_inc(s_sc, 1)
        pe.wait_ge(s_sel, 5)
        for m, src in enumerate((isel, jsel, gsel)):
            for n, (t0, w) in enumerate(TILES):
                last = nc.tensor.transpose(PS[:, 2 * m + n // 4, (n % 4) * P:(n % 4) * P + w], src[0:w, n, :],
                                           ident[0:w, 0:w])
        last.then_inc(s_selT, 1)
        pe.wait_ge(s_selTe, 6)

        def gate_batch(b):
            for q in range(TB // 4):
                n4 = 8 * b + q
                pe.wait_ge(s_gev, n4 + 1)
                for r in range(4):
                    tt = 4 * q + r
                    pe.wait_ge(s_oh, TB * b + tt + 1)
                    pe.wait_ge(s_oha, TB * b + tt + 1)
                    sl = tt % AS
                    mm(PS[:, q % 2, r * P:(r + 1) * P], ohA[:, sl, :], ohB[:, sl, :], start=True, stop=False)
                    mm(PS[:, q % 2, r * P:(r + 1) * P], ohA[:, sl, :], ohC[:, sl, :], start=False,
                       stop=True).then_inc(s_gmm, 1)

        with pe.Fori(0, 17) as i:
            gate_batch(i)

        pe.wait_ge(s_gev, CREDIT + 8 * 17)

        def turn(j, par, first):
            pe.wait_ge(s_utl, j)
            for k in range(KD):
                last = nc.tensor.transpose(PS[:, k // 4, (k % 4) * P:(k % 4 + 1) * P],
                                           uraw[:, (par // 2) % 2, par % 2, k * P:(k + 1) * P], ident)
            last.then_inc(s_ut, 1)

        def up(j, par, first):
            pe.wait_ge(s_utl, j + 1)
            for b in range(2):
                if not first:
                    pe.wait_ge(s_gel, 2 * j - 1 + b)
                for k in range(KD):
                    last = mm3(PS[:, 2 + b, 0:HT], uth[:, par % 2, k, :], utl[:, par % 2, k, :],
                               XH[:, k, b * HT:(b + 1) * HT], XL[:, k, b * HT:(b + 1) * HT], k == 0, k == KD - 1)
                last.then_inc(s_up, 1)

        def down(pr_, par):
            pe.wait_ge(s_vl, 2 * pr_ + 2)
            pe.wait_ge(s_wl, 2 * pr_ + 2)
            for n in range(16):
                dc, b = n // 2, n % 2
                pe.wait_ge(s_add, 16 * pr_ + n + 1)
                for r in range(2):
                    last = mm3(PS[:, 4 + n % 4, 0:HT], vh[:, par, r, dc * P:(dc + 1) * P],
                               vl[:, par, r, dc * P:(dc + 1) * P], wh[:, par, r, b * HT:(b + 1) * HT],
                               wl[:, par, r, b * HT:(b + 1) * HT], r == 0, r == 1)
                last.then_inc(s_om, 1)

        def iteration(i, first, last):
            for q in range(4):
                pr_, j = 4 * i + q, 8 * i + 2 * q
                turn(j + 1, 2 * q + 1, False)
                up(j, 2 * q, first and q == 0)
                if not (last and q == 3):
                    if q % 2 == 1:
                        if q == 1:
                            pe.wait_ge(s_u[0], 32 * i + 32)
                        else:
                            pe.wait_ge(s_u[0], 32 * i + 48)
                    else:
                        pe.wait_ge(s_u[1], 32 * i + 16 + 16 * (q // 2))
                    turn(j + 2, 2 * q + 2, False)
                up(j + 1, 2 * q + 1, False)
                if not (first and q == 0):
                    down(pr_ - 1, (q + 1) % 2)

        pe.wait_ge(s_u[0], 16)
        turn(0, 0, True)
        iteration(0, True, False)
        with pe.Fori(1, 15) as i:
            iteration(i, False, False)
        iteration(15, False, True)
        down(63, 1)

        norm(norms[2], scr1)
        pe.wait_ge(norms[2].y, 1)
        for n, (t0, w) in enumerate(TILES):
            if n >= 2:
                pe.wait_ge(s_ye, n - 1)
            b = 2 + 2 * (n % 2)
            for k in range(KD):
                last = nc.tensor.transpose(PS[0:w, b + k // 4, (k % 4) * P:(k % 4 + 1) * P], scr2[:, k, t0:t0 + w],
                                           ident)
            last.then_inc(s_yt, 1)

    @block.scalar
    def _(act):
        act_ = nc.scalar.activation
        chain = [0]

        def link(ins):
            chain[0] += 1
            ins.then_inc(s_ach, 1)
            act.wait_ge(s_ach, chain[0])

        def squares(st, ready):
            for k in range(KD):
                if k == 0 or len(ready) == KD:
                    act.wait_ge(*ready[k])
                act_(scr1[:, k, :], hT[:, k, :], ACT.Square).then_inc(st.sq, 1)
            act.wait_ge(st.ss, 1)
            act_(halves(rs[:]), pair(0), ACT.Sqrt, bias=epsc[:, 0:1], scale=1.0 / D).then_inc(st.sd, 1)

        def modulated(st, n):
            for k in range(KD):
                act.wait_ge(st.tmp, k + 1)
                for g, cols in enumerate((slice(0, TP), slice(TP, T))):
                    act_(scr1[:, k, cols], scr2[:, k, cols], ACT.Identity, scale=coefA[:, n, k, g:g + 1],
                         bias=modT[:, 24 * n + k, g:g + 1]).then_inc(st.y, 1)
                act.wait_ge(st.y, 2 * k + 2)
                act_(XH[:, k, :], scr1[:, k, :], ACT.Copy).then_inc(st.hi, 1)

        def gemm_out(st, out):
            act.sem_inc(st.ev, CREDIT)

            def group(g):
                for cc in range(4):
                    c = 4 * g + cc
                    act.wait_ge(st.mm, c + 1 + CREDIT)
                    act_(out[:, bass.ds(c, 1), :].rearrange("p a (b t) -> p (a b) t", b=2), pair(2 * (cc % 2)),
                         ACT.Copy).then_inc(st.ev, 1)

            with act.Fori(0, st.groups) as g:
                group(g)

        act.wait_ge(s_rowsT, 1)
        act_(siluT[:].rearrange("p k g -> p g k"), rowsT[:, 0:16].rearrange("p (g k) -> p g k", g=2),
             ACT.Silu).then_inc(s_silu, 1)
        act.wait_ge(s_init, 1)
        squares(norms[0], [(s_hT, 5)])
        act.wait_ge(s_coef, 1)
        modulated(norms[0], 0)
        gemm_out(gemms[0], projT)

        act.wait_ge(gemms[0].ev, CREDIT + NIN)
        act.wait_ge(gemms[0].mm, CREDIT + NIN)
        act_(sw[0:64], projT[64:128, 0:8, :], ACT.Copy).then_inc(s_swap, 1)
        for n in range(15):
            act.wait_ge(s_tp, n + 1)
            if n == 0:
                act.wait_ge(s_zero, 2)
            if n == 10:
                act.wait_ge(s_rope, 3)
            t0, w = TILES[n % 5]
            dst = (rvt, svt, skt)[n // 5]
            act_(dst[0:w, n % 5, :], PS[0:w, n % 4, :], ACT.Copy).then_inc(s_tm, 1)
        for h in range(NH):
            act.wait_ge(s_raux, h + 1)
            act_(stO[:, h, :], PS[:, 6 + h % 2, 0:P], ACT.Copy).then_inc(s_rev, 1)
            act.wait_ge(s_ro, h + 1)
            act_(projT[:, RQ + h, 0:TP], PS[:, 4 + h % 2, :], ACT.Copy).then_inc(s_rev, 1)
            act.wait_ge(s_ros, h + 1)
            act_(projT[:, RQ + h, TP:T], PS[:, 6 + h % 2, 384:384 + TS], ACT.Copy).then_inc(s_rev, 1)
        nc.scalar.preload_act_table_set("natural_log_exp_and_others")
        for h in range(NH):
            par = h % 2
            act.wait_ge(s_bz, QB * (h + 1))
            if h >= 2:
                act.wait_ge(s_bo, h - 1)
            def lkv(kb):
                return lk[:, par, pcol(kb):pcol(kb) + TP - P * kb]
            for kb in range(QB):
                act_(lkv(kb), PS[:, kb, 0:TP - P * kb], ACT.Abs).then_inc(s_ach, 1)
            chain[0] += QB
            act.wait_ge(s_ach, chain[0])
            link(act_(lk[:, par, :], lk[:, par, :], ACT.Exp, scale=-1.0))
            act_(lk[:, par, :], lk[:, par, :], ACT.Ln, bias=1.0).then_inc(s_bln, 1)
            if h >= 1:
                act.wait_ge(s_bo, h)
            for kb in reversed(range(QB)):
                w = TP - P * kb
                act.wait_ge(s_bmin, QB * h + QB - kb)
                if w > P:
                    act_(aw[:, 0, pcol(kb) + P:pcol(kb) + w], PS[:, kb, P:w], ACT.Exp).then_inc(s_ba, 1)
                act_(aw[:, 0, pcol(kb):pcol(kb) + P], aw[:, 0, pcol(kb):pcol(kb) + P], ACT.Exp).then_inc(s_ba, 1)
            act.wait_ge(s_bo, h + 1)
            act_(projT[:, SQ + h, 0:TP], PS[:, 4 + par, :], ACT.Copy).then_inc(s_bev, 1)
        for b in range(NPB):
            act.wait_ge(s_kt, b + 1)
            act_(kT[:, :, b * P:(b + 1) * P], PS[:, 6 + b % 2, :].rearrange("p (h k) -> p h k", h=NH),
                 ACT.Copy).then_inc(s_kte, 1)
        act.wait_ge(s_cz, 1)
        act.wait_ge(s_zero, 4)
        act_(lks[:, 0:NPB, :], PS[:, 0:2, :].rearrange("p b (c x) -> p (b c) x", x=P), ACT.Abs).then_inc(s_ach, 1)
        act_(lks[0:TS, NPB, :], PS[0:TS, 2, 0:P], ACT.Abs).then_inc(s_ach, 1)
        chain[0] += 2
        act.wait_ge(s_ach, chain[0])
        act_(lks[:, 0:NPB, :], lks[:, 0:NPB, :], ACT.Exp, scale=-1.0).then_inc(s_ach, 1)
        act_(lks[0:TS, NPB, :], lks[0:TS, NPB, :], ACT.Exp, scale=-1.0).then_inc(s_ach, 1)
        chain[0] += 2
        act.wait_ge(s_ach, chain[0])
        act_(lks[:, 0:NPB, :], lks[:, 0:NPB, :], ACT.Ln, bias=1.0).then_inc(s_cln, 1)
        act_(lks[0:TS, NPB, :], lks[0:TS, NPB, :], ACT.Ln, bias=1.0).then_inc(s_cln, 1)
        act.wait_ge(s_cc, 1)
        act_(aws[:, 0:NPB, :], PS[:, 0:2, :].rearrange("p b (c x) -> p (b c) x", x=P), ACT.Exp).then_inc(s_ca, 1)
        act.wait_ge(s_cmin, 1)
        act_(aws[0:TS, NPB, :], aws[0:TS, NPB, :], ACT.Exp).then_inc(s_ca, 1)
        act.wait_ge(s_co, 1)
        act_(projT[:, SQ:SQ + NH, TP:T], PS[:, 3, 0:P].rearrange("p (h t) -> p h t", h=NH),
             ACT.Copy).then_inc(s_cev, 1)
        act_(projT[:, RG:RG + NH, :], projT[:, RG:RG + NH, :], ACT.Silu).then_inc(s_gate, 1)
        act.wait_ge(s_cev, 1)
        act.wait_ge(s_out, 96)
        act_(XH[:, 4:8, :], projT[:, SQ:SQ + NH, :], ACT.Copy).then_inc(s_ghi, 1)
        for h in range(NH):
            act.wait_ge(s_gcen, h + 1)
            act_(sqb[:, h, :], projT[:, h, :], ACT.Square).then_inc(s_gsq, 1)
        for h in range(NH):
            act.wait_ge(s_gv, h + 1)
            act_(halves(rsb[:, h, :]), pair(2 * h), ACT.Sqrt, bias=epsc[:, 0:1]).then_inc(s_gsd, 1)
        act.wait_ge(s_gy, 4)
        act_(XH[:, 0:4, :], projT[:, 0:4, :], ACT.Copy).then_inc(s_ghi, 1)
        gemm_out(gemms[1], yT)
        squares(norms[1], [(s_h1, 2 * (k + 1)) for k in range(KD)])
        modulated(norms[1], 1)
        act.wait_ge(norms[1].lo, KD)
        gemm_out(gemms[2], qT)
        act.wait_ge(s_skp, 1)
        act_(skT[:].rearrange("p (b m) k -> p b (m k)", b=4), PS[:, 4:8, :], ACT.Copy).then_inc(s_skT, 1)
        for n, (t0, w) in enumerate(TILES):
            for q in range(4):
                act.wait_ge(s_sc, 4 * n + q + 1)
                if q == 0 and n >= 1:
                    act.wait_ge(s_cmpd, n)
                act_(S[0:w, 4 * q:4 * q + 4, :], PS[0:w, q, :].rearrange("p (m k) -> p m k", m=4),
                     ACT.Copy).then_inc(s_scev, 1)
            act.wait_ge(s_exd, n + 1)
            act_(ex[0:w], tops[0:w], ACT.Exp).then_inc(s_exa, 1)
        act.wait_ge(s_selT, 1)
        for m, dst in enumerate((iT, jT, gT)):
            act_(dst[:, 0:TP], PS[:, 2 * m, :], ACT.Copy).then_inc(s_selTe, 1)
            act_(dst[:, TP:T], PS[:, 2 * m + 1, 0:TS], ACT.Copy).then_inc(s_selTe, 1)
        act.sem_inc(s_gev, CREDIT)

        def gate_out(b, slot):
            for q in range(TB // 4):
                act.wait_ge(s_gmm, TB * b + 4 * q + 4)
                act_(gst[:, slot, :, 4 * q:4 * q + 4, :],
                     PS[:, q % 2, :].rearrange("p (t b j) -> p b t j", t=4, j=JB), ACT.Copy).then_inc(s_gev, 1)

        gate_out(0, 0)
        gate_out(1, 1)
        with act.Fori(1, 8) as i:
            for slot in range(2):
                act.wait_ge(s_gout[slot], 16 * i)
                gate_out(2 * i + slot, slot)
        act.wait_ge(s_gout[0], 16 * 8)
        gate_out(16, 0)

        def u_hi(j, par):
            act.wait_ge(s_ut, j + 1)
            if not isinstance(j, int) or j >= 2:
                act.wait_ge(s_up, 2 * j - 2)
            act_(uth[:, par % 2], PS[:, 0:2, :].rearrange("p b (k i) -> p (b k) i", i=P), ACT.Copy).then_inc(s_uth, 1)

        def gelu(j, par):
            for b in range(2):
                act.wait_ge(s_up, 2 * j + b + 1)
                if not isinstance(j, int) or j >= 2:
                    act.wait_ge(s_wv, j - 1)
                act_(gel[:, par % 2, b * HT:(b + 1) * HT], PS[:, 2 + b, 0:HT], ACT.Gelu_apprx_tanh).then_inc(s_gel, 1)

        def w_hi(j, par):
            act.wait_ge(s_wv, j + 1)
            if not isinstance(j, int) or j >= 4:
                act.wait_ge(s_om, 8 * j - 8 * (par % 2) - 16)
            act_(wh[:, (par // 2) % 2, par % 2, :], wv[:, par % 2, :], ACT.Copy).then_inc(s_wh, 1)

        def iteration(i, last):
            for q in range(4):
                j = 8 * i + 2 * q
                u_hi(j + 1, 2 * q + 1)
                gelu(j, 2 * q)
                w_hi(j, 2 * q)
                if not (last and q == 3):
                    u_hi(j + 2, 2 * q + 2)
                gelu(j + 1, 2 * q + 1)
                w_hi(j + 1, 2 * q + 1)

        u_hi(0, 0)
        iteration(0, False)
        with act.Fori(1, 15) as i:
            iteration(i, False)
        iteration(15, True)

        squares(norms[2], [(s_h2, 2 * (k + 1)) for k in range(KD)])
        for n, (t0, w) in enumerate(TILES):
            act.wait_ge(s_yt, n + 1)
            if n >= 2:
                act.wait_ge(s_yo[n % 2], 16 * (n // 2))
            b = 2 + 2 * (n % 2)
            act_(ys[0:w, n % 2, :].rearrange("p (b x) -> p b x", b=2), PS[0:w, b:b + 2, :], ACT.Copy).then_inc(s_ye, 1)

    @block.gpsimd
    def _(pool):
        def pass_wait():
            pool.sem_inc(s_pool, 1)

        def gemm_hi(st):
            def group(g, slot, i):
                for cc in range(4):
                    c = 4 * g + cc
                    if cc == 0:
                        pool.wait_ge(s_w[slot], 16 * (st.before[slot] + 1) + 16 * i)
                    pool.wait_ge(st.mm, c + 1)
                    pass_wait()
                    nc.gpsimd.tensor_copy(whi[:, cc % 2], wraw[:, slot, :, cc * P:(cc + 1) * P]).then_inc(st.hi, 1)

            with pool.Fori(0, st.groups // 2) as i:
                for slot in range(2):
                    group(2 * i + slot, slot, i)
            if st.groups % 2:
                group(st.groups - 1, 0, st.groups // 2)

        gemm_hi(gemms[0])
        pool.wait_ge(gemms[0].ev, CREDIT + NIN)
        pool.wait_ge(gemms[0].mm, CREDIT + NIN)
        nc.gpsimd.tensor_copy(sw[64:128], projT[0:64, 0:8, :]).then_inc(s_swap, 1)
        gemm_hi(gemms[1])
        gemm_hi(gemms[2])

        pool.wait_ge(s_selTe, 6)

        def onehot(b):
            pool.wait_ge(s_oha, TB * b)
            pass_wait()
            nc.gpsimd.tensor_copy(jcur[:], jT[:, bass.ds(TB * b, TB)]).then_inc(s_jc, 1)
            pool.wait_ge(s_jc, b + 1)
            pass_wait()
            for tt in range(TB):
                if tt < AS and isinstance(b, int) and b == 0:
                    pass
                else:
                    pool.wait_ge(s_gmm, TB * b + tt + 1 - AS)
                pass_wait()
                nc.gpsimd.tensor_scalar(ohA[:, tt % AS, :], iota, jcur[:, tt:tt + 1], None,
                                        ALU.is_equal).then_inc(s_oha, 1)

        onehot(0)
        with pool.Fori(1, 17) as i:
            onehot(i)

        def v_hi(pr_, par, rnd):
            pool.wait_ge(s_v[par], 16 * rnd + 16)
            for r in range(2):
                if not isinstance(pr_, int) or pr_ >= 2:
                    pool.wait_ge(s_om, 16 * pr_ - 16)
                pass_wait()
                nc.gpsimd.tensor_copy(vh[:, par, r, :], vrw[:, par, r, :]).then_inc(s_vh, 1)

        pool.wait_ge(s_gev, CREDIT + 8 * 17)
        pool.wait_ge(s_gout[0], 16 * 9)
        pool.wait_ge(s_gout[1], 16 * 8)
        v_hi(0, 0, 0)
        v_hi(1, 1, 0)
        with pool.Fori(1, 32) as i:
            for par in range(2):
                v_hi(2 * i + par, par, i)

    @block.vector
    def _(dve):
        tt, ts, stt = nc.vector.tensor_tensor, nc.vector.tensor_scalar, nc.vector.scalar_tensor_tensor
        chain = [0]

        def link(*ins):
            for x in ins:
                chain[0] += 1
                x.then_inc(s_dch, 1)
            dve.wait_ge(s_dch, chain[0])

        def gemm_lo(st):
            def group(g, slot):
                for cc in range(4):
                    dve.wait_ge(st.hi, 4 * g + cc + 1)
                    tt(wlo[:, cc % 2], wraw[:, slot, :, cc * P:(cc + 1) * P], f(whi[:, cc % 2]),
                       ALU.subtract).then_inc(st.lo, 1)

            with dve.Fori(0, st.groups // 2) as i:
                for slot in range(2):
                    group(2 * i + slot, slot)
            if st.groups % 2:
                group(st.groups - 1, 0)

        def norm(st, modulated):
            dve.wait_ge(st.sd, 1)
            link(nc.vector.reciprocal(rs[:], rs[:]))
            for k in range(KD):
                tt(scr2[:, k, :], hT[:, k, :], rs[:], ALU.mult).then_inc(st.tmp, 1)
            if modulated:
                for k in range(KD):
                    dve.wait_ge(st.hi, k + 1)
                    tt(XL[:, k, :], scr1[:, k, :], f(XH[:, k, :]), ALU.subtract).then_inc(st.lo, 1)

        nc.vector.memset(ones[:], 1.0)
        nc.vector.memset(negones[:], -1.0)
        nc.vector.memset(meanw[:], 1.0 / P)
        nc.vector.memset(epsc[:], EPS).then_inc(s_dch, 1)
        chain[0] += 1
        dve.wait_ge(s_dch, chain[0])
        dve.sem_inc(s_init, 1)
        dve.wait_ge(s_rowsT_ps, 1)
        nc.vector.tensor_copy(rowsT[:, 0:R_N], PS[:, 6, 0:R_N]).then_inc(s_rowsT, 1)
        for n, (t0, w) in enumerate(TILES):
            dve.wait_ge(s_xT, n + 1)
            b = 2 + 2 * (n % 2)
            nc.vector.tensor_copy(hT[:, :, t0:t0 + w],
                                  PS[:, b:b + 2, :].rearrange("p b (k t) -> p (b k) t", t=P)[:, :, 0:w]).then_inc(s_hT, 1)
        dve.sem_inc(s_ada_row, CREDIT)
        with dve.Fori(0, 6) as i:
            for slot in range(2):
                g = 2 * i + slot
                dve.wait_ge(s_ada_mm, g + 1)
                nc.vector.tensor_copy(adaR[0:2, bass.ds(g, 1), :].rearrange("p a x -> p (a x)"),
                                      PS[0:2, slot, :]).then_inc(s_ada_row, 1)
        dve.wait_ge(s_mod_ps, 1)
        dve.wait_ge(s_rowsT, 1)
        link(tt(modT[:], PS[:, 6, 0:96].rearrange("p (n g) -> p n g", g=2), bc(rowsT[:, R_B:R_N], 2, 2), ALU.add))
        for n in range(2):
            g0 = (R_N1, R_N2)[n]
            ins = stt(coefA[:, n], modT[:, 24 * n + 8:24 * n + 16, :], 1.0, bc(rowsT[:, g0:g0 + 8], 2, 2), ALU.add,
                      ALU.mult)
            link(ins)
        dve.sem_inc(s_coef, 1)
        nc.vector.memset(rvt[:, 4, :], 0.0).then_inc(s_zero, 1)
        nc.vector.memset(svt[:, 4, :], 0.0).then_inc(s_zero, 1)
        norm(norms[0], True)
        gemm_lo(gemms[0])

        dve.wait_ge(s_mixc, 16)
        dve.wait_ge(gemms[0].ev, CREDIT + NIN)
        dve.wait_ge(gemms[0].mm, CREDIT + NIN)
        cosv = bc(mixc[:, M_COS:M_COS + T], 1, 8)
        sinv = bc(mixc[:, M_SIN:M_SIN + T], 1, 8)
        tt(t1[:], projT[:, 0:8, :], cosv, ALU.mult).then_inc(s_rope, 1)
        dve.wait_ge(s_swap, 2)
        tt(sw[:], sw[:], sinv, ALU.mult).then_inc(s_rope, 1)
        dve.wait_ge(s_rope, 2)
        tt(projT[:, 0:8, :], t1[:], sw[:], ALU.add).then_inc(s_rope, 1)
        ts(projT[:, SQ:SQ + NH, :], projT[:, SQ:SQ + NH, :], SCALE, None, ALU.mult).then_inc(s_sqs, 1)
        dve.wait_ge(s_rope, 3)
        tt(qds[:], projT[:, RQ:RQ + NH, TP:T], mixc[:, M_QDEC:M_QDEC + NH * TS].rearrange("p (h t) -> p h t", h=NH),
           ALU.mult).then_inc(s_qds, 1)
        nc.vector.memset(prs[:], 0.0).then_inc(s_qds, 1)
        for b, (t0, w) in enumerate(TILES):
            dve.wait_ge(s_tp, 15 + b + 1)
            tt(rkd[0:w, b, :].rearrange("p (h d) -> p h d", h=NH),
               PS[0:w, (15 + b) % 4, :].rearrange("p (h d) -> p h d", h=NH), bc(kdec(b)[0:w], 2, P),
               ALU.mult).then_inc(s_rkd, 1)
        dve.wait_ge(s_qds, 2)
        gam = [float(np.exp(TS * np.log1p(-np.exp2(-5.0 - h)))) for h in range(NH)]
        for h in range(NH):
            if h >= 2:
                dve.wait_ge(s_ro, h - 1)
            for kb in range(QB):
                w = TP - P * kb
                dve.wait_ge(s_rs_mm, QB * h + kb + 1)
                stt(pr[:, h % 2, pcol(kb):pcol(kb) + w], PS[:, kb, 0:w], SCALE,
                    mixc[:, M_DT + h * TP:M_DT + h * TP + w], ALU.mult, ALU.mult).then_inc(s_rp, 1)
            dve.wait_ge(s_raux, h + 1)
            dve.wait_ge(s_rev, 3 * h + 1)
            stt(prs[0:TS, h, :], PS[0:TS, 6 + h % 2, P:P + TS], SCALE, mixc[0:TS, M_DT + h * TP:M_DT + h * TP + TS],
                ALU.mult, ALU.mult).then_inc(s_rps, 1)
            dve.wait_ge(s_stS, 16)
            stt(stN[:, h, :], stS[:, h, :], gam[h], PS[:, 6 + h % 2, 256:384], ALU.mult, ALU.add).then_inc(s_rsn, 1)
        for h in range(NH):
            par = h % 2
            dve.wait_ge(s_bln, h + 1)
            for kb in range(QB):
                w = TP - P * kb
                v = lk[:, par, pcol(kb):pcol(kb) + w]
                ins = stt(v, PS[:, kb, 0:w], 0.0, v, ALU.max, ALU.add)
                ins.then_inc(s_dch, 1)
                chain[0] += 1
            dve.wait_ge(s_dch, chain[0])
            for kb in range(QB):
                v = lk[:, par, pcol(kb):pcol(kb) + P]
                tt(v, v, mask, ALU.mult).then_inc(s_blk, 1)
            if h >= 1:
                dve.wait_ge(s_bo, h)
            for kb in reversed(range(QB)):
                dve.wait_ge(s_bc, QB * h + QB - kb)
                tt(aw[:, 0, pcol(kb):pcol(kb) + P], PS[:, kb, 0:P], mmin, ALU.min).then_inc(s_bmin, 1)
        dve.wait_ge(s_bo, NH)
        nc.vector.memset(lks[:, NPB, :], 0.0).then_inc(s_zero, 1)
        nc.vector.memset(aws[:, NPB, :], 0.0).then_inc(s_zero, 1)
        dve.wait_ge(s_cln, 2)
        v8, z8 = lks[0:TS, NPB, :], PS[0:TS, 2, 0:P]
        link(stt(lks[:, 0:NPB, :], PS[:, 0:2, :].rearrange("p b (c x) -> p (b c) x", x=P), 0.0, lks[:, 0:NPB, :],
                 ALU.max, ALU.add),
             stt(v8, z8, 0.0, v8, ALU.max, ALU.add))
        v8h = v8.rearrange("p (h t) -> p h t", h=NH)
        link(tt(v8h, v8h, bc(mask[0:TS, 0:TS], 1, NH), ALU.mult),
             nc.vector.tensor_copy(rsum[:, NPB - 2, :], lks[:, NPB - 1, :]))
        for b in reversed(range(NPB - 2)):
            link(tt(rsum[:, b, :], rsum[:, b + 1, :], lks[:, b + 1, :], ALU.add))
        dve.sem_inc(s_clk, 1)
        dve.wait_ge(s_cc, 1)
        tt(aws[0:TS, NPB, :].rearrange("p (h t) -> p h t", h=NH), z8.rearrange("p (h t) -> p h t", h=NH),
           bc(mmin[0:TS, 0:TS], 1, NH), ALU.min).then_inc(s_cmin, 1)
        dve.wait_ge(s_ghi, 1)
        dve.wait_ge(s_out, 96)
        tt(XL[:, 4:8, :], projT[:, SQ:SQ + NH, :], f(XH[:, 4:8, :]), ALU.subtract).then_inc(s_glo, 1)
        for h in range(NH):
            dve.wait_ge(s_gm, h + 1)
            tt(halves(projT[:, h, :]), halves(projT[:, h, :]), pair(2 * h), ALU.subtract).then_inc(s_gcen, 1)
        for h in range(NH):
            dve.wait_ge(s_gsd, h + 1)
            link(nc.vector.reciprocal(rsb[:, h, :], rsb[:, h, :]))
            link(tt(projT[:, h, :], projT[:, h, :], rsb[:, h, :], ALU.mult))
            dve.wait_ge(s_gate, 1)
            stt(projT[:, h, :], projT[:, h, :], rowsT[:, R_RG + h:R_RG + h + 1], projT[:, RG + h, :], ALU.mult,
                ALU.mult).then_inc(s_gy, 1)
        dve.wait_ge(s_ghi, 2)
        tt(XL[:, 0:4, :], projT[:, 0:4, :], f(XH[:, 0:4, :]), ALU.subtract).then_inc(s_glo, 1)
        gemm_lo(gemms[1])

        def residual(src, gate0, done, last):
            for k in range(KD):
                for g, cols in enumerate((slice(0, TP), slice(TP, T))):
                    stt(hT[:, k, cols], src[:, k, cols], modT[:, gate0 + k, g:g + 1], hT[:, k, cols], ALU.mult,
                        ALU.add).then_inc(done, 1)

        dve.wait_ge(gemms[1].ev, CREDIT + 8)
        residual(yT, 16, s_h1, None)
        norm(norms[1], True)
        gemm_lo(gemms[2])

        for n, (t0, w) in enumerate(TILES):
            dve.wait_ge(s_scev, 4 * n + 4)
            r = slice(0, w)
            lo8, hi8 = slice(0, 8), slice(8, 16)
            link(*[nc.vector.max(val[r, hp, lo8], S[r, hp, :]) for hp in range(16)])
            link(*[nc.vector.match_replace(S2[r, hp, :], val[r, hp, lo8], S[r, hp, :], -3.0e38) for hp in range(16)])
            link(*[nc.vector.max(val[r, hp, hi8], S2[r, hp, :]) for hp in range(16)])
            link(*[nc.vector.max_index(ind[r, hp, lo8], val[r, hp, lo8], S[r, hp, :]) for hp in range(16)],
                 *[nc.vector.max_index(ind[r, hp, hi8], val[r, hp, hi8], S2[r, hp, :]) for hp in range(16)])
            dve.sem_inc(s_cmpd, 1)
            va = val[r].rearrange("p (h a) k -> p h a k", a=2)
            cv = cand[r].rearrange("p h (a b) -> p h a b", a=TOPK)
            link(nc.vector.tensor_copy(indf[r], ind[r]),
                 *[tt(cv[:, h], bc(va[:, h, 0, :], 2, TOPK), bc(va[:, h, 1, :], 1, TOPK), ALU.add) for h in range(PH)])
            link(*[nc.vector.max(tops[r, h, lo8], cand[r, h, :]) for h in range(PH)])
            link(*[nc.vector.match_replace(cand2[r, h, :], tops[r, h, lo8], cand[r, h, :], -3.0e38) for h in range(PH)])
            link(*[nc.vector.max(tops[r, h, hi8], cand2[r, h, :]) for h in range(PH)])
            link(*[nc.vector.max_index(pos[r, h, lo8], tops[r, h, lo8], cand[r, h, :]) for h in range(PH)],
                 *[nc.vector.max_index(pos[r, h, hi8], tops[r, h, hi8], cand2[r, h, :]) for h in range(PH)])
            link(nc.vector.tensor_copy(sm[r, 0, :], tops[r, :, 0]),
                 ts(posa[r], pos[r], 4, None, ALU.logical_shift_right))
            link(tt(tops[r], tops[r], bc(sm[r, 0, :], 2, TOPK), ALU.subtract),
                 nc.vector.tensor_copy(posf[r, 0], posa[r]))
            dve.sem_inc(s_exd, 1)
            link(ts(posa[r], pos[r], 15, None, ALU.bitwise_and))
            link(nc.vector.tensor_copy(posf[r, 1], posa[r]))
            dve.wait_ge(s_exa, n + 1)
            link(nc.vector.tensor_reduce(sm[r, 1, :], ex[r], AX_X, ALU.add))
            link(nc.vector.reciprocal(sm[r, 0, :], sm[r, 1, :]))
            link(tt(gsel[r, n, :].rearrange("p (h k) -> p h k", h=PH), ex[r], bc(sm[r, 0, :], 2, TOPK), ALU.mult))
            for side, dst in enumerate((isel, jsel)):
                link(tt(eq[r], bc(posf[r, side].rearrange("p h k -> p (h k)"), 2, TOPK),
                        bc(iota[r, 0:TOPK], 1, PH * TOPK), ALU.is_equal))
                ev = eq[r].rearrange("p (h k) a -> p h k a", h=PH)
                iv = indf[r].rearrange("p (h a) k -> p h a k", a=2)
                link(*[tt(ev[:, h], ev[:, h], bc(iv[:, h, side, :], 1, TOPK), ALU.mult) for h in range(PH)])
                link(nc.vector.tensor_reduce(dst[r, n, :], eq[r], AX_X, ALU.add))
            dve.sem_inc(s_sel, 1)

        dve.wait_ge(s_selTe, 6)
        nc.vector.tensor_copy(gTh[:], gT[:]).then_inc(s_gsplit, 1)
        dve.wait_ge(s_gsplit, 1)
        tt(gTl[:], gT[:], f(gTh[:]), ALU.subtract).then_inc(s_gsplit, 1)
        dve.wait_ge(s_gsplit, 2)

        def onehot(b):
            for k in range(TB):
                if not (isinstance(b, int) and k < AS):
                    dve.wait_ge(s_gmm, TB * b + k + 1 - AS)
                t = bass.ds(TB * b + k, 1)
                ts(ohB[:, k % AS, :], iota, iT[:, t], f(gTh[:, t]), ALU.is_equal, ALU.mult)
                ts(ohC[:, k % AS, :], iota, iT[:, t], gTl[:, t], ALU.is_equal, ALU.mult).then_inc(s_oh, 1)

        onehot(0)
        with dve.Fori(1, 17) as i:
            onehot(i)

        dve.wait_ge(s_gev, CREDIT + 8 * 17)
        dve.wait_ge(s_gout[0], 16 * 9)
        dve.wait_ge(s_gout[1], 16 * 8)
        link(nc.vector.memset(acc[:], 0.0))
        dve.sem_inc(s_add, 4)

        def u_lo(j, par):
            dve.wait_ge(s_uth, j + 1)
            tt(utl[:, par % 2], PS[:, 0:2, :].rearrange("p b (k i) -> p (b k) i", i=P), f(uth[:, par % 2]),
               ALU.subtract).then_inc(s_utl, 1)

        def v_lo(j, par):
            dve.wait_ge(s_vh, j + 1)
            a, b = (par // 2) % 2, par % 2
            tt(vl[:, a, b, :], vrw[:, a, b, :], f(vh[:, a, b, :]), ALU.subtract).then_inc(s_vl, 1)

        def gate(j, par, i):
            blk = par // JB
            if par % JB == 0:
                dve.wait_ge(s_g[blk], 16 * i + 16)
            dve.wait_ge(s_gel, 2 * j + 2)
            if not isinstance(j, int) or j >= 2:
                dve.wait_ge(s_wh, j - 1)
                dve.wait_ge(s_wl, j - 1)
            tt(wv[:, par % 2, :], gel[:, par % 2, :], G[:, blk, :, par % JB], ALU.mult).then_inc(s_wv, 1)

        def w_lo(j, par):
            dve.wait_ge(s_wh, j + 1)
            tt(wl[:, (par // 2) % 2, par % 2, :], wv[:, par % 2, :], f(wh[:, (par // 2) % 2, par % 2, :]),
               ALU.subtract).then_inc(s_wl, 1)

        def add(pr_, n):
            dve.wait_ge(s_om, 16 * pr_ + n + 1)
            dve.wait_ge(s_add, 16 * pr_ + n - 12 + 4) if not isinstance(pr_, int) or 16 * pr_ + n >= 16 else None
            a = acc[:, n // 2, (n % 2) * HT:(n % 2 + 1) * HT]
            tt(a, a, PS[:, 4 + n % 4, 0:HT], ALU.add).then_inc(s_add, 1)

        def iteration(i, first, last):
            for q in range(4):
                pr_, j = 4 * i + q, 8 * i + 2 * q
                u_lo(j + 1, 2 * q + 1)
                v_lo(j, 2 * q)
                gate(j, 2 * q, i)
                w_lo(j, 2 * q)
                if not (last and q == 3):
                    u_lo(j + 2, 2 * q + 2)
                v_lo(j + 1, 2 * q + 1)
                gate(j + 1, 2 * q + 1, i)
                w_lo(j + 1, 2 * q + 1)
                if not (first and q == 0):
                    for n in range(16):
                        add(pr_ - 1, n)

        u_lo(0, 0)
        iteration(0, True, False)
        with dve.Fori(1, 15) as i:
            iteration(i, False, False)
        iteration(15, False, True)
        for n in range(16):
            add(63, n)
        dve.wait_ge(s_add, 4 + 16 * 64)
        residual(acc, 40, s_h2, None)
        norm(norms[2], False)
        dve.wait_ge(norms[2].tmp, KD)
        for k in range(KD):
            ins = ts(scr2[:, k, :], scr2[:, k, :], rowsT[:, R_FG + k:R_FG + k + 1], None, ALU.mult)
        ins.then_inc(norms[2].y, 1)

    ctx.close()


def pcol(kb):
    return sum(TP - P * n for n in range(kb))


_INS = ['x_prompt', 'x_sample', 'c_prompt', 'c_sample', 'state_ret', 'cache_sb_k', 'cache_sb_v', 'w_ada', 'b_ada',
        'norm1_g', 'w_in', 'ret_norm_g', 'w_out', 'norm2_g', 'peer_w_query', 'peer_sub_keys', 'peer_u', 'peer_v',
        'final_norm_g']
_OUTS = [(1, TP, D), (1, TS, D), (1, 1, NH, P, P), (1, 1, TP, NH, P), (1, 1, TP, NH, P), (1, 1, NH, P, P),
         (1, 1, TS, NH, P), (1, 1, TS, NH, P)]


def kernel(**inputs):
    import concourse.bacc as _bacc
    from concourse.bass_utils import run_bass_kernel_spmd as _run

    nc = _bacc.Bacc("TRN2", target_bir_lowering=False, num_devices=1)
    small, mix = shape_constants()
    arrays, args = {}, []
    for name, a in [(n, np.ascontiguousarray(inputs[n])) for n in _INS] + [("small", small), ("mix", mix)]:
        arrays[f"in_{name}_dram"] = a
        args.append(nc.dram_tensor(f"in_{name}_dram", a.shape, mybir.dt.from_np(a.dtype), kind="ExternalInput").ap())
    args.append(nc.dram_tensor("gates_dram", (P, NJB, T, JB), F32, kind="Internal").ap())
    for i, shape in enumerate(_OUTS):
        args.append(nc.dram_tensor(f"out_{i}_dram", shape, F32, kind="ExternalOutput").ap())
    build(nc, *args)
    r = _run(nc, [arrays], core_ids=[0])
    return tuple(r.results[0][f"out_{i}_dram"] for i in range(len(_OUTS)))
```

```python
from contextlib import ExitStack

import numpy as np

import concourse.bass as bass
from concourse import mybir

F32 = mybir.dt.float32
F32R = mybir.dt.float32r
BF16 = mybir.dt.bfloat16
U32 = mybir.dt.uint32
ALU = mybir.AluOpType
ACT = mybir.ActivationFunctionType
AX_X = mybir.AxisListType.X

P = 128
D = 1024
KD = D // P
TP, TS = 512, 32
T = TP + TS
HT = T // 2
TILES = [(0, 128), (128, 128), (256, 128), (384, 128), (512, 32)]
NH = 4
PAST = 1024
NPB = PAST // P
QB = TP // P
EPS = 1e-6
NIN = 28
RQ, RK, RV, RG, SQ, SK, SV = (4 * n for n in range(7))
PH = 8
NK = 128
TOPK = 16
JB = 4
NJB = NK // JB
TB = 32
SCALE = P ** -0.5
NEG = -1.0e30
OG = 8
NU = NK // 2
UPN = 12
UPG = 4
NG = P // OG
CREDIT = 2

C_ID, C_TRI, C_MASK, C_MIN, C_IOTA, C_KDEC = 0, 128, 256, 384, 512, 640
C_N = C_KDEC + NH * 5
M_DT, M_COS, M_SIN, M_QDEC = 0, NH * TP, NH * TP + T, NH * TP + 2 * T
M_N = M_QDEC + NH * TS
R_C, R_N1, R_N2, R_FG, R_RG, R_B, R_N = 0, 16, 24, 32, 40, 44, 92


def shape_constants():
    i = np.arange(P)
    small = np.zeros((P, C_N), np.float32)
    small[:, C_ID:C_ID + P] = np.eye(P)
    small[:, C_TRI:C_TRI + P] = -(i[:, None] >= i[None, :]).astype(np.float32)
    small[:, C_MASK:C_MASK + P] = (i[:, None] < i[None, :])
    small[:, C_MIN:C_MIN + P] = np.where(i[:, None] < i[None, :], 0.0, NEG)
    small[:, C_IOTA:C_IOTA + P] = i[None, :]
    log_g = np.log1p(-np.exp2(-5.0 - np.arange(NH)))
    for b, (t0, n) in enumerate(TILES):
        last = TP - 1 - t0 if t0 < TP else TS - 1
        for h in range(NH):
            left = last - i
            small[:, C_KDEC + b * NH + h] = np.where(left >= 0, np.exp(np.maximum(left, 0) * log_g[h]), 0.0)
    mix = np.zeros((P, M_N), np.float32)
    x = np.arange(TP)
    for h in range(NH):
        gap = x[None, :] - i[:, None]
        mix[:, M_DT + h * TP:M_DT + (h + 1) * TP] = np.where(gap >= 0, np.exp(np.maximum(gap, 0) * log_g[h]), 0.0)
        mix[:, M_QDEC + h * TS:M_QDEC + (h + 1) * TS] = SCALE * np.exp((np.arange(TS) + 1.0) * log_g[h])[None, :]
    half = P // 2
    inv = np.power(np.float32(10000.0), -np.arange(half, dtype=np.float32) / np.float32(half)).astype(np.float32)
    pos = np.concatenate([np.arange(TP), PAST + np.arange(TS)]).astype(np.float32)
    ang = (inv[:, None] * pos[None, :]).astype(np.float32)
    mix[:half, M_COS:M_COS + T] = mix[half:, M_COS:M_COS + T] = np.cos(ang)
    mix[:half, M_SIN:M_SIN + T] = -np.sin(ang)
    mix[half:, M_SIN:M_SIN + T] = np.sin(ang)
    return small, mix


def build(nc, x_prompt, x_sample, c_prompt, c_sample, state_ret, cache_sb_k, cache_sb_v, w_ada, b_ada, norm1_g, w_in,
          ret_norm_g, w_out, norm2_g, peer_w_query, peer_sub_keys, peer_u, peer_v, final_norm_g, small_c, mix_c,
          gate_dram, act_dram, y_prompt, y_sample, st_prompt, k_prompt, v_prompt, st_sample, k_sample, v_sample):
    ctx = ExitStack()
    BASE = nc.sbuf_base + (-nc.sbuf_base) % 32

    place = {}

    def at(name, off, shape, dt=F32):
        place[name] = off
        return nc.alloc_sbuf_tensor_at(name, [P] + list(shape), dt, offset=BASE + off)

    cst = at("cst", 0, [C_N])
    o = 4 * C_N + 16
    ones = at("ones", o, [P])
    negones = at("negones", o + 512, [P])
    meanw = at("meanw", o + 1024, [P])
    o += 1536
    rowsT = at("rowsT", o, [R_N + 4])
    modT = at("modT", o + 384, [48, 2])
    coefA = at("coefA", o + 768, [2, KD, 2])
    siluT = at("siluT", o + 896, [KD, 2])
    epsc = at("epsc", o + 960, [8])
    assert o + 992 <= 6144
    hT = at("hT", 6144, [KD, T])
    XH = at("XH", 6144 + 17408, [KD, T], F32R)
    XL = at("XL", 6144 + 34816, [KD, T], F32R)
    R0 = 6144 + 52224

    wraw = at("wraw", R0, [2, KD, 512])
    whi = at("whi", R0 + 32768, [2, KD, P], F32R)
    wlo = at("wlo", R0 + 40960, [2, KD, P], F32R)
    RP = R0 + 49152
    projT = at("projT", RP, [NIN, T])
    adaR = at("adaR", RP + 16 * 4 * T, [12, 512])
    scr1 = at("scr1", RP, [KD, T])
    scr2 = at("scr2", RP + 8 * 4 * T, [KD, T])
    sqb = at("sqb", RP + 4 * 4 * T, [NH, T])
    rsb = at("rsb", RP + 8 * 4 * T, [NH, T])
    rs = at("rs", RP + 27 * 4 * T, [T])
    yT = at("yT", RP + 20 * 4 * T, [KD, T])
    RF = RP + NIN * 4 * T
    mixc = at("mixc", RF, [M_N])
    RT = RF + 13056
    rvt = at("rvt", RT, [5, 512])
    svt = at("svt", RT + 10240, [5, 512])
    rkd = at("rkd", RT + 20480, [5, 512])
    xin = at("xin", RT, [5, D])
    rows = at("rows", RT + 20480, [P])
    A0 = 6144 + 17408
    sw = at("sw", A0, [8, T])
    t1 = at("t1", A0 + 17408, [8, T])
    skt = at("skt", A0, [5, 512])
    lk = at("lk", A0 + 10240, [2, 1280])
    aw = at("aw", A0 + 20480, [1, 1280])
    pr = at("pr", A0 + 10240, [2, 1280])
    prs = at("prs", A0 + 25600, [NH, TS])
    qds = at("qds", A0 + 26112, [NH, TS])
    stO = at("stO", A0 + 26624, [NH, P])
    stS = at("stS", A0 + 28672, [NH, P])
    stN = at("stN", A0 + 30720, [NH, P])
    lks = at("lks", A0 + 10240, [NPB + 1, P])
    rsum = at("rsum", A0 + 14848, [NPB - 1, P])
    aws = at("aws", A0 + 20480, [NPB + 1, P])
    kraw = at("kraw", R0, [NPB, 512])
    vraw = at("vraw", R0 + 16384, [NPB, 512])
    kT = at("kT", R0 + 32768, [NH, PAST])

    class Region:

        def __init__(self, start, end):
            self.off, self.end = start, end

        def __call__(self, name, shape, dt=F32):
            t = at(name, self.off, shape, dt)
            self.off += int(np.prod(shape)) * (2 if dt == BF16 else 4)
            self.off += -self.off % 32
            assert self.off <= self.end, name
            return t

    negI = at("negI", 5632, [P], F32R)
    low = Region(R0, R0 + 49152)
    uraw = low("uraw", [2, D])
    uth = low("uth", [2, KD, P], F32R)
    utl = low("utl", [2, KD, P], F32R)
    gel = low("gel", [2, T])
    stored = Region(low.off, low.end)
    val = low("val", [16, TOPK])
    ind = low("ind", [16, TOPK], U32)
    indf = low("indf", [16, TOPK])
    tops = low("tops", [PH, TOPK])
    pos = low("pos", [PH, TOPK], U32)
    posa = low("posa", [PH, TOPK], U32)
    posf = low("posf", [2, PH, TOPK])
    ex = low("ex", [PH, TOPK])
    sm = low("sm", [2, PH])
    sel = low("sel", [3, P])
    selT = low("selT", [3, P])
    keyb = low("keyb", [2, P], BF16)
    gres = low("gres", [2, P])
    gb = low("gb", [3, P], BF16)
    eqb = low("eqb", [P, OG], BF16)
    iotaE = low("iotaE", [P, OG], BF16)
    ohA = low("ohA", [2, P, OG], BF16)
    qT = at("qT", RP, [16, T])
    high = Region(RP + 16 * 4 * T, R0 + 154432)
    skT = high("skT", [16, P])
    S = high("S", [16, P])
    S2 = high("S2", [16, P])
    gst = high("gst", [2, NJB, TB, JB])
    ohB = high("ohB", [3, 2, P, OG], BF16)
    cand = at("cand", place["S"], [PH, 256])
    cand2 = at("cand2", place["S2"], [PH, 256])
    eq = at("eq", place["S2"], [PH * TOPK, TOPK])
    skraw = at("skraw", place["gst"], [16, P])

    al = stored("al", [2, T])
    wv = stored("wv", [2, T])
    mid = Region(RP, RP + 16 * 4 * T)
    vrw = mid("vrw", [2, 2, D])
    G = mid("G", [2, T, JB])
    top = Region(RP + 16 * 4 * T, R0 + 154432)
    vh = top("vh", [2, 2, D], F32R)
    vl = top("vl", [2, 2, D], F32R)
    wh = top("wh", [2, 2, T], F32R)
    wl = top("wl", [2, 2, T], F32R)
    acc = top("acc", [KD, T])
    ys = at("ys", R0, [2, D])

    PS = ctx.enter_context(nc.psum_tensor("PS", [P, 8, 512], F32))

    def sem(name):
        return ctx.enter_context(nc.semaphore(name))

    ident = cst[:, C_ID:C_ID + P]
    ntri = cst[:, C_TRI:C_TRI + P]
    mask = cst[:, C_MASK:C_MASK + P]
    mmin = cst[:, C_MIN:C_MIN + P]
    iota = cst[:, C_IOTA:C_IOTA + P]

    def kdec(b):
        return cst[:, C_KDEC + b * NH:C_KDEC + (b + 1) * NH]

    def bc(ap, axis, n):
        v = ap.unsqueeze(axis)
        shape = list(v.shape)
        shape[axis] = n
        return v.to_broadcast(shape)

    def pair(b):
        return PS[:, b:b + 2, 0:HT]

    def halves(ap):
        return ap.rearrange("p (b t) -> p b t", b=2)

    def f(ap):
        return ap.bitcast(F32)

    def groups_of(ap):
        return (ap[..., 0:TP], ap[..., TP:T])

    s_cst, s_mixc, s_rows, s_x = sem("s_cst"), sem("s_mixc"), sem("s_rows"), sem("s_x")
    s_init = sem("s_init")
    s_w = [sem("s_w0"), sem("s_w1")]
    s_rowsT_ps, s_rowsT = sem("s_rowsT_ps"), sem("s_rowsT")
    s_silu = sem("s_silu")
    s_xT, s_hT = sem("s_xT"), sem("s_hT")
    s_ada_mm, s_ada_row, s_mod_ps = sem("s_ada_mm"), sem("s_ada_row"), sem("s_mod_ps")
    s_dch = sem("s_dch")
    s_ach = sem("s_ach")
    s_coef = sem("s_coef")

    class Stage:
        pass

    norms, gemms = [], []
    for n in range(3):
        st = Stage()
        st.sq, st.ss, st.sd, st.rs, st.tmp, st.y, st.hi, st.lo = (
            sem(f"s_n{n}_{x}") for x in ("sq", "ss", "sd", "rs", "tmp", "y", "hi", "lo"))
        norms.append(st)
    for name, groups, arrived, first in (("in", 7, 6, 0), ("out", 2, 10, 0), ("qry", 4, 11, 0)):
        st = Stage()
        st.name, st.groups = name, groups
        st.hi, st.lo, st.mm, st.ev = (sem(f"s_{name}_{x}") for x in ("hi", "lo", "mm", "ev"))
        gemms.append(st)
    gemms[0].before = (6, 6)
    gemms[1].before = (10, 9)
    gemms[2].before = (11, 10)

    s_swap, s_rope, s_sqs = sem("s_swap"), sem("s_rope"), sem("s_sqs")
    s_tp, s_tm, s_rkd = sem("s_tp"), sem("s_tm"), sem("s_rkd")
    s_kc, s_vc, s_stS = sem("s_kc"), sem("s_vc"), sem("s_stS")
    s_rs_mm, s_rp, s_raux, s_rps, s_ro, s_ros, s_rev, s_rsn, s_qds = (
        sem(x) for x in ("s_rs_mm", "s_rp", "s_raux", "s_rps", "s_ro", "s_ros", "s_rev", "s_rsn", "s_qds"))
    s_bz, s_bln, s_blk, s_bc, s_bmin, s_ba, s_bo, s_bev = (
        sem(x) for x in ("s_bz", "s_bln", "s_blk", "s_bc", "s_bmin", "s_ba", "s_bo", "s_bev"))
    s_kt, s_kte, s_cz, s_cln, s_clk, s_cc, s_cmin, s_ca, s_co, s_cev = (
        sem(x) for x in ("s_kt", "s_kte", "s_cz", "s_cln", "s_clk", "s_cc", "s_cmin", "s_ca", "s_co", "s_cev"))
    s_gm, s_gcen, s_gsq, s_gv, s_gsd, s_gate, s_gy, s_ghi, s_glo = (
        sem(x) for x in ("s_gm", "s_gcen", "s_gsq", "s_gv", "s_gsd", "s_gate", "s_gy", "s_ghi", "s_glo"))
    s_h1, s_zero = sem("s_h1"), sem("s_zero")
    s_skl, s_skp, s_skT = sem("s_skl"), sem("s_skp"), sem("s_skT")
    s_sc, s_scev, s_cmpd, s_exd, s_exa, s_sel = (
        sem(x) for x in ("s_sc", "s_scev", "s_cmpd", "s_exd", "s_exa", "s_sel"))
    s_selT, s_selTe = sem("s_selT"), sem("s_selTe")
    s_oh, s_gmm, s_gev = sem("s_oh"), sem("s_gmm"), sem("s_gev")
    s_pool, s_vpass, s_cch, s_us = sem("s_pool"), sem("s_vpass"), sem("s_cch"), sem("s_us")
    s_ao = [sem("s_ao0"), sem("s_ao1")]
    s_al = [sem("s_al0"), sem("s_al1")]
    s_gout = [sem("s_gout0"), sem("s_gout1")]
    s_u = [sem("s_u0"), sem("s_u1")]
    s_v = [sem("s_v0"), sem("s_v1")]
    s_g = [sem("s_g0"), sem("s_g1")]
    s_ut, s_uth, s_utl, s_up, s_gel, s_wv, s_wh, s_wl, s_vh, s_vl, s_om, s_add, s_acc0 = (
        sem(x) for x in ("s_ut", "s_uth", "s_utl", "s_up", "s_gel", "s_wv", "s_wh", "s_wl", "s_vh", "s_vl", "s_om",
                         "s_add", "s_acc0"))
    s_h2 = sem("s_h2")
    s_yt, s_ye = sem("s_yt"), sem("s_ye")
    s_yo = [sem("s_yo0"), sem("s_yo1")]
    s_out = sem("s_out")

    def w_view(w, g):
        return w[0].rearrange("(k p) n -> p k n", p=P)[:, :, bass.ds(g * 512, 512)]

    u_d = peer_u[0].rearrange("(j p) d -> p j d", p=P)
    v_d = peer_v[0].rearrange("(j p) d -> p j d", p=P)

    block = ctx.enter_context(nc.Block())

    @block.sync
    def _(sp):
        n_out = [0]

        def store(dst, src):
            sp.dma_start(dst, src).then_inc(s_out, 16)
            n_out[0] += 1

        sp.dma_start(rows[R_C:R_C + 8, :], c_prompt[0].rearrange("(k p) -> k p", p=P)).then_inc(s_rows, 16)
        sp.dma_start(rows[R_C + 8:R_C + 16, :], c_sample[0].rearrange("(k p) -> k p", p=P)).then_inc(s_rows, 16)
        sp.dma_start(rows[R_N1:R_N1 + 8, :], norm1_g[0].rearrange("(k p) -> k p", p=P)).then_inc(s_rows, 16)
        sp.dma_start(rows[R_N2:R_N2 + 8, :], norm2_g[0].rearrange("(k p) -> k p", p=P)).then_inc(s_rows, 16)
        sp.dma_start(rows[R_FG:R_FG + 8, :], final_norm_g.rearrange("(k p) -> k p", p=P)).then_inc(s_rows, 16)
        sp.dma_start(rows[R_RG:R_RG + 4, :], ret_norm_g[0].rearrange("(k p) -> k p", p=P)).then_inc(s_rows, 16)
        sp.dma_start(rows[R_B:R_B + 48, :], b_ada[0].rearrange("(k p) -> k p", p=P)).then_inc(s_rows, 16)
        sp.dma_start(cst[:], small_c).then_inc(s_cst, 16)

        def ada_load(g, slot):
            sp.dma_start(wraw[:, slot], w_view(w_ada, g)).then_inc(s_w[slot], 16)

        ada_load(0, 0)
        ada_load(1, 1)
        sp.dma_start(xin[:, 0:4, :], x_prompt[0].rearrange("(b p) d -> p b d", p=P)).then_inc(s_x, 16)
        sp.dma_start(xin[0:TS, 4, :], x_sample[0]).then_inc(s_x, 16)
        sp.dma_start(mixc[:], mix_c).then_inc(s_mixc, 16)
        with sp.Fori(1, 6) as i:
            for slot in range(2):
                sp.wait_ge(s_ada_mm, 2 * i + slot - 1)
                ada_load(2 * i + slot, slot)

        def gemm_loads(st, w, first_waits):
            for slot in range(2):
                for s, v in first_waits[slot]:
                    sp.wait_ge(s, v)
                sp.dma_start(wraw[:, slot], w_view(w, slot)).then_inc(s_w[slot], 16)
            if st.groups // 2 > 1:
                with sp.Fori(1, st.groups // 2) as i:
                    for slot in range(2):
                        g = 2 * i + slot
                        sp.wait_ge(st.lo, 4 * g - 4)
                        sp.dma_start(wraw[:, slot], w_view(w, g)).then_inc(s_w[slot], 16)
            if st.groups % 2:
                g = st.groups - 1
                sp.wait_ge(st.lo, 4 * g - 4)
                sp.dma_start(wraw[:, 0], w_view(w, g)).then_inc(s_w[0], 16)

        gemm_loads(gemms[0], w_in, (((s_ada_mm, 11),), ((s_ada_mm, 12),)))
        sp.wait_ge(gemms[0].lo, NIN)
        sp.dma_start(kraw[:], cache_sb_k[0, 0].rearrange("(b p) h d -> p b (h d)", p=P)).then_inc(s_kc, 16)
        sp.dma_start(vraw[:], cache_sb_v[0, 0].rearrange("(b p) h d -> p b (h d)", p=P)).then_inc(s_vc, 16)
        sp.wait_ge(s_rope, 3)
        sp.dma_start(stS[:], state_ret[0, 0].rearrange("h k v -> k h v")).then_inc(s_stS, 16)
        sp.wait_ge(s_tm, 10)
        store(v_prompt[0, 0].rearrange("(b p) h d -> p b (h d)", p=P), svt[:, 0:4, :])
        store(v_sample[0, 0].rearrange("p h d -> p (h d)"), svt[0:TS, 4, :])
        sp.wait_ge(s_tm, 15)
        store(k_prompt[0, 0].rearrange("(b p) h d -> p b (h d)", p=P), skt[:, 0:4, :])
        store(k_sample[0, 0].rearrange("p h d -> p (h d)"), skt[0:TS, 4, :])
        sp.wait_ge(s_rev, 3 * NH)
        store(st_prompt[0, 0].rearrange("h k v -> k h v"), stO[:])
        sp.wait_ge(s_rsn, NH)
        store(st_sample[0, 0].rearrange("h k v -> k h v"), stN[:])
        sp.wait_ge(s_out, 16 * n_out[0])

        gemm_loads(gemms[1], w_out, (((s_kt, NPB),), ((s_co, 1),)))
        gemm_loads(gemms[2], peer_w_query, (((gemms[1].lo, 4),), ((gemms[1].lo, 8),)))
        sp.wait_ge(gemms[1].ev, CREDIT + 8)
        sp.dma_start(skraw[:], peer_sub_keys[0].rearrange("a h k d -> k (a h) d")).then_inc(s_skl, 16)

        def u_load(tile, slot):
            sp.dma_start(uraw[:, slot], u_d[:, bass.ds(tile, 1), :].rearrange("p a d -> p (a d)")
                         ).then_inc(s_u[slot], 16)

        def v_load(pr_, slot):
            sp.dma_start(vrw[:, slot], v_d[:, bass.ds(2 * pr_, 2), :]).then_inc(s_v[slot], 16)

        def a_load(pr_, slot):
            sp.dma_start(al[:, slot], act_dram[:, bass.ds(pr_, 1), :].rearrange("p a t -> p (a t)")
                         ).then_inc(s_al[slot], 16)

        def g_load(b, slot):
            sp.dma_start(G[:, slot], gate_dram[:, bass.ds(b, 1), :, :].rearrange("p a t j -> p (a t) j")
                         ).then_inc(s_g[slot], 16)

        def g_store(n, q):
            b = 4 * n + q
            sp.wait_ge(s_gev, CREDIT + 8 * b + 8)
            sp.dma_start(gate_dram[:, :, bass.ds(TB * b, TB), :], gst[:, q % 2]).then_inc(s_gout[q % 2], 16)

        def u_next(m, par, tile=None):
            sp.wait_ge(s_ut, m + 1)
            u_load(2 * m + 4 if tile is None else tile, par)

        sp.wait_ge(gemms[2].lo, 16)
        u_load(0, 0)
        u_load(2, 1)

        def choice(n):
            for k in range(UPN):
                u_next(UPN * n + k, k % 2)
                if k >= UPN - UPG:
                    g_store(n, k - (UPN - UPG))

        with sp.Fori(0, 4) as n:
            choice(n)
        sp.wait_ge(s_sc, 20)
        v_load(0, 0)
        v_load(1, 1)
        for m in range(4 * UPN, NU):
            u_next(m, m % 2, None if m < NU - 2 else 2 * (m - (NU - 2)) + 1)
            if m == 5 * UPN - UPG:
                g_store(4, 0)
        sp.wait_ge(s_gout[0], 16 * 9)
        sp.wait_ge(s_gout[1], 16 * 8)
        g_load(0, 0)
        g_load(1, 1)
        for slot in range(2):
            sp.wait_ge(s_ao[slot], 16 * NU // 2)
        a_load(0, 0)
        a_load(1, 1)

        def expert_loads(i, last):
            for q in range(4):
                pr_ = 4 * i + q
                if not (last and q >= 2):
                    sp.wait_ge(s_ut, NU + pr_ + 1)
                    u_load(2 * pr_ + 5, q % 2)
                    sp.wait_ge(s_wv, 2 * pr_ + 1)
                    a_load(pr_ + 2, q % 2)
                    sp.wait_ge(s_vl, 2 * pr_ + 2)
                    v_load(pr_ + 2, q % 2)
                if q % 2 and not last:
                    sp.wait_ge(s_wv, 2 * pr_ + 2)
                    g_load(2 * i + q // 2 + 2, q // 2)

        with sp.Fori(0, 15) as i:
            expert_loads(i, False)
        expert_loads(15, True)

        for n, (t0, w) in enumerate(TILES):
            sp.wait_ge(s_ye, n + 1)
            dst = y_prompt[0, t0:t0 + w, :] if t0 < TP else y_sample[0]
            sp.dma_start(dst, ys[0:w, n % 2, :]).then_inc(s_yo[n % 2], 16)
        sp.wait_ge(s_yo[0], 48)
        sp.wait_ge(s_yo[1], 32)
        sp.wait_ge(s_out, 16 * n_out[0])

    @block.tensor
    def _(pe):
        mm = nc.tensor.matmul

        def mm3(out, ah, al, bh, bl, start, stop):
            mm(out, ah, bh, start=start, stop=False)
            mm(out, ah, bl, start=False, stop=False)
            return mm(out, al, bh, start=False, stop=stop)

        def norm(st, squares):
            for k in range(KD):
                pe.wait_ge(st.sq, k + 1)
                for b in range(2):
                    last = mm(PS[:, b, 0:HT], ones[:], squares[:, k, b * HT:(b + 1) * HT], start=(k == 0),
                              stop=(k == KD - 1))
            last.then_inc(st.ss, 1)

        def gemm(st):
            pe.sem_inc(st.mm, CREDIT)

            def group(g, slot):
                for cc in range(4):
                    c = 4 * g + cc
                    par = cc % 2
                    pe.wait_ge(st.lo, c + 1)
                    pe.wait_ge(st.ev, c + 1)
                    for b in range(2):
                        for k in range(KD):
                            last = mm3(PS[:, 2 * par + b, 0:HT], whi[:, par, k, :], wlo[:, par, k, :],
                                       XH[:, k, b * HT:(b + 1) * HT], XL[:, k, b * HT:(b + 1) * HT],
                                       k == 0, k == KD - 1)
                    last.then_inc(st.mm, 1)

            with pe.Fori(0, st.groups // 2) as i:
                for slot in range(2):
                    group(2 * i + slot, slot)
            if st.groups % 2:
                group(st.groups - 1, 0)

        pe.wait_ge(s_cst, 16)
        pe.wait_ge(s_rows, 16 * 7)
        nc.tensor.transpose(PS[:, 6, 0:R_N], rows[0:R_N, :], ident[0:R_N, 0:R_N]).then_inc(s_rowsT_ps, 1)
        pe.wait_ge(s_x, 32)
        for n, (t0, w) in enumerate(TILES):
            if n >= 2:
                pe.wait_ge(s_hT, n - 1)
            b = 2 + 2 * (n % 2)
            for k in range(KD):
                last = nc.tensor.transpose(PS[:, b + k // 4, (k % 4) * P:(k % 4) * P + w],
                                           xin[0:w, n, k * P:(k + 1) * P], ident[0:w, 0:w])
            last.then_inc(s_xT, 1)
        pe.wait_ge(s_silu, 1)
        with pe.Fori(0, 6) as i:
            for slot in range(2):
                g = 2 * i + slot
                pe.wait_ge(s_w[slot], 16 * i + 16)
                pe.wait_ge(s_ada_row, g + 1)
                for k in range(KD):
                    last = mm(PS[0:2, slot, :], siluT[:, k, :], wraw[:, slot, k, :], start=(k == 0),
                              stop=(k == KD - 1))
                last.then_inc(s_ada_mm, 1)
        pe.wait_ge(s_ada_row, CREDIT + 12)
        for n in range(48):
            last = nc.tensor.transpose(PS[:, 6, 2 * n:2 * n + 2], adaR[0:2, n // 4, (n % 4) * P:(n % 4) * P + P],
                                       ident[0:2, 0:2])
        last.then_inc(s_mod_ps, 1)
        pe.wait_ge(s_init, 1)
        norm(norms[0], scr1)
        pe.wait_ge(norms[0].lo, KD)
        pe.wait_ge(norms[0].hi, KD)
        pe.wait_ge(norms[0].sd, 1)
        gemm(gemms[0])

        pe.wait_ge(gemms[0].ev, CREDIT + NIN)
        n = 0
        for chunk in (RV, SV, SK, RK):
            if chunk == RK:
                pe.wait_ge(s_rope, 3)
            for t0, w in TILES:
                if n >= 4:
                    m = n - 4
                    if m < 15:
                        pe.wait_ge(s_tm, m + 1)
                    else:
                        pe.wait_ge(s_rkd, m - 14)
                for h in range(NH):
                    last = nc.tensor.transpose(PS[0:w, n % 4, h * P:(h + 1) * P], projT[:, chunk + h, t0:t0 + w], ident)
                last.then_inc(s_tp, 1)
                n += 1

        pe.wait_ge(s_rkd, 5)
        pe.wait_ge(s_tm, 15)
        pe.wait_ge(s_stS, 16)
        pe.wait_ge(s_qds, 2)
        for h in range(NH):
            hs = slice(h * P, (h + 1) * P)
            for kb in range(QB):
                if h >= 1:
                    pe.wait_ge(s_rp, QB * (h - 1) + kb + 1)
                mm(PS[:, kb, 0:TP - P * kb], projT[:, RK + h, kb * P:(kb + 1) * P], projT[:, RQ + h, kb * P:TP],
                   start=True, stop=True).then_inc(s_rs_mm, 1)
            if h >= 2:
                pe.wait_ge(s_rev, 3 * (h - 1))
                pe.wait_ge(s_rsn, h - 1)
                pe.wait_ge(s_rps, h - 1)
            aux = 6 + h % 2
            for kb in range(QB):
                mm(PS[:, aux, 0:P], rkd[:, kb, hs], rvt[:, kb, hs], start=(kb == 0), stop=(kb == QB - 1))
            mm(PS[0:TS, aux, P:P + TS], projT[:, RK + h, TP:T], projT[:, RQ + h, TP:T], start=True, stop=True)
            mm(PS[:, aux, 256:384], rkd[0:TS, 4, hs], rvt[0:TS, 4, hs], start=True, stop=True).then_inc(s_raux, 1)
            for kb in range(QB):
                pe.wait_ge(s_rp, QB * h + kb + 1)
                last = mm(PS[:, 4 + h % 2, kb * P:TP], rvt[:, kb, hs], pr[:, h % 2, pcol(kb):pcol(kb) + TP - P * kb],
                          start=(kb == 0), stop=(kb == QB - 1))
            last.then_inc(s_ro, 1)
            pe.wait_ge(s_rps, h + 1)
            pe.wait_ge(s_rsn, h + 1)
            mm(PS[:, aux, 384:384 + TS], stS[:, h, :], qds[:, h, :], start=True, stop=False)
            mm(PS[:, aux, 384:384 + TS], rvt[:, 4, hs], prs[:, h, :], start=False, stop=True).then_inc(s_ros, 1)

        pe.wait_ge(s_sqs, 1)
        pe.wait_ge(s_rev, 3 * NH)
        pe.wait_ge(s_rsn, NH)
        for h in range(NH):
            hs = slice(h * P, (h + 1) * P)
            for kb in range(QB):
                if h >= 1:
                    pe.wait_ge(s_ba, 7 * h)
                mm(PS[:, kb, 0:TP - P * kb], projT[:, SK + h, kb * P:(kb + 1) * P], projT[:, SQ + h, kb * P:TP],
                   start=True, stop=True).then_inc(s_bz, 1)
            pe.wait_ge(s_blk, QB * (h + 1))
            for kb in reversed(range(QB)):
                w = TP - P * kb
                last = mm(PS[:, kb, 0:w], ntri, lk[:, h % 2, pcol(kb):pcol(kb) + w], start=False, stop=(kb == QB - 1),
                          skip_group_check=True)
                for later in range(kb + 1, QB):
                    wl_ = TP - P * later
                    last = mm(PS[:, kb, w - wl_:w], negones[:], lk[:, h % 2, pcol(later):pcol(later) + wl_],
                              start=False, stop=(later == QB - 1), skip_group_check=True)
                last.then_inc(s_bc, 1)
            pe.wait_ge(s_ba, 7 * (h + 1))
            if h >= 2:
                pe.wait_ge(s_bev, h - 1)
            for kb in range(QB):
                last = mm(PS[:, 4 + h % 2, kb * P:TP], svt[:, kb, hs], aw[:, 0, pcol(kb):pcol(kb) + TP - P * kb],
                          start=(kb == 0), stop=(kb == QB - 1))
            last.then_inc(s_bo, 1)

        pe.wait_ge(s_kc, 16)
        for b in range(NPB):
            if b >= 2:
                pe.wait_ge(s_kte, b - 1)
            for h in range(NH):
                last = nc.tensor.transpose(PS[:, 6 + b % 2, h * P:(h + 1) * P], kraw[:, b, h * P:(h + 1) * P], ident)
            last.then_inc(s_kt, 1)
        pe.wait_ge(s_kte, NPB)
        for b in range(NPB):
            for h in range(NH):
                mm(PS[:, b // 4, (b % 4) * P + h * TS:(b % 4) * P + (h + 1) * TS], kT[:, h, b * P:(b + 1) * P],
                   projT[:, SQ + h, TP:T], start=(b % 4 == 0 and h == 0), stop=(b % 4 == 3 and h == NH - 1),
                   skip_group_check=True)
        for h in range(NH):
            last = mm(PS[0:TS, 2, h * TS:(h + 1) * TS], projT[:, SK + h, TP:T], projT[:, SQ + h, TP:T],
                      start=(h == 0), stop=(h == NH - 1), skip_group_check=True)
        last.then_inc(s_cz, 1)
        pe.wait_ge(s_clk, 1)
        for b in range(NPB):
            out = PS[:, b // 4, (b % 4) * P:(b % 4 + 1) * P]
            mm(out, ntri, lks[:, b, :], start=False, stop=False, skip_group_check=True)
            if b < NPB - 1:
                mm(out, negones[:], rsum[:, b, :], start=False, stop=False, skip_group_check=True)
            mm(out, negones[:], lks[:, NPB, :], start=False, stop=True, skip_group_check=True)
        mm(PS[0:TS, 2, 0:P], ntri[:, 0:TS], lks[:, NPB, :], start=False, stop=True,
           skip_group_check=True).then_inc(s_cc, 1)
        pe.wait_ge(s_ca, 2)
        pe.wait_ge(s_vc, 16)
        for h in range(NH):
            hs = slice(h * P, (h + 1) * P)
            for b in range(NPB + 1):
                lhs = vraw[:, b, hs] if b < NPB else svt[:, 4, hs]
                last = mm(PS[:, 3, h * TS:(h + 1) * TS], lhs, aws[:, b, h * TS:(h + 1) * TS], start=(b == 0),
                          stop=(b == NPB))
        last.then_inc(s_co, 1)

        pe.wait_ge(s_cev, 1)
        pe.wait_ge(s_bev, NH)
        for h in range(NH):
            for b in range(2):
                last = mm(PS[:, 2 * h + b, 0:HT], meanw[:], projT[:, h, b * HT:(b + 1) * HT], start=True, stop=True)
            last.then_inc(s_gm, 1)
        for h in range(NH):
            pe.wait_ge(s_gsq, h + 1)
            for b in range(2):
                last = mm(PS[:, 2 * h + b, 0:HT], meanw[:], sqb[:, h, b * HT:(b + 1) * HT], start=True, stop=True)
            last.then_inc(s_gv, 1)
        pe.wait_ge(s_gsd, NH)
        pe.wait_ge(s_ghi, 2)
        pe.wait_ge(s_glo, 2)
        gemm(gemms[1])
        pe.wait_ge(gemms[1].ev, CREDIT + 8)
        norm(norms[1], scr1)
        pe.wait_ge(norms[1].lo, KD)
        pe.wait_ge(norms[1].hi, KD)
        pe.wait_ge(norms[1].sd, 1)
        gemm(gemms[2])

        pe.wait_ge(s_skl, 16)
        for n in range(4):
            for m in range(4):
                last = nc.tensor.transpose(PS[:, 4 + n, m * P:(m + 1) * P], skraw[:, 4 * n + m, :], ident)
        last.then_inc(s_skp, 1)
        pe.wait_ge(s_skT, 1)
        pe.wait_ge(gemms[2].ev, CREDIT + 16)

        def scores(n, w):
            for hp in range(16):
                last = mm(PS[0:w, 4 + hp // 4, (hp % 4) * P:(hp % 4 + 1) * P], qT[:, hp, bass.ds(P * n, w)],
                          skT[:, (hp % 2) * PH + hp // 2, :], start=True, stop=True)
                if hp % 4 == 3:
                    last.then_inc(s_sc, 1)

        def turn(m, par, arrivals):
            pe.wait_ge(s_u[par], 16 * arrivals)
            if not isinstance(m, int) or m >= 1:
                pe.wait_ge(s_utl, m)
            for k in range(KD):
                last = mm(PS[:, k // 4, (k % 4) * P:(k % 4 + 1) * P], uraw[:, par, k * P:(k + 1) * P], ident,
                          start=(k % 4 == 0), stop=(k % 4 == 3), is_transpose=True, skip_group_check=True)
            last.then_inc(s_ut, 1)

        def less_hi(m, par):
            pe.wait_ge(s_uth, m + 1)
            for b in range(2):
                last = mm(PS[:, b, :], negI[:], uth[:, par, 4 * b:4 * b + 4, :].rearrange("p k i -> p (k i)"),
                          start=False, stop=True, skip_group_check=True)
            last.then_inc(s_us, 1)

        def up(m, par, b, first):
            if b == 0:
                pe.wait_ge(s_utl, m + 1)
            if not first:
                pe.wait_ge(s_gel, 2 * m - 1 + b)
            for k in range(KD):
                last = mm3(PS[:, 2 + b, 0:HT], uth[:, par, k, :], utl[:, par, k, :],
                           XH[:, k, b * HT:(b + 1) * HT], XL[:, k, b * HT:(b + 1) * HT], k == 0, k == KD - 1)
            last.then_inc(s_up, 1)

        def u_half(m, b, first=False):
            par = m % 2
            if b == 0:
                turn(m + 1, 1 - par, (m + 1) // 2 + 1)
            up(m, par, b, first)
            if b == 0:
                less_hi(m + 1, 1 - par)

        def gates(n, g):
            for r in range(OG // 4):
                pe.wait_ge(s_gev, 2 * (NG * n + g) + r + 1)
                if r == 0:
                    pe.wait_ge(s_oh, NG * n + g + 1)
                for x in range(4):
                    for part in range(3):
                        last = mm(PS[:, 4 + r, x * P:(x + 1) * P], ohA[:, g % 2, :, 4 * r + x],
                                  ohB[:, part, g % 2, :, 4 * r + x], start=(part == 0), stop=(part == 2))
                last.then_inc(s_gmm, 1)

        def sel_turn(n, w):
            pe.wait_ge(s_sel, n + 1)
            for c in range(3):
                last = nc.tensor.transpose(PS[:, 6, c * P:c * P + w], sel[0:w, c, :], ident[0:w, 0:w])
            last.then_inc(s_selT, 1)

        def choice(n, w_next):
            for k in range(UPN - UPG):
                if k == UPN - UPG - 1:
                    sel_turn(n, P)
                u_half(UPN * n + k, 0, n == 0 and k == 0)
                u_half(UPN * n + k, 1, n == 0 and k == 0)
            for g in range(NG):
                if g == NG - 4:
                    pe.wait_ge(s_scev, 4 * n + 6)
                gates(n, g)
                if g == NG - 5:
                    pe.wait_ge(s_gev, CREDIT + 2 * (NG * n + g + 1))
                    scores(n + 1, w_next)
                if g % 2:
                    u_half(UPN * n + UPN - UPG + g // 4, g // 2 % 2)

        scores(0, P)
        turn(0, 0, 1)
        less_hi(0, 0)
        for n in range(4):
            choice(n, P if n < 3 else TS)
        for m in range(4 * UPN, NU):
            if m == 5 * UPN - UPG - 1:
                sel_turn(4, TS)
            for b in range(2):
                if m == 5 * UPN - UPG:
                    gates(4, 2 * b)
                    gates(4, 2 * b + 1)
                u_half(m, b)

        def down(pr_, par):
            pe.wait_ge(s_vl, 2 * pr_ + 2)
            pe.wait_ge(s_wl, 2 * pr_ + 2)
            for n in range(16):
                dc, b = n // 2, n % 2
                pe.wait_ge(s_add, 16 * pr_ + n + 1)
                for r in range(2):
                    last = mm3(PS[:, 4 + n % 4, 0:HT], vh[:, par, r, dc * P:(dc + 1) * P],
                               vl[:, par, r, dc * P:(dc + 1) * P], wh[:, par, r, b * HT:(b + 1) * HT],
                               wl[:, par, r, b * HT:(b + 1) * HT], r == 0, r == 1)
                last.then_inc(s_om, 1)

        def iteration(i, first, last):
            for q in range(4):
                pr_ = 4 * i + q
                up(NU + pr_, q % 2, 0, False)
                up(NU + pr_, q % 2, 1, False)
                if not (last and q == 3):
                    turn(NU + pr_ + 1, (q + 1) % 2, NU // 2 + 2 * i + (q + 1) // 2 + 1)
                if not (first and q == 0):
                    down(pr_ - 1, (q + 1) % 2)

        iteration(0, True, False)
        with pe.Fori(1, 15) as i:
            iteration(i, False, False)
        iteration(15, False, True)
        down(63, 1)

        norm(norms[2], scr1)
        pe.wait_ge(norms[2].y, 1)
        for n, (t0, w) in enumerate(TILES):
            if n >= 2:
                pe.wait_ge(s_ye, n - 1)
            b = 2 + 2 * (n % 2)
            for k in range(KD):
                last = nc.tensor.transpose(PS[0:w, b + k // 4, (k % 4) * P:(k % 4 + 1) * P], scr2[:, k, t0:t0 + w],
                                           ident)
            last.then_inc(s_yt, 1)

    @block.scalar
    def _(act):
        act_ = nc.scalar.activation
        chain = [0]

        def link(ins):
            chain[0] += 1
            ins.then_inc(s_ach, 1)
            act.wait_ge(s_ach, chain[0])

        def squares(st, ready):
            for k in range(KD):
                if k == 0 or len(ready) == KD:
                    act.wait_ge(*ready[k])
                act_(scr1[:, k, :], hT[:, k, :], ACT.Square).then_inc(st.sq, 1)
            act.wait_ge(st.ss, 1)
            act_(halves(rs[:]), pair(0), ACT.Sqrt, bias=epsc[:, 0:1], scale=1.0 / D).then_inc(st.sd, 1)

        def modulated(st, n):
            for k in range(KD):
                act.wait_ge(st.tmp, k + 1)
                for g, cols in enumerate((slice(0, TP), slice(TP, T))):
                    act_(scr1[:, k, cols], scr2[:, k, cols], ACT.Identity, scale=coefA[:, n, k, g:g + 1],
                         bias=modT[:, 24 * n + k, g:g + 1]).then_inc(st.y, 1)
                act.wait_ge(st.y, 2 * k + 2)
                act_(XH[:, k, :], scr1[:, k, :], ACT.Copy).then_inc(st.hi, 1)

        def gemm_out(st, out):
            act.sem_inc(st.ev, CREDIT)

            def group(g):
                for cc in range(4):
                    c = 4 * g + cc
                    act.wait_ge(st.mm, c + 1 + CREDIT)
                    act_(out[:, bass.ds(c, 1), :].rearrange("p a (b t) -> p (a b) t", b=2), pair(2 * (cc % 2)),
                         ACT.Copy).then_inc(st.ev, 1)

            with act.Fori(0, st.groups) as g:
                group(g)

        act.wait_ge(s_rowsT, 1)
        act_(siluT[:].rearrange("p k g -> p g k"), rowsT[:, 0:16].rearrange("p (g k) -> p g k", g=2),
             ACT.Silu).then_inc(s_silu, 1)
        act.wait_ge(s_init, 1)
        squares(norms[0], [(s_hT, 5)])
        act.wait_ge(s_coef, 1)
        modulated(norms[0], 0)
        gemm_out(gemms[0], projT)

        act.wait_ge(gemms[0].ev, CREDIT + NIN)
        act.wait_ge(gemms[0].mm, CREDIT + NIN)
        act_(sw[0:64], projT[64:128, 0:8, :], ACT.Copy).then_inc(s_swap, 1)
        for n in range(15):
            act.wait_ge(s_tp, n + 1)
            if n == 0:
                act.wait_ge(s_zero, 2)
            if n == 10:
                act.wait_ge(s_rope, 3)
            t0, w = TILES[n % 5]
            dst = (rvt, svt, skt)[n // 5]
            act_(dst[0:w, n % 5, :], PS[0:w, n % 4, :], ACT.Copy).then_inc(s_tm, 1)
        for h in range(NH):
            act.wait_ge(s_raux, h + 1)
            act_(stO[:, h, :], PS[:, 6 + h % 2, 0:P], ACT.Copy).then_inc(s_rev, 1)
            act.wait_ge(s_ro, h + 1)
            act_(projT[:, RQ + h, 0:TP], PS[:, 4 + h % 2, :], ACT.Copy).then_inc(s_rev, 1)
            act.wait_ge(s_ros, h + 1)
            act_(projT[:, RQ + h, TP:T], PS[:, 6 + h % 2, 384:384 + TS], ACT.Copy).then_inc(s_rev, 1)
        nc.scalar.preload_act_table_set("natural_log_exp_and_others")
        for h in range(NH):
            par = h % 2
            act.wait_ge(s_bz, QB * (h + 1))
            if h >= 2:
                act.wait_ge(s_bo, h - 1)
            def lkv(kb):
                return lk[:, par, pcol(kb):pcol(kb) + TP - P * kb]
            for kb in range(QB):
                act_(lkv(kb), PS[:, kb, 0:TP - P * kb], ACT.Abs).then_inc(s_ach, 1)
            chain[0] += QB
            act.wait_ge(s_ach, chain[0])
            link(act_(lk[:, par, :], lk[:, par, :], ACT.Exp, scale=-1.0))
            act_(lk[:, par, :], lk[:, par, :], ACT.Ln, bias=1.0).then_inc(s_bln, 1)
            if h >= 1:
                act.wait_ge(s_bo, h)
            for kb in reversed(range(QB)):
                w = TP - P * kb
                act.wait_ge(s_bmin, QB * h + QB - kb)
                if w > P:
                    act_(aw[:, 0, pcol(kb) + P:pcol(kb) + w], PS[:, kb, P:w], ACT.Exp).then_inc(s_ba, 1)
                act_(aw[:, 0, pcol(kb):pcol(kb) + P], aw[:, 0, pcol(kb):pcol(kb) + P], ACT.Exp).then_inc(s_ba, 1)
            act.wait_ge(s_bo, h + 1)
            act_(projT[:, SQ + h, 0:TP], PS[:, 4 + par, :], ACT.Copy).then_inc(s_bev, 1)
        for b in range(NPB):
            act.wait_ge(s_kt, b + 1)
            act_(kT[:, :, b * P:(b + 1) * P], PS[:, 6 + b % 2, :].rearrange("p (h k) -> p h k", h=NH),
                 ACT.Copy).then_inc(s_kte, 1)
        act.wait_ge(s_cz, 1)
        act.wait_ge(s_zero, 4)
        act_(lks[:, 0:NPB, :], PS[:, 0:2, :].rearrange("p b (c x) -> p (b c) x", x=P), ACT.Abs).then_inc(s_ach, 1)
        act_(lks[0:TS, NPB, :], PS[0:TS, 2, 0:P], ACT.Abs).then_inc(s_ach, 1)
        chain[0] += 2
        act.wait_ge(s_ach, chain[0])
        act_(lks[:, 0:NPB, :], lks[:, 0:NPB, :], ACT.Exp, scale=-1.0).then_inc(s_ach, 1)
        act_(lks[0:TS, NPB, :], lks[0:TS, NPB, :], ACT.Exp, scale=-1.0).then_inc(s_ach, 1)
        chain[0] += 2
        act.wait_ge(s_ach, chain[0])
        act_(lks[:, 0:NPB, :], lks[:, 0:NPB, :], ACT.Ln, bias=1.0).then_inc(s_cln, 1)
        act_(lks[0:TS, NPB, :], lks[0:TS, NPB, :], ACT.Ln, bias=1.0).then_inc(s_cln, 1)
        act.wait_ge(s_cc, 1)
        act_(aws[:, 0:NPB, :], PS[:, 0:2, :].rearrange("p b (c x) -> p (b c) x", x=P), ACT.Exp).then_inc(s_ca, 1)
        act.wait_ge(s_cmin, 1)
        act_(aws[0:TS, NPB, :], aws[0:TS, NPB, :], ACT.Exp).then_inc(s_ca, 1)
        act.wait_ge(s_co, 1)
        act_(projT[:, SQ:SQ + NH, TP:T], PS[:, 3, 0:P].rearrange("p (h t) -> p h t", h=NH),
             ACT.Copy).then_inc(s_cev, 1)
        act_(projT[:, RG:RG + NH, :], projT[:, RG:RG + NH, :], ACT.Silu).then_inc(s_gate, 1)
        act.wait_ge(s_cev, 1)
        act.wait_ge(s_out, 96)
        act_(XH[:, 4:8, :], projT[:, SQ:SQ + NH, :], ACT.Copy).then_inc(s_ghi, 1)
        for h in range(NH):
            act.wait_ge(s_gcen, h + 1)
            act_(sqb[:, h, :], projT[:, h, :], ACT.Square).then_inc(s_gsq, 1)
        for h in range(NH):
            act.wait_ge(s_gv, h + 1)
            act_(halves(rsb[:, h, :]), pair(2 * h), ACT.Sqrt, bias=epsc[:, 0:1]).then_inc(s_gsd, 1)
        act.wait_ge(s_gy, 4)
        act_(XH[:, 0:4, :], projT[:, 0:4, :], ACT.Copy).then_inc(s_ghi, 1)
        gemm_out(gemms[1], yT)
        squares(norms[1], [(s_h1, 2 * (k + 1)) for k in range(KD)])
        modulated(norms[1], 1)
        act.wait_ge(norms[1].lo, KD)
        gemm_out(gemms[2], qT)
        act.wait_ge(s_skp, 1)
        act_(skT[:].rearrange("p (b m) k -> p b (m k)", b=4), PS[:, 4:8, :], ACT.Copy).then_inc(s_skT, 1)

        def scores_out(n, w):
            for q in range(4):
                act.wait_ge(s_sc, 4 * n + q + 1)
                if q == 0 and (not isinstance(n, int) or n >= 1):
                    act.wait_ge(s_sel, n)
                act_(S[0:w, 4 * q:4 * q + 4, :], PS[0:w, 4 + q, :].rearrange("p (m k) -> p m k", m=4),
                     ACT.Copy).then_inc(s_scev, 1)

        def u_hi(m, par, first=False):
            act.wait_ge(s_ut, m + 1)
            if not first:
                act.wait_ge(s_up, 2 * m - 2)
            act_(uth[:, par], PS[:, 0:2, :].rearrange("p b (k i) -> p (b k) i", i=P), ACT.Copy).then_inc(s_uth, 1)

        def u_lo(m, par):
            act.wait_ge(s_us, m + 1)
            act_(utl[:, par], PS[:, 0:2, :].rearrange("p b (k i) -> p (b k) i", i=P), ACT.Copy).then_inc(s_utl, 1)

        def gelu(m, par, b):
            act.wait_ge(s_up, 2 * m + b + 1)
            act_(gel[:, par, b * HT:(b + 1) * HT], PS[:, 2 + b, 0:HT], ACT.Gelu_apprx_tanh).then_inc(s_gel, 1)

        def u_half(m, par, half, b, first=False):
            if b == 0:
                u_hi(m + 1, 1 - par, first)
                if not isinstance(m, int) or m >= 2:
                    act.wait_ge(s_ao[par], 16 * half)
                gelu(m, par, 0)
            else:
                u_lo(m + 1, 1 - par)
                gelu(m, par, 1)
                act.wait_ge(s_gel, 2 * m + 2)
                act.dma_start(act_dram[:, bass.ds(m, 1), :].rearrange("p a t -> p (a t)"), gel[:, par]
                              ).then_inc(s_ao[par], 16)

        def gates_out(n, g):
            q = g // 4
            if g % 4 == 0 and (q >= 2 or not isinstance(n, int) or n >= 1):
                act.wait_ge(s_gout[q % 2], 32 * n + 16 * (q // 2))
            for r in range(OG // 4):
                t0 = OG * (g % 4) + 4 * r
                act.wait_ge(s_gmm, 2 * (NG * n + g) + r + 1)
                act_(gst[:, q % 2, :, t0:t0 + 4, :],
                     PS[:, 4 + r, :].rearrange("p (t b j) -> p b t j", t=4, j=JB), ACT.Copy).then_inc(s_gev, 1)

        def sel_out(n, w):
            act.wait_ge(s_selT, n + 1)
            if not isinstance(n, int) or n >= 1:
                act.wait_ge(s_oh, 16 * n)
            act_(selT[:, :, 0:w], PS[:, 6, 0:3 * P].rearrange("p (c t) -> p c t", c=3)[:, :, 0:w],
                 ACT.Copy).then_inc(s_selTe, 1)

        def softmax_exp(n, w):
            act.wait_ge(s_exd, n + 1)
            act_(ex[0:w], tops[0:w], ACT.Exp).then_inc(s_exa, 1)

        def choice(n, w_next, first=False):
            for k in range(UPN - UPG):
                if k == UPN - UPG - 1:
                    sel_out(n, P)
                for b in range(2):
                    u_half(UPN * n + k, k % 2, UPN // 2 * n + k // 2, b, first and k == 0)
                if k == 5:
                    softmax_exp(n, P)
            for g in range(NG):
                gates_out(n, g)
                if g == NG - 5:
                    scores_out(n + 1, w_next)
                if g % 2:
                    k = UPN - UPG + g // 4
                    u_half(UPN * n + k, k % 2, UPN // 2 * n + k // 2, g // 2 % 2)

        scores_out(0, P)
        act.sem_inc(s_gev, CREDIT)
        u_hi(0, 0, True)
        u_lo(0, 0)
        choice(0, P, True)
        with act.Fori(1, 3) as n:
            choice(n, P)
        choice(3, TS)
        for m in range(4 * UPN, NU):
            if m == 5 * UPN - UPG - 1:
                sel_out(4, TS)
            for b in range(2):
                if m == 5 * UPN - UPG:
                    gates_out(4, 2 * b)
                    gates_out(4, 2 * b + 1)
                u_half(m, m % 2, m // 2, b)
            if m == 4 * UPN + 5:
                softmax_exp(4, TS)

        def w_hi(t, r, par):
            act.wait_ge(s_wv, t + 1)
            if not isinstance(t, int) or t >= 4:
                act.wait_ge(s_om, 8 * t - 8 * r - 16)
            act_(wh[:, par, r, :], wv[:, r, :], ACT.Copy).then_inc(s_wh, 1)

        def iteration(i, last):
            for q in range(4):
                pr_, par = 4 * i + q, q % 2
                w_hi(2 * pr_, 0, par)
                if isinstance(pr_, int) and pr_ < 2:
                    act.wait_ge(s_ao[par], 16 * NU // 2)
                else:
                    act.wait_ge(s_wv, 2 * pr_ - 2)
                gelu(NU + pr_, par, 0)
                gelu(NU + pr_, par, 1)
                if not (last and q == 3):
                    u_hi(NU + pr_ + 1, 1 - par)
                w_hi(2 * pr_ + 1, 1, par)

        iteration(0, False)
        with act.Fori(1, 15) as i:
            iteration(i, False)
        iteration(15, True)

        squares(norms[2], [(s_h2, 2 * (k + 1)) for k in range(KD)])
        for n, (t0, w) in enumerate(TILES):
            act.wait_ge(s_yt, n + 1)
            if n >= 2:
                act.wait_ge(s_yo[n % 2], 16 * (n // 2))
            b = 2 + 2 * (n % 2)
            act_(ys[0:w, n % 2, :].rearrange("p (b x) -> p b x", b=2), PS[0:w, b:b + 2, :], ACT.Copy).then_inc(s_ye, 1)

    @block.gpsimd
    def _(pool):
        def pass_wait():
            pool.sem_inc(s_pool, 1)

        def gemm_hi(st):
            def group(g, slot, i):
                for cc in range(4):
                    c = 4 * g + cc
                    if cc == 0:
                        pool.wait_ge(s_w[slot], 16 * (st.before[slot] + 1) + 16 * i)
                    pool.wait_ge(st.mm, c + 1)
                    pass_wait()
                    nc.gpsimd.tensor_copy(whi[:, cc % 2], wraw[:, slot, :, cc * P:(cc + 1) * P]).then_inc(st.hi, 1)

            with pool.Fori(0, st.groups // 2) as i:
                for slot in range(2):
                    group(2 * i + slot, slot, i)
            if st.groups % 2:
                group(st.groups - 1, 0, st.groups // 2)

        gemm_hi(gemms[0])
        pool.wait_ge(gemms[0].ev, CREDIT + NIN)
        pool.wait_ge(gemms[0].mm, CREDIT + NIN)
        nc.gpsimd.tensor_copy(sw[64:128], projT[0:64, 0:8, :]).then_inc(s_swap, 1)
        gemm_hi(gemms[1])
        gemm_hi(gemms[2])

        def v_hi(pr_, par, rnd):
            pool.wait_ge(s_v[par], 16 * rnd + 16)
            for r in range(2):
                if not isinstance(pr_, int) or pr_ >= 2:
                    pool.wait_ge(s_om, 16 * pr_ - 16)
                pass_wait()
                nc.gpsimd.tensor_copy(vh[:, par, r, :], vrw[:, par, r, :]).then_inc(s_vh, 1)

        pool.wait_ge(s_gev, CREDIT + 8 * 17)
        pool.wait_ge(s_gout[0], 16 * 9)
        pool.wait_ge(s_gout[1], 16 * 8)
        v_hi(0, 0, 0)
        v_hi(1, 1, 0)
        with pool.Fori(1, 32) as i:
            for par in range(2):
                v_hi(2 * i + par, par, i)

    @block.vector
    def _(dve):
        tt, ts, stt = nc.vector.tensor_tensor, nc.vector.tensor_scalar, nc.vector.scalar_tensor_tensor
        chain = [0]

        def link(*ins):
            for x in ins:
                chain[0] += 1
                x.then_inc(s_dch, 1)
            dve.wait_ge(s_dch, chain[0])

        def gemm_lo(st):
            def group(g, slot):
                for cc in range(4):
                    dve.wait_ge(st.hi, 4 * g + cc + 1)
                    tt(wlo[:, cc % 2], wraw[:, slot, :, cc * P:(cc + 1) * P], f(whi[:, cc % 2]),
                       ALU.subtract).then_inc(st.lo, 1)

            with dve.Fori(0, st.groups // 2) as i:
                for slot in range(2):
                    group(2 * i + slot, slot)
            if st.groups % 2:
                group(st.groups - 1, 0)

        def norm(st, modulated):
            dve.wait_ge(st.sd, 1)
            link(nc.vector.reciprocal(rs[:], rs[:]))
            for k in range(KD):
                tt(scr2[:, k, :], hT[:, k, :], rs[:], ALU.mult).then_inc(st.tmp, 1)
            if modulated:
                for k in range(KD):
                    dve.wait_ge(st.hi, k + 1)
                    tt(XL[:, k, :], scr1[:, k, :], f(XH[:, k, :]), ALU.subtract).then_inc(st.lo, 1)

        nc.vector.memset(ones[:], 1.0)
        nc.vector.memset(negones[:], -1.0)
        nc.vector.memset(meanw[:], 1.0 / P)
        dve.wait_ge(s_cst, 16)
        ts(negI[:], ident, -1.0, None, ALU.mult)
        nc.vector.memset(epsc[:], EPS).then_inc(s_dch, 1)
        chain[0] += 1
        dve.wait_ge(s_dch, chain[0])
        dve.sem_inc(s_init, 1)
        dve.wait_ge(s_rowsT_ps, 1)
        nc.vector.tensor_copy(rowsT[:, 0:R_N], PS[:, 6, 0:R_N]).then_inc(s_rowsT, 1)
        for n, (t0, w) in enumerate(TILES):
            dve.wait_ge(s_xT, n + 1)
            b = 2 + 2 * (n % 2)
            nc.vector.tensor_copy(hT[:, :, t0:t0 + w],
                                  PS[:, b:b + 2, :].rearrange("p b (k t) -> p (b k) t", t=P)[:, :, 0:w]).then_inc(s_hT, 1)
        dve.sem_inc(s_ada_row, CREDIT)
        with dve.Fori(0, 6) as i:
            for slot in range(2):
                g = 2 * i + slot
                dve.wait_ge(s_ada_mm, g + 1)
                nc.vector.tensor_copy(adaR[0:2, bass.ds(g, 1), :].rearrange("p a x -> p (a x)"),
                                      PS[0:2, slot, :]).then_inc(s_ada_row, 1)
        dve.wait_ge(s_mod_ps, 1)
        dve.wait_ge(s_rowsT, 1)
        link(tt(modT[:], PS[:, 6, 0:96].rearrange("p (n g) -> p n g", g=2), bc(rowsT[:, R_B:R_N], 2, 2), ALU.add))
        for n in range(2):
            g0 = (R_N1, R_N2)[n]
            ins = stt(coefA[:, n], modT[:, 24 * n + 8:24 * n + 16, :], 1.0, bc(rowsT[:, g0:g0 + 8], 2, 2), ALU.add,
                      ALU.mult)
            link(ins)
        dve.sem_inc(s_coef, 1)
        nc.vector.memset(rvt[:, 4, :], 0.0).then_inc(s_zero, 1)
        nc.vector.memset(svt[:, 4, :], 0.0).then_inc(s_zero, 1)
        norm(norms[0], True)
        gemm_lo(gemms[0])

        dve.wait_ge(s_mixc, 16)
        dve.wait_ge(gemms[0].ev, CREDIT + NIN)
        dve.wait_ge(gemms[0].mm, CREDIT + NIN)
        cosv = bc(mixc[:, M_COS:M_COS + T], 1, 8)
        sinv = bc(mixc[:, M_SIN:M_SIN + T], 1, 8)
        tt(t1[:], projT[:, 0:8, :], cosv, ALU.mult).then_inc(s_rope, 1)
        dve.wait_ge(s_swap, 2)
        tt(sw[:], sw[:], sinv, ALU.mult).then_inc(s_rope, 1)
        dve.wait_ge(s_rope, 2)
        tt(projT[:, 0:8, :], t1[:], sw[:], ALU.add).then_inc(s_rope, 1)
        ts(projT[:, SQ:SQ + NH, :], projT[:, SQ:SQ + NH, :], SCALE, None, ALU.mult).then_inc(s_sqs, 1)
        dve.wait_ge(s_rope, 3)
        tt(qds[:], projT[:, RQ:RQ + NH, TP:T], mixc[:, M_QDEC:M_QDEC + NH * TS].rearrange("p (h t) -> p h t", h=NH),
           ALU.mult).then_inc(s_qds, 1)
        nc.vector.memset(prs[:], 0.0).then_inc(s_qds, 1)
        for b, (t0, w) in enumerate(TILES):
            dve.wait_ge(s_tp, 15 + b + 1)
            tt(rkd[0:w, b, :].rearrange("p (h d) -> p h d", h=NH),
               PS[0:w, (15 + b) % 4, :].rearrange("p (h d) -> p h d", h=NH), bc(kdec(b)[0:w], 2, P),
               ALU.mult).then_inc(s_rkd, 1)
        dve.wait_ge(s_qds, 2)
        gam = [float(np.exp(TS * np.log1p(-np.exp2(-5.0 - h)))) for h in range(NH)]
        for h in range(NH):
            if h >= 2:
                dve.wait_ge(s_ro, h - 1)
            for kb in range(QB):
                w = TP - P * kb
                dve.wait_ge(s_rs_mm, QB * h + kb + 1)
                stt(pr[:, h % 2, pcol(kb):pcol(kb) + w], PS[:, kb, 0:w], SCALE,
                    mixc[:, M_DT + h * TP:M_DT + h * TP + w], ALU.mult, ALU.mult).then_inc(s_rp, 1)
            dve.wait_ge(s_raux, h + 1)
            dve.wait_ge(s_rev, 3 * h + 1)
            stt(prs[0:TS, h, :], PS[0:TS, 6 + h % 2, P:P + TS], SCALE, mixc[0:TS, M_DT + h * TP:M_DT + h * TP + TS],
                ALU.mult, ALU.mult).then_inc(s_rps, 1)
            dve.wait_ge(s_stS, 16)
            stt(stN[:, h, :], stS[:, h, :], gam[h], PS[:, 6 + h % 2, 256:384], ALU.mult, ALU.add).then_inc(s_rsn, 1)
        for h in range(NH):
            par = h % 2
            dve.wait_ge(s_bln, h + 1)
            for kb in range(QB):
                w = TP - P * kb
                v = lk[:, par, pcol(kb):pcol(kb) + w]
                ins = stt(v, PS[:, kb, 0:w], 0.0, v, ALU.max, ALU.add)
                ins.then_inc(s_dch, 1)
                chain[0] += 1
            dve.wait_ge(s_dch, chain[0])
            for kb in range(QB):
                v = lk[:, par, pcol(kb):pcol(kb) + P]
                tt(v, v, mask, ALU.mult).then_inc(s_blk, 1)
            if h >= 1:
                dve.wait_ge(s_bo, h)
            for kb in reversed(range(QB)):
                dve.wait_ge(s_bc, QB * h + QB - kb)
                tt(aw[:, 0, pcol(kb):pcol(kb) + P], PS[:, kb, 0:P], mmin, ALU.min).then_inc(s_bmin, 1)
        dve.wait_ge(s_bo, NH)
        nc.vector.memset(lks[:, NPB, :], 0.0).then_inc(s_zero, 1)
        nc.vector.memset(aws[:, NPB, :], 0.0).then_inc(s_zero, 1)
        dve.wait_ge(s_cln, 2)
        v8, z8 = lks[0:TS, NPB, :], PS[0:TS, 2, 0:P]
        link(stt(lks[:, 0:NPB, :], PS[:, 0:2, :].rearrange("p b (c x) -> p (b c) x", x=P), 0.0, lks[:, 0:NPB, :],
                 ALU.max, ALU.add),
             stt(v8, z8, 0.0, v8, ALU.max, ALU.add))
        v8h = v8.rearrange("p (h t) -> p h t", h=NH)
        link(tt(v8h, v8h, bc(mask[0:TS, 0:TS], 1, NH), ALU.mult),
             nc.vector.tensor_copy(rsum[:, NPB - 2, :], lks[:, NPB - 1, :]))
        for b in reversed(range(NPB - 2)):
            link(tt(rsum[:, b, :], rsum[:, b + 1, :], lks[:, b + 1, :], ALU.add))
        dve.sem_inc(s_clk, 1)
        dve.wait_ge(s_cc, 1)
        tt(aws[0:TS, NPB, :].rearrange("p (h t) -> p h t", h=NH), z8.rearrange("p (h t) -> p h t", h=NH),
           bc(mmin[0:TS, 0:TS], 1, NH), ALU.min).then_inc(s_cmin, 1)
        dve.wait_ge(s_ghi, 1)
        dve.wait_ge(s_out, 96)
        tt(XL[:, 4:8, :], projT[:, SQ:SQ + NH, :], f(XH[:, 4:8, :]), ALU.subtract).then_inc(s_glo, 1)
        for h in range(NH):
            dve.wait_ge(s_gm, h + 1)
            tt(halves(projT[:, h, :]), halves(projT[:, h, :]), pair(2 * h), ALU.subtract).then_inc(s_gcen, 1)
        for h in range(NH):
            dve.wait_ge(s_gsd, h + 1)
            link(nc.vector.reciprocal(rsb[:, h, :], rsb[:, h, :]))
            link(tt(projT[:, h, :], projT[:, h, :], rsb[:, h, :], ALU.mult))
            dve.wait_ge(s_gate, 1)
            stt(projT[:, h, :], projT[:, h, :], rowsT[:, R_RG + h:R_RG + h + 1], projT[:, RG + h, :], ALU.mult,
                ALU.mult).then_inc(s_gy, 1)
        dve.wait_ge(s_ghi, 2)
        tt(XL[:, 0:4, :], projT[:, 0:4, :], f(XH[:, 0:4, :]), ALU.subtract).then_inc(s_glo, 1)
        gemm_lo(gemms[1])

        def residual(src, gate0, done, last):
            for k in range(KD):
                for g, cols in enumerate((slice(0, TP), slice(TP, T))):
                    stt(hT[:, k, cols], src[:, k, cols], modT[:, gate0 + k, g:g + 1], hT[:, k, cols], ALU.mult,
                        ALU.add).then_inc(done, 1)

        dve.wait_ge(gemms[1].ev, CREDIT + 8)
        residual(yT, 16, s_h1, None)
        norm(norms[1], True)
        gemm_lo(gemms[2])

        dve.wait_ge(gemms[2].ev, CREDIT + 16)
        nc.vector.tensor_copy(iotaE[:], bc(iota, 2, OG)).then_inc(s_dch, 1)
        chain[0] += 1
        dve.wait_ge(s_dch, chain[0])

        def choose(n, w, per):
            count = [0]

            def step(*ins):
                for x in ins:
                    count[0] += 1
                    x.then_inc(s_cch, 1)
                dve.wait_ge(s_cch, per * n + count[0])
                if not isinstance(n, int):
                    dve.sem_inc(s_vpass, 1)

            dve.wait_ge(s_scev, 4 * n + 4)
            if not isinstance(n, int):
                dve.sem_inc(s_vpass, 1)
            r = slice(0, w)
            lo8, hi8 = slice(0, 8), slice(8, 16)
            step(*[nc.vector.max(val[r, hp, lo8], S[r, hp, :]) for hp in range(16)])
            step(*[nc.vector.match_replace(S2[r, hp, :], val[r, hp, lo8], S[r, hp, :], -3.0e38) for hp in range(16)])
            step(*[nc.vector.max(val[r, hp, hi8], S2[r, hp, :]) for hp in range(16)])
            step(*[nc.vector.max_index(ind[r, hp, lo8], val[r, hp, lo8], S[r, hp, :]) for hp in range(16)],
                 *[nc.vector.max_index(ind[r, hp, hi8], val[r, hp, hi8], S2[r, hp, :]) for hp in range(16)])
            va = val[r].rearrange("p (h a) k -> p h a k", a=2)
            cv = cand[r].rearrange("p h (a b) -> p h a b", a=TOPK)
            step(nc.vector.tensor_copy(indf[r], ind[r]),
                 *[tt(cv[:, h], bc(va[:, h, 0, :], 2, TOPK), bc(va[:, h, 1, :], 1, TOPK), ALU.add) for h in range(PH)])
            step(*[nc.vector.max(tops[r, h, lo8], cand[r, h, :]) for h in range(PH)])
            step(*[nc.vector.match_replace(cand2[r, h, :], tops[r, h, lo8], cand[r, h, :], -3.0e38) for h in range(PH)])
            step(*[nc.vector.max(tops[r, h, hi8], cand2[r, h, :]) for h in range(PH)])
            step(*[nc.vector.max_index(pos[r, h, lo8], tops[r, h, lo8], cand[r, h, :]) for h in range(PH)],
                 *[nc.vector.max_index(pos[r, h, hi8], tops[r, h, hi8], cand2[r, h, :]) for h in range(PH)])
            step(nc.vector.tensor_copy(sm[r, 0, :], tops[r, :, 0]),
                 ts(posa[r], pos[r], 4, None, ALU.logical_shift_right))
            step(tt(tops[r], tops[r], bc(sm[r, 0, :], 2, TOPK), ALU.subtract),
                 nc.vector.tensor_copy(posf[r, 0], posa[r]))
            dve.sem_inc(s_exd, 1)
            step(ts(posa[r], pos[r], 15, None, ALU.bitwise_and))
            step(nc.vector.tensor_copy(posf[r, 1], posa[r]))
            for side in range(2):
                step(tt(eq[r], bc(posf[r, side].rearrange("p h k -> p (h k)"), 2, TOPK),
                        bc(iota[r, 0:TOPK], 1, PH * TOPK), ALU.is_equal))
                ev = eq[r].rearrange("p (h k) a -> p h k a", h=PH)
                iv = indf[r].rearrange("p (h a) k -> p h a k", a=2)
                step(*[tt(ev[:, h], ev[:, h], bc(iv[:, h, side, :], 1, TOPK), ALU.mult) for h in range(PH)])
                step(nc.vector.tensor_reduce(sel[r, side, :], eq[r], AX_X, ALU.add))
            dve.wait_ge(s_exa, n + 1)
            step(nc.vector.tensor_reduce(sm[r, 1, :], ex[r], AX_X, ALU.add))
            step(nc.vector.reciprocal(sm[r, 0, :], sm[r, 1, :]))
            step(tt(sel[r, 2, :].rearrange("p (h k) -> p h k", h=PH), ex[r], bc(sm[r, 0, :], 2, TOPK), ALU.mult))
            dve.sem_inc(s_sel, 1)
            dve.wait_ge(s_selTe, n + 1)
            step(nc.vector.tensor_copy(keyb[:, :, 0:w], selT[:, 0:2, 0:w]),
                 nc.vector.tensor_copy(gb[:, 0, 0:w], selT[:, 2, 0:w]))
            step(tt(gres[:, 0, 0:w], selT[:, 2, 0:w], gb[:, 0, 0:w], ALU.subtract))
            step(nc.vector.tensor_copy(gb[:, 1, 0:w], gres[:, 0, 0:w]))
            step(tt(gres[:, 1, 0:w], gres[:, 0, 0:w], gb[:, 1, 0:w], ALU.subtract))
            step(nc.vector.tensor_copy(gb[:, 2, 0:w], gres[:, 1, 0:w]))
            for g in range(w // OG):
                gi = NG * n + g
                sl, cols = g % 2, slice(OG * g, OG * (g + 1))
                if g >= 2 or not isinstance(n, int) or n >= 1:
                    dve.wait_ge(s_gmm, 2 * gi - 2)
                tt(ohA[:, sl], iotaE[:], bc(keyb[:, 1, cols], 1, P), ALU.is_equal)
                step(tt(eqb[:], iotaE[:], bc(keyb[:, 0, cols], 1, P), ALU.is_equal))
                for part in range(3):
                    last = tt(ohB[:, part, sl], eqb[:], bc(gb[:, part, cols], 1, P), ALU.mult)
                last.then_inc(s_oh, 1)
                dve.wait_ge(s_oh, gi + 1)
            return count[0]

        per = choose(0, P, 0)
        with dve.Fori(1, 4) as n:
            again = choose(n, P, per)
        assert again == per
        choose(4, TS, per)

        dve.wait_ge(s_gev, CREDIT + 8 * 17)
        dve.wait_ge(s_gout[0], 16 * 9)
        dve.wait_ge(s_gout[1], 16 * 8)
        link(nc.vector.memset(acc[:], 0.0))
        dve.sem_inc(s_add, 4)

        def u_lo(m, par):
            dve.wait_ge(s_uth, m + 1)
            tt(utl[:, par], PS[:, 0:2, :].rearrange("p b (k i) -> p (b k) i", i=P), f(uth[:, par]),
               ALU.subtract).then_inc(s_utl, 1)

        def v_lo(t, r, par):
            dve.wait_ge(s_vh, t + 1)
            tt(vl[:, par, r, :], vrw[:, par, r, :], f(vh[:, par, r, :]), ALU.subtract).then_inc(s_vl, 1)

        def gate(t, r, par, src, blk, j):
            if not isinstance(t, int) or t >= 2:
                dve.wait_ge(s_wh, t - 1)
                dve.wait_ge(s_wl, t - 1)
            tt(wv[:, r, :], src, G[:, blk, :, j], ALU.mult).then_inc(s_wv, 1)

        def w_lo(t, r, par):
            dve.wait_ge(s_wh, t + 1)
            tt(wl[:, par, r, :], wv[:, r, :], f(wh[:, par, r, :]), ALU.subtract).then_inc(s_wl, 1)

        def add(pr_, n):
            dve.wait_ge(s_om, 16 * pr_ + n + 1)
            if not isinstance(pr_, int) or pr_ >= 1:
                dve.wait_ge(s_add, 16 * pr_ + n - 12 + 4)
            a = acc[:, n // 2, (n % 2) * HT:(n % 2 + 1) * HT]
            tt(a, a, PS[:, 4 + n % 4, 0:HT], ALU.add).then_inc(s_add, 1)

        def iteration(i, first, last):
            for q in range(4):
                pr_, par, blk, j = 4 * i + q, q % 2, q // 2, 2 * (q % 2)
                adds = not (first and q == 0)
                if j == 0:
                    dve.wait_ge(s_g[blk], 16 * i + 16)
                dve.wait_ge(s_al[par], 32 * i + 16 * (q // 2) + 16)
                gate(2 * pr_, 0, par, al[:, par, :], blk, j)
                v_lo(2 * pr_, 0, par)
                w_lo(2 * pr_, 0, par)
                dve.wait_ge(s_gel, 2 * (NU + pr_) + 2)
                gate(2 * pr_ + 1, 1, par, gel[:, par, :], blk, j + 1)
                if adds:
                    add(pr_ - 1, 0)
                if not (last and q == 3):
                    u_lo(NU + pr_ + 1, 1 - par)
                for n in range(1, 5) if adds else ():
                    add(pr_ - 1, n)
                w_lo(2 * pr_ + 1, 1, par)
                for n in range(5, 8) if adds else ():
                    add(pr_ - 1, n)
                v_lo(2 * pr_ + 1, 1, par)
                for n in range(8, 16) if adds else ():
                    add(pr_ - 1, n)

        iteration(0, True, False)
        with dve.Fori(1, 15) as i:
            iteration(i, False, False)
        iteration(15, False, True)
        for n in range(16):
            add(63, n)
        dve.wait_ge(s_add, 4 + 16 * 64)
        residual(acc, 40, s_h2, None)
        norm(norms[2], False)
        dve.wait_ge(norms[2].tmp, KD)
        for k in range(KD):
            ins = ts(scr2[:, k, :], scr2[:, k, :], rowsT[:, R_FG + k:R_FG + k + 1], None, ALU.mult)
        ins.then_inc(norms[2].y, 1)

    ctx.close()


def pcol(kb):
    return sum(TP - P * n for n in range(kb))


_INS = ['x_prompt', 'x_sample', 'c_prompt', 'c_sample', 'state_ret', 'cache_sb_k', 'cache_sb_v', 'w_ada', 'b_ada',
        'norm1_g', 'w_in', 'ret_norm_g', 'w_out', 'norm2_g', 'peer_w_query', 'peer_sub_keys', 'peer_u', 'peer_v',
        'final_norm_g']
_OUTS = [(1, TP, D), (1, TS, D), (1, 1, NH, P, P), (1, 1, TP, NH, P), (1, 1, TP, NH, P), (1, 1, NH, P, P),
         (1, 1, TS, NH, P), (1, 1, TS, NH, P)]


def kernel(**inputs):
    import concourse.bacc as _bacc
    from concourse.bass_utils import run_bass_kernel_spmd as _run

    nc = _bacc.Bacc("TRN2", target_bir_lowering=False, num_devices=1)
    small, mix = shape_constants()
    arrays, args = {}, []
    for name, a in [(n, np.ascontiguousarray(inputs[n])) for n in _INS] + [("small", small), ("mix", mix)]:
        arrays[f"in_{name}_dram"] = a
        args.append(nc.dram_tensor(f"in_{name}_dram", a.shape, mybir.dt.from_np(a.dtype), kind="ExternalInput").ap())
    args.append(nc.dram_tensor("gates_dram", (P, NJB, T, JB), F32, kind="Internal").ap())
    args.append(nc.dram_tensor("acts_dram", (P, NU, T), F32, kind="Internal").ap())
    for i, shape in enumerate(_OUTS):
        args.append(nc.dram_tensor(f"out_{i}_dram", shape, F32, kind="ExternalOutput").ap())
    build(nc, *args)
    r = _run(nc, [arrays], core_ids=[0])
    return tuple(r.results[0][f"out_{i}_dram"] for i in range(len(_OUTS)))
```

```python
from contextlib import ExitStack

import numpy as np

import concourse.bass as bass
from concourse import mybir

F32 = mybir.dt.float32
F32R = mybir.dt.float32r
BF16 = mybir.dt.bfloat16
U32 = mybir.dt.uint32
ALU = mybir.AluOpType
ACT = mybir.ActivationFunctionType
AX_X = mybir.AxisListType.X

P = 128
D = 1024
KD = D // P
TP, TS = 512, 32
T = TP + TS
HT = T // 2
TILES = [(0, 128), (128, 128), (256, 128), (384, 128), (512, 32)]
NH = 4
PAST = 1024
NPB = PAST // P
QB = TP // P
EPS = 1e-6
NIN = 28
RQ, RK, RV, RG, SQ, SK, SV = (4 * n for n in range(7))
PH = 8
NK = 128
TOPK = 16
JB = 4
NJB = NK // JB
TB = 32
SCALE = P ** -0.5
NEG = -1.0e30
OG = 8
NU = NK // 2
UPN = 12
UPG = 4
NG = P // OG
CREDIT = 2

C_ID, C_TRI, C_MASK, C_MIN, C_IOTA, C_KDEC = 0, 128, 256, 384, 512, 640
C_N = C_KDEC + NH * 5
M_DT, M_COS, M_SIN, M_QDEC = 0, NH * TP, NH * TP + T, NH * TP + 2 * T
M_N = M_QDEC + NH * TS
R_C, R_N1, R_N2, R_FG, R_RG, R_B, R_N = 0, 16, 24, 32, 40, 44, 92


def shape_constants():
    i = np.arange(P)
    small = np.zeros((P, C_N), np.float32)
    small[:, C_ID:C_ID + P] = np.eye(P)
    small[:, C_TRI:C_TRI + P] = -(i[:, None] >= i[None, :]).astype(np.float32)
    small[:, C_MASK:C_MASK + P] = (i[:, None] < i[None, :])
    small[:, C_MIN:C_MIN + P] = np.where(i[:, None] < i[None, :], 0.0, NEG)
    small[:, C_IOTA:C_IOTA + P] = i[None, :]
    log_g = np.log1p(-np.exp2(-5.0 - np.arange(NH)))
    for b, (t0, n) in enumerate(TILES):
        last = TP - 1 - t0 if t0 < TP else TS - 1
        for h in range(NH):
            left = last - i
            small[:, C_KDEC + b * NH + h] = np.where(left >= 0, np.exp(np.maximum(left, 0) * log_g[h]), 0.0)
    mix = np.zeros((P, M_N), np.float32)
    x = np.arange(TP)
    for h in range(NH):
        gap = x[None, :] - i[:, None]
        mix[:, M_DT + h * TP:M_DT + (h + 1) * TP] = np.where(gap >= 0, np.exp(np.maximum(gap, 0) * log_g[h]), 0.0)
        mix[:, M_QDEC + h * TS:M_QDEC + (h + 1) * TS] = SCALE * np.exp((np.arange(TS) + 1.0) * log_g[h])[None, :]
    half = P // 2
    inv = np.power(np.float32(10000.0), -np.arange(half, dtype=np.float32) / np.float32(half)).astype(np.float32)
    pos = np.concatenate([np.arange(TP), PAST + np.arange(TS)]).astype(np.float32)
    ang = (inv[:, None] * pos[None, :]).astype(np.float32)
    mix[:half, M_COS:M_COS + T] = mix[half:, M_COS:M_COS + T] = np.cos(ang)
    mix[:half, M_SIN:M_SIN + T] = -np.sin(ang)
    mix[half:, M_SIN:M_SIN + T] = np.sin(ang)
    return small, mix


def build(nc, x_prompt, x_sample, c_prompt, c_sample, state_ret, cache_sb_k, cache_sb_v, w_ada, b_ada, norm1_g, w_in,
          ret_norm_g, w_out, norm2_g, peer_w_query, peer_sub_keys, peer_u, peer_v, final_norm_g, small_c, mix_c,
          gate_dram, act_dram, y_prompt, y_sample, st_prompt, k_prompt, v_prompt, st_sample, k_sample, v_sample):
    ctx = ExitStack()
    BASE = nc.sbuf_base + (-nc.sbuf_base) % 32

    place = {}

    def at(name, off, shape, dt=F32):
        place[name] = off
        return nc.alloc_sbuf_tensor_at(name, [P] + list(shape), dt, offset=BASE + off)

    cst = at("cst", 0, [C_N])
    o = 4 * C_N + 16
    ones = at("ones", o, [P])
    negones = at("negones", o + 512, [P])
    meanw = at("meanw", o + 1024, [P])
    o += 1536
    rowsT = at("rowsT", o, [R_N + 4])
    modT = at("modT", o + 384, [48, 2])
    coefA = at("coefA", o + 768, [2, KD, 2])
    siluT = at("siluT", o + 896, [KD, 2])
    epsc = at("epsc", o + 960, [8])
    assert o + 992 <= 6144
    hT = at("hT", 6144, [KD, T])
    XH = at("XH", 6144 + 17408, [KD, T], F32R)
    XL = at("XL", 6144 + 34816, [KD, T], F32R)
    R0 = 6144 + 52224

    wraw = at("wraw", R0, [2, KD, 512])
    whi = at("whi", R0 + 32768, [2, KD, P], F32R)
    wlo = at("wlo", R0 + 40960, [2, KD, P], F32R)
    RP = R0 + 49152
    wxh = at("wxh", R0 + 49152 + NIN * 4 * T + 13056 + 20992, [KD, P], F32R)
    wxl = at("wxl", R0 + 49152 + NIN * 4 * T + 13056 + 25088, [KD, P], F32R)
    projT = at("projT", RP, [NIN, T])
    scr1 = at("scr1", RP, [KD, T])
    scr2 = at("scr2", RP + 8 * 4 * T, [KD, T])
    sqb = at("sqb", RP + 4 * 4 * T, [NH, T])
    rsb = at("rsb", RP + 8 * 4 * T, [NH, T])
    rs = at("rs", RP + 27 * 4 * T, [T])
    RF = RP + NIN * 4 * T
    mixc = at("mixc", RF, [M_N])
    RT = RF + 13056
    rvt = at("rvt", RT, [5, 512])
    svt = at("svt", RT + 10240, [5, 512])
    rkd = at("rkd", RT + 20480, [5, 512])
    xin = at("xin", RT, [5, D])
    adaw = at("adaw", RT, [KD, 512])
    adar = at("adar", RT + 16384, [2, 512])
    rows = at("rows", RT + 20480, [P])
    A0 = 6144 + 17408
    sw = at("sw", A0, [8, T])
    t1 = at("t1", A0 + 17408, [8, T])
    skt = at("skt", A0, [5, 512])
    lk = at("lk", A0 + 10240, [2, 1280])
    aw = at("aw", A0 + 20480, [1, 1280])
    pr = at("pr", A0 + 10240, [2, 1280])
    prs = at("prs", A0 + 25600, [NH, TS])
    qds = at("qds", A0 + 26112, [NH, TS])
    stO = at("stO", A0 + 26624, [NH, P])
    stS = at("stS", A0 + 28672, [NH, P])
    stN = at("stN", A0 + 30720, [NH, P])
    lks = at("lks", A0 + 10240, [NPB + 1, P])
    rsum = at("rsum", RF, [NPB - 1, P])
    aws = at("aws", RF + 3584, [NPB + 1, P])
    kraw = at("kraw", R0, [NPB, 512])
    vraw = at("vraw", R0 + 16384, [NPB, 512])
    kT = at("kT", R0 + 32768, [NH, PAST])

    class Region:

        def __init__(self, start, end):
            self.off, self.end = start, end

        def __call__(self, name, shape, dt=F32):
            t = at(name, self.off, shape, dt)
            self.off += int(np.prod(shape)) * (2 if dt == BF16 else 4)
            self.off += -self.off % 32
            assert self.off <= self.end, name
            return t

    negI = at("negI", 5632, [P], F32R)
    low = Region(R0, R0 + 49152)
    uraw = low("uraw", [2, D])
    uth = low("uth", [2, KD, P], F32R)
    utl = low("utl", [2, KD, P], F32R)
    gel = low("gel", [2, T])
    stored = Region(low.off, low.end)
    val = low("val", [16, TOPK])
    ind = low("ind", [16, TOPK], U32)
    indf = low("indf", [16, TOPK])
    tops = low("tops", [PH, TOPK])
    pos = low("pos", [PH, TOPK], U32)
    posa = low("posa", [PH, TOPK], U32)
    posf = low("posf", [2, PH, TOPK])
    ex = low("ex", [PH, TOPK])
    sm = low("sm", [2, PH])
    sel = low("sel", [3, P])
    selT = low("selT", [3, P])
    keyb = low("keyb", [2, P], BF16)
    gres = low("gres", [2, P])
    gb = low("gb", [3, P], BF16)
    eqb = low("eqb", [P, OG], BF16)
    iotaE = low("iotaE", [P, OG], BF16)
    ohA = low("ohA", [2, P, OG], BF16)
    qT = at("qT", RP, [16, T])
    high = Region(RP + 16 * 4 * T, R0 + 154432)
    skT = high("skT", [16, P])
    S = high("S", [16, P])
    S2 = high("S2", [16, P])
    gst = high("gst", [2, NJB, TB, JB])
    ohB = high("ohB", [3, 2, P, OG], BF16)
    cand = at("cand", place["S"], [PH, 256])
    cand2 = at("cand2", place["S2"], [PH, 256])
    eq = at("eq", place["S2"], [PH * TOPK, TOPK])
    skraw = at("skraw", place["gst"], [16, P])

    al = stored("al", [2, T])
    wv = stored("wv", [2, T])
    mid = Region(RP, RP + 16 * 4 * T)
    vrw = mid("vrw", [2, 2, D])
    G = mid("G", [2, T, JB])
    top = Region(RP + 16 * 4 * T, R0 + 154432)
    vh = top("vh", [2, 2, D], F32R)
    vl = top("vl", [2, 2, D], F32R)
    wh = top("wh", [2, 2, T], F32R)
    wl = top("wl", [2, 2, T], F32R)
    acc = top("acc", [KD, T])
    ys = at("ys", R0, [2, D])

    PS = ctx.enter_context(nc.psum_tensor("PS", [P, 8, 512], F32))

    def sem(name):
        return ctx.enter_context(nc.semaphore(name))

    ident = cst[:, C_ID:C_ID + P]
    ntri = cst[:, C_TRI:C_TRI + P]
    mask = cst[:, C_MASK:C_MASK + P]
    mmin = cst[:, C_MIN:C_MIN + P]
    iota = cst[:, C_IOTA:C_IOTA + P]

    def kdec(b):
        return cst[:, C_KDEC + b * NH:C_KDEC + (b + 1) * NH]

    def bc(ap, axis, n):
        v = ap.unsqueeze(axis)
        shape = list(v.shape)
        shape[axis] = n
        return v.to_broadcast(shape)

    def pair(b):
        return PS[:, b:b + 2, 0:HT]

    def halves(ap):
        return ap.rearrange("p (b t) -> p b t", b=2)

    def f(ap):
        return ap.bitcast(F32)

    def groups_of(ap):
        return (ap[..., 0:TP], ap[..., TP:T])

    s_cst, s_mixc, s_rows, s_x = sem("s_cst"), sem("s_mixc"), sem("s_rows"), sem("s_x")
    s_init = sem("s_init")
    s_w = [sem("s_w0"), sem("s_w1")]
    s_rowsT_ps, s_rowsT = sem("s_rowsT_ps"), sem("s_rowsT")
    s_silu = sem("s_silu")
    s_xT, s_hT = sem("s_xT"), sem("s_hT")
    s_sum = sem("s_sum")
    s_ada_mm, s_adaw, s_adar, s_adat = sem("s_ada_mm"), sem("s_adaw"), sem("s_adar"), sem("s_adat")
    s_dch = sem("s_dch")
    s_ach = sem("s_ach")

    class Stage:
        pass

    norms, gemms = [], []
    for n in range(3):
        st = Stage()
        st.sq, st.ss, st.sd, st.rs, st.tmp, st.y, st.hi, st.lo = (
            sem(f"s_n{n}_{x}") for x in ("sq", "ss", "sd", "rs", "tmp", "y", "hi", "lo"))
        norms.append(st)
    for name, groups, reads in (("in", 7, 1), ("out", 2, 3), ("qry", 4, 1)):
        st = Stage()
        st.reads = reads
        st.name, st.groups = name, groups
        st.hi, st.lo, st.mm, st.ev = (sem(f"s_{name}_{x}") for x in ("hi", "lo", "mm", "ev"))
        gemms.append(st)
    gemms[0].before = (2, 2)
    gemms[1].before = (6, 5)
    gemms[2].before = (7, 6)

    s_swap, s_rope, s_sqs = sem("s_swap"), sem("s_rope"), sem("s_sqs")
    s_tp, s_tm, s_rkd = sem("s_tp"), sem("s_tm"), sem("s_rkd")
    s_kc, s_vc, s_stS = sem("s_kc"), sem("s_vc"), sem("s_stS")
    s_rs_mm, s_rp, s_raux, s_rps, s_ro, s_ros, s_rev, s_rsn, s_qds = (
        sem(x) for x in ("s_rs_mm", "s_rp", "s_raux", "s_rps", "s_ro", "s_ros", "s_rev", "s_rsn", "s_qds"))
    s_bz, s_bln, s_blk, s_bc, s_bmin, s_ba, s_bo, s_bev = (
        sem(x) for x in ("s_bz", "s_bln", "s_blk", "s_bc", "s_bmin", "s_ba", "s_bo", "s_bev"))
    s_kt, s_kte, s_cz, s_cln, s_clk, s_cc, s_cmin, s_ca, s_co, s_cev = (
        sem(x) for x in ("s_kt", "s_kte", "s_cz", "s_cln", "s_clk", "s_cc", "s_cmin", "s_ca", "s_co", "s_cev"))
    s_gm, s_gcen, s_gsq, s_gv, s_gsd, s_gate, s_gy, s_ghi, s_glo = (
        sem(x) for x in ("s_gm", "s_gcen", "s_gsq", "s_gv", "s_gsd", "s_gate", "s_gy", "s_ghi", "s_glo"))
    s_zero = sem("s_zero")
    s_skl, s_skp, s_skT = sem("s_skl"), sem("s_skp"), sem("s_skT")
    s_sc, s_scev, s_cmpd, s_exd, s_exa, s_sel = (
        sem(x) for x in ("s_sc", "s_scev", "s_cmpd", "s_exd", "s_exa", "s_sel"))
    s_selT, s_selTe = sem("s_selT"), sem("s_selTe")
    s_oh, s_gmm, s_gev = sem("s_oh"), sem("s_gmm"), sem("s_gev")
    s_pool, s_vpass, s_cch, s_us = sem("s_pool"), sem("s_vpass"), sem("s_cch"), sem("s_us")
    s_ao = [sem("s_ao0"), sem("s_ao1")]
    s_al = [sem("s_al0"), sem("s_al1")]
    s_gout = [sem("s_gout0"), sem("s_gout1")]
    s_u = [sem("s_u0"), sem("s_u1")]
    s_v = [sem("s_v0"), sem("s_v1")]
    s_g = [sem("s_g0"), sem("s_g1")]
    s_ut, s_uth, s_utl, s_up, s_gel, s_wv, s_wh, s_wl, s_vh, s_vl, s_om, s_add, s_acc0 = (
        sem(x) for x in ("s_ut", "s_uth", "s_utl", "s_up", "s_gel", "s_wv", "s_wh", "s_wl", "s_vh", "s_vl", "s_om",
                         "s_add", "s_acc0"))
    s_h2 = sem("s_h2")
    s_yt, s_ye = sem("s_yt"), sem("s_ye")
    s_yo = [sem("s_yo0"), sem("s_yo1")]
    s_out = sem("s_out")

    def w_view(w, g):
        return w[0].rearrange("(k p) n -> p k n", p=P)[:, :, bass.ds(g * 512, 512)]

    u_d = peer_u[0].rearrange("(j p) d -> p j d", p=P)
    v_d = peer_v[0].rearrange("(j p) d -> p j d", p=P)

    block = ctx.enter_context(nc.Block())

    @block.sync
    def _(sp):
        n_out = [0]

        def store(dst, src):
            sp.dma_start(dst, src).then_inc(s_out, 16)
            n_out[0] += 1

        sp.dma_start(rows[R_C:R_C + 8, :], c_prompt[0].rearrange("(k p) -> k p", p=P)).then_inc(s_rows, 16)
        sp.dma_start(rows[R_C + 8:R_C + 16, :], c_sample[0].rearrange("(k p) -> k p", p=P)).then_inc(s_rows, 16)
        sp.dma_start(rows[R_N1:R_N1 + 8, :], norm1_g[0].rearrange("(k p) -> k p", p=P)).then_inc(s_rows, 16)
        sp.dma_start(rows[R_N2:R_N2 + 8, :], norm2_g[0].rearrange("(k p) -> k p", p=P)).then_inc(s_rows, 16)
        sp.dma_start(rows[R_FG:R_FG + 8, :], final_norm_g.rearrange("(k p) -> k p", p=P)).then_inc(s_rows, 16)
        sp.dma_start(rows[R_RG:R_RG + 4, :], ret_norm_g[0].rearrange("(k p) -> k p", p=P)).then_inc(s_rows, 16)
        sp.dma_start(rows[R_B:R_B + 48, :], b_ada[0].rearrange("(k p) -> k p", p=P)).then_inc(s_rows, 16)
        sp.dma_start(cst[:], small_c).then_inc(s_cst, 16)

        def ada_load(g, slot):
            sp.dma_start(wraw[:, slot], w_view(w_ada, g)).then_inc(s_w[slot], 16)

        sp.dma_start(xin[:, 0:4, :], x_prompt[0].rearrange("(b p) d -> p b d", p=P)).then_inc(s_x, 16)
        sp.dma_start(xin[0:TS, 4, :], x_sample[0]).then_inc(s_x, 16)
        ada_load(0, 0)
        ada_load(1, 1)
        for g in (2, 3):
            sp.wait_ge(s_ada_mm, g - 1)
            ada_load(g, g % 2)

        def adaw_load(g):
            if not isinstance(g, int) or g > 4:
                sp.wait_ge(s_ada_mm, g)
            sp.dma_start(adaw[:], w_view(w_ada, g)).then_inc(s_adaw, 16)

        def gemm_loads(st, w, first_waits):
            for slot in range(2):
                sp.wait_ge(*first_waits[slot])
                sp.dma_start(wraw[:, slot], w_view(w, slot)).then_inc(s_w[slot], 16)
            if st is gemms[0]:
                sp.dma_start(mixc[:], mix_c).then_inc(s_mixc, 16)
                adaw_load(5)
            if st.groups // 2 > 1:
                with sp.Fori(1, st.groups // 2) as i:
                    for slot in range(2):
                        g = 2 * i + slot
                        sp.wait_ge(st.lo, 4 * g - 4)
                        sp.dma_start(wraw[:, slot], w_view(w, g)).then_inc(s_w[slot], 16)
                        if st is gemms[0]:
                            adaw_load(g + 4)
            if st.groups % 2:
                g = st.groups - 1
                sp.wait_ge(st.lo, 4 * g - 4)
                sp.dma_start(wraw[:, 0], w_view(w, g)).then_inc(s_w[0], 16)

        sp.wait_ge(s_xT, 5)
        adaw_load(4)
        gemm_loads(gemms[0], w_in, ((s_ada_mm, 3), (s_ada_mm, 4)))
        for g in (10, 11):
            adaw_load(g)
        sp.wait_ge(gemms[0].lo, NIN)
        sp.dma_start(kraw[:], cache_sb_k[0, 0].rearrange("(b p) h d -> p b (h d)", p=P)).then_inc(s_kc, 16)
        sp.dma_start(vraw[:], cache_sb_v[0, 0].rearrange("(b p) h d -> p b (h d)", p=P)).then_inc(s_vc, 16)
        sp.wait_ge(s_rope, 3)
        sp.dma_start(stS[:], state_ret[0, 0].rearrange("h k v -> k h v")).then_inc(s_stS, 16)
        sp.wait_ge(s_tm, 10)
        store(v_prompt[0, 0].rearrange("(b p) h d -> p b (h d)", p=P), svt[:, 0:4, :])
        store(v_sample[0, 0].rearrange("p h d -> p (h d)"), svt[0:TS, 4, :])
        sp.wait_ge(s_tm, 15)
        store(k_prompt[0, 0].rearrange("(b p) h d -> p b (h d)", p=P), skt[:, 0:4, :])
        store(k_sample[0, 0].rearrange("p h d -> p (h d)"), skt[0:TS, 4, :])
        sp.wait_ge(s_rev, 3 * NH)
        store(st_prompt[0, 0].rearrange("h k v -> k h v"), stO[:])
        sp.wait_ge(s_rsn, NH)
        store(st_sample[0, 0].rearrange("h k v -> k h v"), stN[:])
        sp.wait_ge(s_out, 16 * n_out[0])

        gemm_loads(gemms[1], w_out, ((s_kt, NPB), (s_co, 1)))
        sp.wait_ge(s_glo, 5)
        sp.dma_start(skraw[:], peer_sub_keys[0].rearrange("a h k d -> k (a h) d")).then_inc(s_skl, 16)
        gemm_loads(gemms[2], peer_w_query, ((gemms[1].lo, 4), (gemms[1].lo, 8)))

        def u_load(tile, slot):
            sp.dma_start(uraw[:, slot], u_d[:, bass.ds(tile, 1), :].rearrange("p a d -> p (a d)")
                         ).then_inc(s_u[slot], 16)

        def v_load(pr_, slot):
            sp.dma_start(vrw[:, slot], v_d[:, bass.ds(2 * pr_, 2), :]).then_inc(s_v[slot], 16)

        def a_load(pr_, slot):
            sp.dma_start(al[:, slot], act_dram[:, bass.ds(pr_, 1), :].rearrange("p a t -> p (a t)")
                         ).then_inc(s_al[slot], 16)

        def g_load(b, slot):
            sp.dma_start(G[:, slot], gate_dram[:, bass.ds(b, 1), :, :].rearrange("p a t j -> p (a t) j")
                         ).then_inc(s_g[slot], 16)

        def g_store(n, q):
            b = 4 * n + q
            sp.wait_ge(s_gev, CREDIT + 8 * b + 8)
            sp.dma_start(gate_dram[:, :, bass.ds(TB * b, TB), :], gst[:, q % 2]).then_inc(s_gout[q % 2], 16)

        def u_next(m, par, tile=None):
            sp.wait_ge(s_ut, m + 1)
            u_load(2 * m + 4 if tile is None else tile, par)

        sp.wait_ge(gemms[2].lo, 16)
        u_load(0, 0)
        u_load(2, 1)

        def choice(n):
            for k in range(UPN):
                u_next(UPN * n + k, k % 2)
                if k >= UPN - UPG:
                    g_store(n, k - (UPN - UPG))

        with sp.Fori(0, 4) as n:
            choice(n)
        sp.wait_ge(s_sc, 20)
        v_load(0, 0)
        v_load(1, 1)
        for m in range(4 * UPN, NU):
            u_next(m, m % 2, None if m < NU - 2 else 2 * (m - (NU - 2)) + 1)
            if m == 5 * UPN - UPG:
                g_store(4, 0)
        sp.wait_ge(s_gout[0], 16 * 9)
        sp.wait_ge(s_gout[1], 16 * 8)
        g_load(0, 0)
        g_load(1, 1)
        for slot in range(2):
            sp.wait_ge(s_ao[slot], 16 * NU // 2)
        a_load(0, 0)
        a_load(1, 1)

        def expert_loads(i, last):
            for q in range(4):
                pr_ = 4 * i + q
                if not (last and q >= 2):
                    sp.wait_ge(s_ut, NU + pr_ + 1)
                    u_load(2 * pr_ + 5, q % 2)
                    sp.wait_ge(s_wv, 2 * pr_ + 1)
                    a_load(pr_ + 2, q % 2)
                    sp.wait_ge(s_vl, 2 * pr_ + 2)
                    v_load(pr_ + 2, q % 2)
                if q % 2 and not last:
                    sp.wait_ge(s_wv, 2 * pr_ + 2)
                    g_load(2 * i + q // 2 + 2, q // 2)

        with sp.Fori(0, 15) as i:
            expert_loads(i, False)
        expert_loads(15, True)

        for n, (t0, w) in enumerate(TILES):
            sp.wait_ge(s_ye, n + 1)
            dst = y_prompt[0, t0:t0 + w, :] if t0 < TP else y_sample[0]
            sp.dma_start(dst, ys[0:w, n % 2, :]).then_inc(s_yo[n % 2], 16)
        sp.wait_ge(s_yo[0], 48)
        sp.wait_ge(s_yo[1], 32)
        sp.wait_ge(s_out, 16 * n_out[0])

    @block.tensor
    def _(pe):
        mm = nc.tensor.matmul

        def mm3(out, ah, al, bh, bl, start, stop):
            mm(out, ah, bh, start=start, stop=False)
            mm(out, ah, bl, start=False, stop=False)
            return mm(out, al, bh, start=False, stop=stop)

        def sum_squares(st, k, b):
            pe.wait_ge(st.sq, k + 1)
            for x in range(2):
                last = mm(PS[:, b + x, 0:HT], ones[:], scr1[:, k, x * HT:(x + 1) * HT], start=(k == 0),
                          stop=(k == KD - 1))
            if k == KD - 1:
                last.then_inc(st.ss, 1)

        def sum_once(st, n, b):
            pe.wait_ge(s_sum, n)
            for x in range(2):
                last = mm(PS[:, b + x, 0:HT], ones[:], scr1[:, 0, x * HT:(x + 1) * HT], start=True, stop=True)
            last.then_inc(st.ss, 1)

        def ada(g, par, w):
            if not isinstance(g, int) or g >= 2:
                pe.wait_ge(s_adar, g - 1)
            for k in range(KD):
                last = mm(PS[0:2, 4 + par, :], siluT[:, k, :], w[:, k, :], start=(k == 0), stop=(k == KD - 1))
            last.then_inc(s_ada_mm, 1)

        def ada_turn(g, par, bank, col):
            pe.wait_ge(s_adar, g + 1)
            for x in range(4):
                last = mm(PS[:, bank, bass.ds(col + 2 * x, 2)], adar[0:2, par, x * P:(x + 1) * P], ident[0:2, 0:2],
                          start=True, stop=True)
            last.then_inc(s_adat, 1)

        def gemm_chunk(st, c, par, hi=None, lo=None):
            hi, lo = (whi[:, par], wlo[:, par]) if hi is None else (hi, lo)
            pe.wait_ge(st.lo, c + 1)
            pe.wait_ge(st.ev, st.reads * (c + 1))
            for b in range(2):
                for k in range(KD):
                    last = mm3(PS[:, 2 * par + b, 0:HT], hi[:, k, :], lo[:, k, :], XH[:, k, b * HT:(b + 1) * HT], 
                               XL[:, k, b * HT:(b + 1) * HT], k == 0, k == KD - 1)
            last.then_inc(st.mm, 1)

        def gemm_start(st, parts):
            pe.wait_ge(st.lo, 2)
            for ks, waits in parts:
                for c in range(2):
                    for b in range(2):
                        for s_, v in waits[c][b]:
                            pe.wait_ge(s_, v)
                        for k in ks:
                            last = mm3(PS[:, 2 * c + b, 0:HT], whi[:, c, k, :], wlo[:, c, k, :],
                                       XH[:, k, b * HT:(b + 1) * HT], XL[:, k, b * HT:(b + 1) * HT], k == 0,
                                       k == KD - 1)
                    if ks[-1] == KD - 1:
                        last.then_inc(st.mm, 1)

        def chunk_by_chunk(done, n, value):
            return [((k,), ((((done, value(k)),), ()), ((), ()))) for k in range(n, KD)]

        def gemm(st):
            def group(g, slot, first=0):
                for cc in range(first, 4):
                    if first and cc == 2:
                        gemm_chunk(st, 2, 0, wxh, wxl)
                    else:
                        gemm_chunk(st, 4 * g + cc, cc % 2)
                    if st is gemms[0] and cc == 2:
                        pe.wait_ge(s_adaw, 16 * g + 32)
                        ada(g + 5, 1 - slot, adaw)
                    if st is gemms[0] and cc == 3:
                        ada_turn(g + 5, 1 - slot, 7, 8 * g + 8)

            group(0, 0, 2)
            group(1, 1)
            with pe.Fori(1, st.groups // 2) as i:
                for slot in range(2):
                    group(2 * i + slot, slot)
            if st.groups % 2:
                group(st.groups - 1, 0)

        pe.wait_ge(s_cst, 16)
        pe.wait_ge(s_rows, 16 * 7)
        nc.tensor.transpose(PS[:, 6, 0:R_N], rows[0:R_N, :], ident[0:R_N, 0:R_N]).then_inc(s_rowsT_ps, 1)
        pe.wait_ge(s_x, 32)
        for n, (t0, w) in enumerate(TILES):
            if n >= 2:
                pe.wait_ge(s_hT, n - 1)
            b = 2 + 2 * (n % 2)
            for k in range(KD):
                last = nc.tensor.transpose(PS[:, b + k // 4, (k % 4) * P:(k % 4) * P + w],
                                           xin[0:w, n, k * P:(k + 1) * P], ident[0:w, 0:w])
            last.then_inc(s_xT, 1)
        pe.wait_ge(s_rowsT, 1)
        pe.wait_ge(s_silu, 1)
        pe.wait_ge(s_hT, 5)
        for g in range(4):
            pe.wait_ge(s_w[g % 2], 16 * (g // 2) + 16)
            ada(g, g % 2, wraw[:, g % 2])
            if g == 1:
                pe.wait_ge(s_init, 1)
                sum_once(norms[0], 1, 0)
            if g >= 1:
                ada_turn(g - 1, (g - 1) % 2, 6, 8 * (g - 1))
        ada_turn(3, 1, 6, 24)
        pe.sem_inc(gemms[0].mm, CREDIT)
        pe.wait_ge(s_adaw, 16)
        ada(4, 0, adaw)
        pe.wait_ge(norms[0].sd, 1)
        gemm_start(gemms[0], chunk_by_chunk(norms[0].lo, 0, lambda k: k + 1))
        ada_turn(4, 0, 7, 0)
        gemm(gemms[0])

        pe.wait_ge(gemms[0].ev, CREDIT + NIN)
        n = 0
        for chunk in (RV, SV, SK, RK):
            if chunk == SK:
                pe.wait_ge(s_kc, 16)
                for b in range(NPB):
                    if b >= 2:
                        pe.wait_ge(s_kte, b - 1)
                    for h in range(NH):
                        last = nc.tensor.transpose(PS[:, 4 + b % 2, h * P:(h + 1) * P],
                                                   kraw[:, b, h * P:(h + 1) * P], ident)
                    last.then_inc(s_kt, 1)
            if chunk == RK:
                pe.wait_ge(s_rope, 3)
            for t0, w in TILES:
                if n >= 4:
                    m = n - 4
                    if m < 15:
                        pe.wait_ge(s_tm, m + 1)
                    else:
                        pe.wait_ge(s_rkd, m - 14)
                for h in range(NH):
                    last = nc.tensor.transpose(PS[0:w, n % 4, h * P:(h + 1) * P], projT[:, chunk + h, t0:t0 + w], ident)
                last.then_inc(s_tp, 1)
                n += 1

        pe.wait_ge(s_rkd, 5)
        pe.wait_ge(s_tm, 15)
        pe.wait_ge(s_kte, NPB)
        pe.wait_ge(s_stS, 16)
        pe.wait_ge(s_qds, 2)
        for h in range(NH):
            hs = slice(h * P, (h + 1) * P)
            for kb in range(QB):
                if h >= 1:
                    pe.wait_ge(s_rp, QB * (h - 1) + kb + 1)
                mm(PS[:, kb, 0:TP - P * kb], projT[:, RK + h, kb * P:(kb + 1) * P], projT[:, RQ + h, kb * P:TP],
                   start=True, stop=True).then_inc(s_rs_mm, 1)
            if h >= 2:
                pe.wait_ge(s_rev, 3 * (h - 1))
                pe.wait_ge(s_rsn, h - 1)
                pe.wait_ge(s_rps, h - 1)
            aux = 6 + h % 2
            for kb in range(QB):
                mm(PS[:, aux, 0:P], rkd[:, kb, hs], rvt[:, kb, hs], start=(kb == 0), stop=(kb == QB - 1))
            mm(PS[0:TS, aux, P:P + TS], projT[:, RK + h, TP:T], projT[:, RQ + h, TP:T], start=True, stop=True)
            mm(PS[:, aux, 256:384], rkd[0:TS, 4, hs], rvt[0:TS, 4, hs], start=True, stop=True).then_inc(s_raux, 1)
            for kb in range(QB):
                pe.wait_ge(s_rp, QB * h + kb + 1)
                last = mm(PS[:, 4 + h % 2, kb * P:TP], rvt[:, kb, hs], pr[:, h % 2, pcol(kb):pcol(kb) + TP - P * kb],
                          start=(kb == 0), stop=(kb == QB - 1))
            last.then_inc(s_ro, 1)
            pe.wait_ge(s_rps, h + 1)
            pe.wait_ge(s_rsn, h + 1)
            mm(PS[:, aux, 384:384 + TS], stS[:, h, :], qds[:, h, :], start=True, stop=False)
            mm(PS[:, aux, 384:384 + TS], rvt[:, 4, hs], prs[:, h, :], start=False, stop=True).then_inc(s_ros, 1)

        pe.wait_ge(s_rev, 3 * NH)
        pe.wait_ge(s_rsn, NH)
        for h in range(NH):
            for b in range(2):
                last = mm(PS[:, 2 * h + b, 0:HT], meanw[:], projT[:, h, b * HT:(b + 1) * HT], start=True, stop=True)
            last.then_inc(s_gm, 1)
        for h in range(NH):
            pe.wait_ge(s_gsq, h + 1)
            for b in range(2):
                last = mm(PS[:, 2 * h + b, 0:HT], meanw[:], sqb[:, h, b * HT:(b + 1) * HT], start=True, stop=True)
            last.then_inc(s_gv, 1)
        pe.wait_ge(s_gsd, NH)
        pe.wait_ge(s_sqs, 1)

        def sb_z(h):
            if h >= 2:
                pe.wait_ge(s_bev, h - 1)
            for kb in range(QB):
                mm(PS[:, 4 * (h % 2) + kb, 0:TP - P * kb], projT[:, SK + h, kb * P:(kb + 1) * P],
                   projT[:, SQ + h, kb * P:TP], start=True, stop=True).then_inc(s_bz, 1)

        def sb_sums(h):
            pe.wait_ge(s_blk, QB * (h + 1))
            for kb in reversed(range(QB)):
                w = TP - P * kb
                out = PS[:, 4 * (h % 2) + kb, 0:w]
                last = mm(out, ntri, lk[:, h % 2, pcol(kb):pcol(kb) + w], start=False, stop=(kb == QB - 1),
                          skip_group_check=True)
                for later in range(kb + 1, QB):
                    wl_ = TP - P * later
                    last = mm(out[:, w - wl_:w], negones[:], lk[:, h % 2, pcol(later):pcol(later) + wl_],
                              start=False, stop=(later == QB - 1), skip_group_check=True)
                last.then_inc(s_bc, 1)

        def sb_out(h):
            pe.wait_ge(s_ba, 7 * (h + 1))
            for kb in range(QB):
                last = mm(PS[:, 4 * (h % 2), kb * P:TP], svt[:, kb, h * P:(h + 1) * P],
                          aw[:, 0, pcol(kb):pcol(kb) + TP - P * kb], start=(kb == 0), stop=(kb == QB - 1))
            last.then_inc(s_bo, 1)

        def sample_z():
            pe.wait_ge(s_bev, NH - 1)
            for b in range(NPB):
                for h in range(NH):
                    mm(PS[:, b // 4, (b % 4) * P + h * TS:(b % 4) * P + (h + 1) * TS], kT[:, h, b * P:(b + 1) * P],
                       projT[:, SQ + h, TP:T], start=(b % 4 == 0 and h == 0), stop=(b % 4 == 3 and h == NH - 1),
                       skip_group_check=True)
            for h in range(NH):
                last = mm(PS[0:TS, 2, h * TS:(h + 1) * TS], projT[:, SK + h, TP:T], projT[:, SQ + h, TP:T],
                          start=(h == 0), stop=(h == NH - 1), skip_group_check=True)
            last.then_inc(s_cz, 1)
            pe.sem_inc(gemms[1].mm, CREDIT)

        sb_z(0)
        sb_z(1)
        sb_sums(0)
        for h in range(NH):
            sb_out(h)
            if h < NH - 1:
                sb_sums(h + 1)
            if h < NH - 2:
                sb_z(h + 2)
            if h == NH - 2:
                sample_z()
        pe.wait_ge(s_clk, 1)
        for b in range(NPB):
            out = PS[:, b // 4, (b % 4) * P:(b % 4 + 1) * P]
            mm(out, ntri, lks[:, b, :], start=False, stop=False, skip_group_check=True)
            if b < NPB - 1:
                mm(out, negones[:], rsum[:, b, :], start=False, stop=False, skip_group_check=True)
            mm(out, negones[:], lks[:, NPB, :], start=False, stop=True, skip_group_check=True)
        mm(PS[0:TS, 2, 0:P], ntri[:, 0:TS], lks[:, NPB, :], start=False, stop=True,
           skip_group_check=True).then_inc(s_cc, 1)
        pe.wait_ge(s_ca, 2)
        pe.wait_ge(s_vc, 16)
        for h in range(NH):
            hs = slice(h * P, (h + 1) * P)
            for b in range(NPB + 1):
                lhs = vraw[:, b, hs] if b < NPB else svt[:, 4, hs]
                last = mm(PS[:, 3, h * TS:(h + 1) * TS], lhs, aws[:, b, h * TS:(h + 1) * TS], start=(b == 0),
                          stop=(b == NPB))
        last.then_inc(s_co, 1)

        pe.wait_ge(s_bev, NH)
        def sub_keys(n):
            pe.wait_ge(s_skl, 16)
            if n >= 2:
                pe.wait_ge(s_skT, n - 1)
            for m in range(4):
                last = nc.tensor.transpose(PS[:, 6 + n % 2, m * P:(m + 1) * P], skraw[:, 4 * n + m, :], ident)
            last.then_inc(s_skp, 1)

        gemm_start(gemms[1], [((0, 1, 2, 3), (((((s_glo, 1),), ()), ((), ((s_cev, 1),)))))]
                   + chunk_by_chunk(s_glo, 4, lambda k: k - 2))
        for c in range(2, KD):
            if c == 2:
                gemm_chunk(gemms[1], 2, 0, wxh, wxl)
            else:
                gemm_chunk(gemms[1], c, c % 2)
            if 3 <= c < 7:
                sub_keys(c - 3)
        pe.sem_inc(gemms[2].mm, CREDIT)
        sum_once(norms[1], 2, 4)
        pe.wait_ge(gemms[1].ev, 3 * (CREDIT + 8))
        gemm_start(gemms[2], chunk_by_chunk(norms[1].lo, 0, lambda k: 2 * k + 2))
        gemm(gemms[2])

        pe.wait_ge(gemms[2].ev, CREDIT + 16)

        def scores(n, w):
            for hp in range(16):
                last = mm(PS[0:w, 4 + hp // 4, (hp % 4) * P:(hp % 4 + 1) * P], qT[:, hp, bass.ds(P * n, w)],
                          skT[:, (hp % 2) * PH + hp // 2, :], start=True, stop=True)
                if hp % 4 == 3:
                    last.then_inc(s_sc, 1)

        def turn(m, par, arrivals):
            pe.wait_ge(s_u[par], 16 * arrivals)
            if not isinstance(m, int) or m >= 1:
                pe.wait_ge(s_utl, m)
            for k in range(KD):
                last = mm(PS[:, k // 4, (k % 4) * P:(k % 4 + 1) * P], uraw[:, par, k * P:(k + 1) * P], ident,
                          start=(k % 4 == 0), stop=(k % 4 == 3), is_transpose=True, skip_group_check=True)
            last.then_inc(s_ut, 1)

        def less_hi(m, par):
            pe.wait_ge(s_uth, m + 1)
            for b in range(2):
                last = mm(PS[:, b, :], negI[:], uth[:, par, 4 * b:4 * b + 4, :].rearrange("p k i -> p (k i)"),
                          start=False, stop=True, skip_group_check=True)
            last.then_inc(s_us, 1)

        def up(m, par, b, first):
            if b == 0:
                pe.wait_ge(s_utl, m + 1)
            if not first:
                pe.wait_ge(s_gel, 2 * m - 1 + b)
            for k in range(KD):
                last = mm3(PS[:, 2 + b, 0:HT], uth[:, par, k, :], utl[:, par, k, :],
                           XH[:, k, b * HT:(b + 1) * HT], XL[:, k, b * HT:(b + 1) * HT], k == 0, k == KD - 1)
            last.then_inc(s_up, 1)

        def u_half(m, b, first=False):
            par = m % 2
            if b == 0:
                turn(m + 1, 1 - par, (m + 1) // 2 + 1)
            up(m, par, b, first)
            if b == 0:
                less_hi(m + 1, 1 - par)

        def gates(n, g):
            for r in range(OG // 4):
                pe.wait_ge(s_gev, 2 * (NG * n + g) + r + 1)
                if r == 0:
                    pe.wait_ge(s_oh, NG * n + g + 1)
                for x in range(4):
                    for part in range(3):
                        last = mm(PS[:, 4 + r, x * P:(x + 1) * P], ohA[:, g % 2, :, 4 * r + x],
                                  ohB[:, part, g % 2, :, 4 * r + x], start=(part == 0), stop=(part == 2))
                last.then_inc(s_gmm, 1)

        def sel_turn(n, w):
            pe.wait_ge(s_sel, n + 1)
            for c in range(3):
                last = nc.tensor.transpose(PS[:, 6, c * P:c * P + w], sel[0:w, c, :], ident[0:w, 0:w])
            last.then_inc(s_selT, 1)

        def choice(n, w_next):
            for k in range(UPN - UPG):
                if k == UPN - UPG - 1:
                    sel_turn(n, P)
                u_half(UPN * n + k, 0, n == 0 and k == 0)
                u_half(UPN * n + k, 1, n == 0 and k == 0)
            for g in range(NG):
                if g == NG - 4:
                    pe.wait_ge(s_scev, 4 * n + 6)
                gates(n, g)
                if g == NG - 5:
                    pe.wait_ge(s_gev, CREDIT + 2 * (NG * n + g + 1))
                    scores(n + 1, w_next)
                if g % 2:
                    u_half(UPN * n + UPN - UPG + g // 4, g // 2 % 2)

        scores(0, P)
        turn(0, 0, 1)
        less_hi(0, 0)
        for n in range(4):
            choice(n, P if n < 3 else TS)
        for m in range(4 * UPN, NU):
            if m == 5 * UPN - UPG - 1:
                sel_turn(4, TS)
            for b in range(2):
                if m == 5 * UPN - UPG:
                    gates(4, 2 * b)
                    gates(4, 2 * b + 1)
                u_half(m, b)

        def down(pr_, par, squares=False):
            pe.wait_ge(s_vl, 2 * pr_ + 2)
            pe.wait_ge(s_wl, 2 * pr_ + 2)
            for n in range(16):
                dc, b = n // 2, n % 2
                pe.wait_ge(s_add, 16 * pr_ + n + 1)
                for r in range(2):
                    last = mm3(PS[:, 4 + n % 4, 0:HT], vh[:, par, r, dc * P:(dc + 1) * P],
                               vl[:, par, r, dc * P:(dc + 1) * P], wh[:, par, r, b * HT:(b + 1) * HT],
                               wl[:, par, r, b * HT:(b + 1) * HT], r == 0, r == 1)
                last.then_inc(s_om, 1)
                if squares and n >= 5 and n % 2:
                    sum_squares(norms[2], (n - 5) // 2, 0)

        def iteration(i, first, last):
            for q in range(4):
                pr_ = 4 * i + q
                up(NU + pr_, q % 2, 0, False)
                up(NU + pr_, q % 2, 1, False)
                if not (last and q == 3):
                    turn(NU + pr_ + 1, (q + 1) % 2, NU // 2 + 2 * i + (q + 1) // 2 + 1)
                if not (first and q == 0):
                    down(pr_ - 1, (q + 1) % 2)

        iteration(0, True, False)
        with pe.Fori(1, 15) as i:
            iteration(i, False, False)
        iteration(15, False, True)
        down(63, 1, True)

        for k in (KD - 2, KD - 1):
            sum_squares(norms[2], k, 0)
        for n, (t0, w) in enumerate(TILES):
            if n >= 2:
                pe.wait_ge(s_ye, n - 1)
            b = 2 + 2 * (n % 2)
            for k in range(KD):
                if n == 0:
                    pe.wait_ge(norms[2].y, k + 1)
                last = nc.tensor.transpose(PS[0:w, b + k // 4, (k % 4) * P:(k % 4 + 1) * P], scr2[:, k, t0:t0 + w],
                                           ident)
            last.then_inc(s_yt, 1)

    @block.scalar
    def _(act):
        act_ = nc.scalar.activation
        chain = [0]

        def link(ins):
            chain[0] += 1
            ins.then_inc(s_ach, 1)
            act.wait_ge(s_ach, chain[0])

        def squares(st, ready, b, rows=0):
            for k in range(KD):
                act.wait_ge(ready[0], ready[1] + ready[2] * k)
                act_(scr1[:, k, :], hT[:, k, :], ACT.Square).then_inc(st.sq, 1)
                if st is norms[1] and 2 <= k < 6:
                    act.wait_ge(s_skp, k - 1)
                    act_(skT[:, 4 * k - 8:4 * k - 4, :], PS[:, 6 + k % 2, :].rearrange("p (m k) -> p m k", m=4),
                         ACT.Copy).then_inc(s_skT, 1)
            for g in range(rows):
                ada_row(g, g % 2)
            act.wait_ge(st.ss, 1)
            act_(halves(rs[:]), pair(b), ACT.Sqrt, bias=epsc[:, 0:1], scale=1.0 / D).then_inc(st.sd, 1)

        def ada_row(g, par):
            act.wait_ge(s_ada_mm, g + 1)
            if not isinstance(g, int) or g >= 2:
                act.wait_ge(s_adat, g - 1)
            act_(adar[0:2, par, :], PS[0:2, 4 + par, :], ACT.Copy).then_inc(s_adar, 1)

        def gemm_out(st, out):
            act.sem_inc(st.ev, CREDIT)

            def group(g, slot=0):
                for cc in range(4):
                    c = 4 * g + cc
                    act.wait_ge(st.mm, c + 1 + CREDIT)
                    act_(out[:, bass.ds(c, 1), :].rearrange("p a (b t) -> p (a b) t", b=2), pair(2 * (cc % 2)),
                         ACT.Copy).then_inc(st.ev, 1)
                    if st is gemms[0] and cc == 2:
                        ada_row(g + 5, 1 - slot)

            if st is gemms[0]:
                with act.Fori(0, st.groups // 2) as i:
                    for slot in range(2):
                        group(2 * i + slot, slot)
                group(st.groups - 1)
            else:
                with act.Fori(0, st.groups) as g:
                    group(g)

        act.wait_ge(s_rowsT, 1)
        act_(siluT[:].rearrange("p k g -> p g k"), rowsT[:, 0:16].rearrange("p (g k) -> p g k", g=2),
             ACT.Silu).then_inc(s_silu, 1)
        act.wait_ge(s_init, 1)
        squares(norms[0], (s_hT, 5, 0), 0, 2)
        for g in range(2, 4):
            ada_row(g, g % 2)
        for k in range(KD):
            act.wait_ge(norms[0].y, 2 * k + 2)
            act_(XH[:, k, :], scr1[:, k, :], ACT.Copy).then_inc(norms[0].hi, 1)
        ada_row(4, 0)
        act.wait_ge(norms[0].lo, KD)
        gemm_out(gemms[0], projT)

        act.wait_ge(gemms[0].ev, CREDIT + NIN)
        act.wait_ge(gemms[0].mm, CREDIT + NIN)
        act_(sw[0:64], projT[64:128, 0:8, :], ACT.Copy).then_inc(s_swap, 1)
        for n in range(15):
            if n == 10:
                for b in range(NPB):
                    act.wait_ge(s_kt, b + 1)
                    act_(kT[:, :, b * P:(b + 1) * P], PS[:, 4 + b % 2, :].rearrange("p (h k) -> p h k", h=NH),
                         ACT.Copy).then_inc(s_kte, 1)
                act.wait_ge(s_rope, 3)
            act.wait_ge(s_tp, n + 1)
            if n == 0:
                act.wait_ge(s_zero, 2)
            t0, w = TILES[n % 5]
            dst = (rvt, svt, skt)[n // 5]
            act_(dst[0:w, n % 5, :], PS[0:w, n % 4, :], ACT.Copy).then_inc(s_tm, 1)
        act_(projT[:, RG:RG + NH, :], projT[:, RG:RG + NH, :], ACT.Silu).then_inc(s_gate, 1)
        for h in range(NH):
            act.wait_ge(s_raux, h + 1)
            act_(stO[:, h, :], PS[:, 6 + h % 2, 0:P], ACT.Copy).then_inc(s_rev, 1)
            act.wait_ge(s_ro, h + 1)
            act_(projT[:, RQ + h, 0:TP], PS[:, 4 + h % 2, :], ACT.Copy).then_inc(s_rev, 1)
            act.wait_ge(s_ros, h + 1)
            act_(projT[:, RQ + h, TP:T], PS[:, 6 + h % 2, 384:384 + TS], ACT.Copy).then_inc(s_rev, 1)
        for h in range(NH):
            act.wait_ge(s_gcen, h + 1)
            act_(sqb[:, h, :], projT[:, h, :], ACT.Square).then_inc(s_gsq, 1)
        for h in range(NH):
            act.wait_ge(s_gv, h + 1)
            act_(halves(rsb[:, h, :]), pair(2 * h), ACT.Sqrt, bias=epsc[:, 0:1]).then_inc(s_gsd, 1)

        nc.scalar.preload_act_table_set("natural_log_exp_and_others")

        def softplus(h):
            par = h % 2
            act.wait_ge(s_bz, QB * (h + 1))
            if h >= 2:
                act.wait_ge(s_bo, h - 1)
            for kb in range(QB):
                w = TP - P * kb
                act_(lk[:, par, pcol(kb):pcol(kb) + w], PS[:, 4 * par + kb, 0:w], ACT.Abs).then_inc(s_ach, 1)
            chain[0] += QB
            act.wait_ge(s_ach, chain[0])
            link(act_(lk[:, par, :], lk[:, par, :], ACT.Exp, scale=-1.0))
            act_(lk[:, par, :], lk[:, par, :], ACT.Ln, bias=1.0).then_inc(s_bln, 1)

        def weights(h):
            par = h % 2
            if h >= 1:
                act.wait_ge(s_bo, h)
            for kb in reversed(range(QB)):
                w = TP - P * kb
                act.wait_ge(s_bmin, QB * h + QB - kb)
                if w > P:
                    act_(aw[:, 0, pcol(kb) + P:pcol(kb) + w], PS[:, 4 * par + kb, P:w], ACT.Exp).then_inc(s_ba, 1)
                act_(aw[:, 0, pcol(kb):pcol(kb) + P], aw[:, 0, pcol(kb):pcol(kb) + P], ACT.Exp).then_inc(s_ba, 1)

        def result(h):
            act.wait_ge(s_bo, h + 1)
            act_(projT[:, SQ + h, 0:TP], PS[:, 4 * (h % 2), :], ACT.Copy).then_inc(s_bev, 1)

        def softplus_sample():
            act.wait_ge(s_cz, 1)
            act.wait_ge(s_zero, 4)
            act_(lks[:, 0:NPB, :], PS[:, 0:2, :].rearrange("p b (c x) -> p (b c) x", x=P), ACT.Abs).then_inc(s_ach, 1)
            act_(lks[0:TS, NPB, :], PS[0:TS, 2, 0:P], ACT.Abs).then_inc(s_ach, 1)
            chain[0] += 2
            act.wait_ge(s_ach, chain[0])
            act_(lks[:, 0:NPB, :], lks[:, 0:NPB, :], ACT.Exp, scale=-1.0).then_inc(s_ach, 1)
            act_(lks[0:TS, NPB, :], lks[0:TS, NPB, :], ACT.Exp, scale=-1.0).then_inc(s_ach, 1)
            chain[0] += 2
            act.wait_ge(s_ach, chain[0])
            act_(lks[:, 0:NPB, :], lks[:, 0:NPB, :], ACT.Ln, bias=1.0).then_inc(s_cln, 1)
            act_(lks[0:TS, NPB, :], lks[0:TS, NPB, :], ACT.Ln, bias=1.0).then_inc(s_cln, 1)

        softplus(0)
        softplus(1)
        weights(0)
        result(0)
        for h in range(1, NH):
            weights(h)
            if h < NH - 1:
                softplus(h + 1)
            else:
                softplus_sample()
            result(h)
            if h == 2:
                act.wait_ge(s_gy, 4)
                act.wait_ge(s_out, 96)
                act_(XH[:, 0:4, :], projT[:, 0:4, :], ACT.Copy).then_inc(s_ghi, 1)
        act.wait_ge(s_cc, 1)
        act_(aws[:, 0:NPB, :], PS[:, 0:2, :].rearrange("p b (c x) -> p (b c) x", x=P), ACT.Exp).then_inc(s_ca, 1)
        act.wait_ge(s_cmin, 1)
        act_(aws[0:TS, NPB, :], aws[0:TS, NPB, :], ACT.Exp).then_inc(s_ca, 1)
        act.wait_ge(s_co, 1)
        act_(projT[:, SQ:SQ + NH, TP:T], PS[:, 3, 0:P].rearrange("p (h t) -> p h t", h=NH),
             ACT.Copy).then_inc(s_cev, 1)
        act.wait_ge(s_cev, 1)
        for h in range(NH):
            act_(XH[:, 4 + h, :], projT[:, SQ + h, :], ACT.Copy).then_inc(s_ghi, 1)
        squares(norms[1], (gemms[1].ev, 3 * (CREDIT + 1), 3), 4)
        for k in range(KD):
            act.wait_ge(norms[1].tmp, 2 * k + 2)
            for g, cols in enumerate((slice(0, TP), slice(TP, T))):
                act_(XH[:, k, cols], scr2[:, k, cols], ACT.Identity, bias=modT[:, 24 + k, g:g + 1]
                     ).then_inc(norms[1].hi, 1)
        act.wait_ge(norms[1].lo, 2 * KD)
        gemm_out(gemms[2], qT)

        def scores_out(n, w):
            for q in range(4):
                act.wait_ge(s_sc, 4 * n + q + 1)
                if q == 0 and (not isinstance(n, int) or n >= 1):
                    act.wait_ge(s_sel, n)
                act_(S[0:w, 4 * q:4 * q + 4, :], PS[0:w, 4 + q, :].rearrange("p (m k) -> p m k", m=4),
                     ACT.Copy).then_inc(s_scev, 1)

        def u_hi(m, par, first=False):
            act.wait_ge(s_ut, m + 1)
            if not first:
                act.wait_ge(s_up, 2 * m - 2)
            act_(uth[:, par], PS[:, 0:2, :].rearrange("p b (k i) -> p (b k) i", i=P), ACT.Copy).then_inc(s_uth, 1)

        def u_lo(m, par):
            act.wait_ge(s_us, m + 1)
            act_(utl[:, par], PS[:, 0:2, :].rearrange("p b (k i) -> p (b k) i", i=P), ACT.Copy).then_inc(s_utl, 1)

        def gelu(m, par, b):
            act.wait_ge(s_up, 2 * m + b + 1)
            act_(gel[:, par, b * HT:(b + 1) * HT], PS[:, 2 + b, 0:HT], ACT.Gelu_apprx_tanh).then_inc(s_gel, 1)

        def u_half(m, par, half, b, first=False):
            if b == 0:
                u_hi(m + 1, 1 - par, first)
                if not isinstance(m, int) or m >= 2:
                    act.wait_ge(s_ao[par], 16 * half)
                gelu(m, par, 0)
            else:
                u_lo(m + 1, 1 - par)
                gelu(m, par, 1)
                act.wait_ge(s_gel, 2 * m + 2)
                act.dma_start(act_dram[:, bass.ds(m, 1), :].rearrange("p a t -> p (a t)"), gel[:, par]
                              ).then_inc(s_ao[par], 16)

        def gates_out(n, g):
            q = g // 4
            if g % 4 == 0 and (q >= 2 or not isinstance(n, int) or n >= 1):
                act.wait_ge(s_gout[q % 2], 32 * n + 16 * (q // 2))
            for r in range(OG // 4):
                t0 = OG * (g % 4) + 4 * r
                act.wait_ge(s_gmm, 2 * (NG * n + g) + r + 1)
                act_(gst[:, q % 2, :, t0:t0 + 4, :],
                     PS[:, 4 + r, :].rearrange("p (t b j) -> p b t j", t=4, j=JB), ACT.Copy).then_inc(s_gev, 1)

        def sel_out(n, w):
            act.wait_ge(s_selT, n + 1)
            if not isinstance(n, int) or n >= 1:
                act.wait_ge(s_oh, 16 * n)
            act_(selT[:, :, 0:w], PS[:, 6, 0:3 * P].rearrange("p (c t) -> p c t", c=3)[:, :, 0:w],
                 ACT.Copy).then_inc(s_selTe, 1)

        def softmax_exp(n, w):
            act.wait_ge(s_exd, n + 1)
            act_(ex[0:w], tops[0:w], ACT.Exp).then_inc(s_exa, 1)

        def choice(n, w_next, first=False):
            for k in range(UPN - UPG):
                if k == UPN - UPG - 1:
                    sel_out(n, P)
                for b in range(2):
                    u_half(UPN * n + k, k % 2, UPN // 2 * n + k // 2, b, first and k == 0)
                if k == 5:
                    softmax_exp(n, P)
            for g in range(NG):
                gates_out(n, g)
                if g == NG - 5:
                    scores_out(n + 1, w_next)
                if g % 2:
                    k = UPN - UPG + g // 4
                    u_half(UPN * n + k, k % 2, UPN // 2 * n + k // 2, g // 2 % 2)

        scores_out(0, P)
        act.sem_inc(s_gev, CREDIT)
        u_hi(0, 0, True)
        u_lo(0, 0)
        choice(0, P, True)
        with act.Fori(1, 3) as n:
            choice(n, P)
        choice(3, TS)
        for m in range(4 * UPN, NU):
            if m == 5 * UPN - UPG - 1:
                sel_out(4, TS)
            for b in range(2):
                if m == 5 * UPN - UPG:
                    gates_out(4, 2 * b)
                    gates_out(4, 2 * b + 1)
                u_half(m, m % 2, m // 2, b)
            if m == 4 * UPN + 5:
                softmax_exp(4, TS)

        def w_hi(t, r, par):
            act.wait_ge(s_wv, t + 1)
            if not isinstance(t, int) or t >= 4:
                act.wait_ge(s_om, 8 * t - 8 * r - 16)
            act_(wh[:, par, r, :], wv[:, r, :], ACT.Copy).then_inc(s_wh, 1)

        def iteration(i, last):
            for q in range(4):
                pr_, par = 4 * i + q, q % 2
                w_hi(2 * pr_, 0, par)
                if isinstance(pr_, int) and pr_ < 2:
                    act.wait_ge(s_ao[par], 16 * NU // 2)
                else:
                    act.wait_ge(s_wv, 2 * pr_ - 2)
                gelu(NU + pr_, par, 0)
                gelu(NU + pr_, par, 1)
                if not (last and q == 3):
                    u_hi(NU + pr_ + 1, 1 - par)
                w_hi(2 * pr_ + 1, 1, par)

        iteration(0, False)
        with act.Fori(1, 15) as i:
            iteration(i, False)
        iteration(15, True)

        squares(norms[2], (s_h2, 2, 2), 0)
        for n, (t0, w) in enumerate(TILES):
            act.wait_ge(s_yt, n + 1)
            if n >= 2:
                act.wait_ge(s_yo[n % 2], 16 * (n // 2))
            b = 2 + 2 * (n % 2)
            act_(ys[0:w, n % 2, :].rearrange("p (b x) -> p b x", b=2), PS[0:w, b:b + 2, :], ACT.Copy).then_inc(s_ye, 1)

    @block.gpsimd
    def _(pool):
        def pass_wait():
            pool.sem_inc(s_pool, 1)

        def gemm_hi(st):
            def group(g, slot, i):
                for cc in range(4):
                    c = 4 * g + cc
                    out = whi[:, cc % 2]
                    if cc == 0:
                        pool.wait_ge(s_w[slot], 16 * (st.before[slot] + 1) + 16 * i)
                    if isinstance(c, int) and c == 2:
                        out = wxh[:]
                    else:
                        pool.wait_ge(st.mm, c + 1)
                    pass_wait()
                    nc.gpsimd.tensor_copy(out, wraw[:, slot, :, cc * P:(cc + 1) * P]).then_inc(st.hi, 1)

            group(0, 0, 0)
            group(1, 1, 0)
            if st.groups > 3:
                with pool.Fori(1, st.groups // 2) as i:
                    for slot in range(2):
                        group(2 * i + slot, slot, i)
            if st.groups % 2:
                group(st.groups - 1, 0, st.groups // 2)

        gemm_hi(gemms[0])
        pool.wait_ge(gemms[0].ev, CREDIT + NIN)
        pool.wait_ge(gemms[0].mm, CREDIT + NIN)
        nc.gpsimd.tensor_copy(sw[64:128], projT[0:64, 0:8, :]).then_inc(s_swap, 1)
        pool.wait_ge(s_cz, 1)
        gemm_hi(gemms[1])
        pool.wait_ge(gemms[1].mm, CREDIT + 8)
        gemm_hi(gemms[2])

        def v_hi(pr_, par, rnd):
            pool.wait_ge(s_v[par], 16 * rnd + 16)
            for r in range(2):
                if not isinstance(pr_, int) or pr_ >= 2:
                    pool.wait_ge(s_om, 16 * pr_ - 16)
                pass_wait()
                nc.gpsimd.tensor_copy(vh[:, par, r, :], vrw[:, par, r, :]).then_inc(s_vh, 1)

        pool.wait_ge(s_gev, CREDIT + 8 * 17)
        pool.wait_ge(s_gout[0], 16 * 9)
        pool.wait_ge(s_gout[1], 16 * 8)
        v_hi(0, 0, 0)
        v_hi(1, 1, 0)
        with pool.Fori(1, 32) as i:
            for par in range(2):
                v_hi(2 * i + par, par, i)

    @block.vector
    def _(dve):
        tt, ts, stt = nc.vector.tensor_tensor, nc.vector.tensor_scalar, nc.vector.scalar_tensor_tensor
        chain = [0]

        def link(*ins):
            for x in ins:
                chain[0] += 1
                x.then_inc(s_dch, 1)
            dve.wait_ge(s_dch, chain[0])

        def lo(st, c, slot, cc):
            dve.wait_ge(st.hi, c + 1)
            hi_, lo_ = (wxh[:], wxl[:]) if isinstance(c, int) and c == 2 else (whi[:, cc % 2], wlo[:, cc % 2])
            tt(lo_, wraw[:, slot, :, cc * P:(cc + 1) * P], f(hi_), ALU.subtract).then_inc(st.lo, 1)

        def gemm_lo(st, done):
            for c in range(done, 8):
                lo(st, c, c // 4, c % 4)
            with dve.Fori(1, st.groups // 2) as i:
                for slot in range(2):
                    for cc in range(4):
                        lo(st, 4 * (2 * i + slot) + cc, slot, cc)
            for c in range(4 * (st.groups - st.groups % 2), 4 * st.groups):
                lo(st, c, 0, c % 4)

        def coefficients(n):
            g0 = (R_N1, R_N2)[n]
            link(stt(coefA[:, n], modT[:, 24 * n + 8:24 * n + 16, :], 1.0, bc(rowsT[:, g0:g0 + 8], 2, 2), ALU.add,
                     ALU.mult))

        nc.vector.memset(ones[:], 1.0)
        nc.vector.memset(negones[:], -1.0)
        nc.vector.memset(meanw[:], 1.0 / P)
        dve.wait_ge(s_cst, 16)
        ts(negI[:], ident, -1.0, None, ALU.mult)
        nc.vector.memset(epsc[:], EPS).then_inc(s_dch, 1)
        chain[0] += 1
        dve.wait_ge(s_dch, chain[0])
        dve.sem_inc(s_init, 1)
        dve.wait_ge(s_rowsT_ps, 1)
        nc.vector.tensor_copy(rowsT[:, 0:R_N], PS[:, 6, 0:R_N]).then_inc(s_rowsT, 1)
        for n, (t0, w) in enumerate(TILES):
            dve.wait_ge(s_xT, n + 1)
            b = 2 + 2 * (n % 2)
            nc.vector.tensor_copy(hT[:, :, t0:t0 + w],
                                  PS[:, b:b + 2, :].rearrange("p b (k t) -> p (b k) t", t=P)[:, :, 0:w]).then_inc(s_hT, 1)
        def add_squares(st):
            dve.wait_ge(st.sq, 1)
            for k in range(1, KD):
                dve.wait_ge(st.sq, k + 1)
                link(tt(scr1[:, 0, :], scr1[:, 0, :], scr1[:, k, :], ALU.add))
            dve.sem_inc(s_sum, 1)

        add_squares(norms[0])
        dve.wait_ge(norms[0].sd, 1)
        link(nc.vector.reciprocal(rs[:], rs[:]))
        for k in range(KD):
            last = tt(scr2[:, k, :], hT[:, k, :], rs[:], ALU.mult)
        last.then_inc(s_dch, 1)
        chain[0] += 1
        dve.wait_ge(s_adat, 4)
        link(tt(modT[:, 0:16], PS[:, 6, 0:32].rearrange("p (n g) -> p n g", g=2), bc(rowsT[:, R_B:R_B + 16], 2, 2),
                ALU.add))
        coefficients(0)

        def norm1_lo(k):
            dve.wait_ge(norms[0].hi, k + 1)
            tt(XL[:, k, :], scr1[:, k, :], f(XH[:, k, :]), ALU.subtract).then_inc(norms[0].lo, 1)

        for k in range(KD):
            for g, cols in enumerate((slice(0, TP), slice(TP, T))):
                ts(scr1[:, k, cols], scr2[:, k, cols], coefA[:, 0, k, g:g + 1], modT[:, k, g:g + 1], ALU.mult,
                   ALU.add).then_inc(norms[0].y, 1)
            if k == 1:
                for c in range(2):
                    lo(gemms[0], c, 0, c)
            if k >= 2:
                norm1_lo(k - 2)
        norm1_lo(KD - 2)
        norm1_lo(KD - 1)
        gemm_lo(gemms[0], 2)
        dve.wait_ge(s_adat, 12)
        link(tt(modT[:, 16:48], PS[:, 7, 0:64].rearrange("p (n g) -> p n g", g=2), bc(rowsT[:, R_B + 16:R_N], 2, 2),
                ALU.add))
        coefficients(1)
        nc.vector.memset(rvt[:, 4, :], 0.0).then_inc(s_zero, 1)
        nc.vector.memset(svt[:, 4, :], 0.0).then_inc(s_zero, 1)

        dve.wait_ge(s_mixc, 16)
        dve.wait_ge(gemms[0].ev, CREDIT + NIN)
        dve.wait_ge(gemms[0].mm, CREDIT + NIN)
        cosv = bc(mixc[:, M_COS:M_COS + T], 1, 8)
        sinv = bc(mixc[:, M_SIN:M_SIN + T], 1, 8)
        tt(t1[:], projT[:, 0:8, :], cosv, ALU.mult).then_inc(s_rope, 1)
        dve.wait_ge(s_swap, 2)
        tt(sw[:], sw[:], sinv, ALU.mult).then_inc(s_rope, 1)
        dve.wait_ge(s_rope, 2)
        tt(projT[:, 0:8, :], t1[:], sw[:], ALU.add).then_inc(s_rope, 1)
        ts(projT[:, SQ:SQ + NH, :], projT[:, SQ:SQ + NH, :], SCALE, None, ALU.mult).then_inc(s_sqs, 1)
        dve.wait_ge(s_rope, 3)
        tt(qds[:], projT[:, RQ:RQ + NH, TP:T], mixc[:, M_QDEC:M_QDEC + NH * TS].rearrange("p (h t) -> p h t", h=NH),
           ALU.mult).then_inc(s_qds, 1)
        nc.vector.memset(prs[:], 0.0).then_inc(s_qds, 1)
        for b, (t0, w) in enumerate(TILES):
            dve.wait_ge(s_tp, 15 + b + 1)
            tt(rkd[0:w, b, :].rearrange("p (h d) -> p h d", h=NH),
               PS[0:w, (15 + b) % 4, :].rearrange("p (h d) -> p h d", h=NH), bc(kdec(b)[0:w], 2, P),
               ALU.mult).then_inc(s_rkd, 1)
        dve.wait_ge(s_qds, 2)
        gam = [float(np.exp(TS * np.log1p(-np.exp2(-5.0 - h)))) for h in range(NH)]
        for h in range(NH):
            if h >= 2:
                dve.wait_ge(s_ro, h - 1)
            for kb in range(QB):
                w = TP - P * kb
                dve.wait_ge(s_rs_mm, QB * h + kb + 1)
                stt(pr[:, h % 2, pcol(kb):pcol(kb) + w], PS[:, kb, 0:w], SCALE,
                    mixc[:, M_DT + h * TP:M_DT + h * TP + w], ALU.mult, ALU.mult).then_inc(s_rp, 1)
            dve.wait_ge(s_raux, h + 1)
            dve.wait_ge(s_rev, 3 * h + 1)
            stt(prs[0:TS, h, :], PS[0:TS, 6 + h % 2, P:P + TS], SCALE, mixc[0:TS, M_DT + h * TP:M_DT + h * TP + TS],
                ALU.mult, ALU.mult).then_inc(s_rps, 1)
            dve.wait_ge(s_stS, 16)
            stt(stN[:, h, :], stS[:, h, :], gam[h], PS[:, 6 + h % 2, 256:384], ALU.mult, ALU.add).then_inc(s_rsn, 1)
        for h in range(NH):
            dve.wait_ge(s_gm, h + 1)
            tt(halves(projT[:, h, :]), halves(projT[:, h, :]), pair(2 * h), ALU.subtract).then_inc(s_gcen, 1)

        def scaled(h):
            dve.wait_ge(s_gsd, h + 1)
            link(nc.vector.reciprocal(rsb[:, h, :], rsb[:, h, :]))
            link(tt(projT[:, h, :], projT[:, h, :], rsb[:, h, :], ALU.mult))
            dve.wait_ge(s_gate, 1)
            stt(projT[:, h, :], projT[:, h, :], rowsT[:, R_RG + h:R_RG + h + 1], projT[:, RG + h, :], ALU.mult,
                ALU.mult).then_inc(s_gy, 1)

        def masked(h):
            par = h % 2
            dve.wait_ge(s_bln, h + 1)
            for kb in range(QB):
                w = TP - P * kb
                v = lk[:, par, pcol(kb):pcol(kb) + w]
                stt(v, PS[:, 4 * par + kb, 0:w], 0.0, v, ALU.max, ALU.add).then_inc(s_dch, 1)
                chain[0] += 1
            dve.wait_ge(s_dch, chain[0])
            for kb in range(QB):
                v = lk[:, par, pcol(kb):pcol(kb) + P]
                tt(v, v, mask, ALU.mult).then_inc(s_blk, 1)

        def least(h):
            if h >= 1:
                dve.wait_ge(s_bo, h)
            for kb in reversed(range(QB)):
                dve.wait_ge(s_bc, QB * h + QB - kb)
                tt(aw[:, 0, pcol(kb):pcol(kb) + P], PS[:, 4 * (h % 2) + kb, 0:P], mmin, ALU.min).then_inc(s_bmin, 1)

        scaled(0)
        masked(0)
        scaled(1)
        masked(1)
        least(0)
        scaled(2)
        least(1)
        scaled(3)
        masked(2)
        least(2)
        nc.vector.memset(lks[:, NPB, :], 0.0).then_inc(s_zero, 1)
        nc.vector.memset(aws[:, NPB, :], 0.0).then_inc(s_zero, 1)
        masked(3)
        least(3)
        dve.wait_ge(s_cln, 2)
        v8, z8 = lks[0:TS, NPB, :], PS[0:TS, 2, 0:P]
        link(stt(lks[:, 0:NPB, :], PS[:, 0:2, :].rearrange("p b (c x) -> p (b c) x", x=P), 0.0, lks[:, 0:NPB, :],
                 ALU.max, ALU.add),
             stt(v8, z8, 0.0, v8, ALU.max, ALU.add))
        v8h = v8.rearrange("p (h t) -> p h t", h=NH)
        link(tt(v8h, v8h, bc(mask[0:TS, 0:TS], 1, NH), ALU.mult),
             nc.vector.tensor_copy(rsum[:, NPB - 2, :], lks[:, NPB - 1, :]))
        for b in reversed(range(NPB - 2)):
            link(tt(rsum[:, b, :], rsum[:, b + 1, :], lks[:, b + 1, :], ALU.add))
        dve.sem_inc(s_clk, 1)
        dve.wait_ge(s_bo, NH)
        dve.wait_ge(s_out, 96)
        dve.wait_ge(s_ghi, 1)
        tt(XL[:, 0:4, :], projT[:, 0:4, :], f(XH[:, 0:4, :]), ALU.subtract).then_inc(s_glo, 1)
        dve.wait_ge(s_cc, 1)
        tt(aws[0:TS, NPB, :].rearrange("p (h t) -> p h t", h=NH), z8.rearrange("p (h t) -> p h t", h=NH),
           bc(mmin[0:TS, 0:TS], 1, NH), ALU.min).then_inc(s_cmin, 1)
        for c in range(2):
            lo(gemms[1], c, 0, c)
        for h in range(NH):
            dve.wait_ge(s_ghi, 2 + h)
            tt(XL[:, 4 + h, :], projT[:, SQ + h, :], f(XH[:, 4 + h, :]), ALU.subtract).then_inc(s_glo, 1)
        dve.sem_inc(gemms[1].ev, 3 * CREDIT)

        def square(k):
            dve.wait_ge(norms[1].sq, k + 1)
            link(tt(scr1[:, 0, :], scr1[:, 0, :], scr1[:, k, :], ALU.add))

        for c in range(KD):
            dve.wait_ge(gemms[1].mm, c + 1 + CREDIT)
            for b, t0, n, g in ((0, 0, HT, 0), (1, HT, TP - HT, 0), (1, TP, TS, 1)):
                stt(hT[:, c, t0:t0 + n], PS[:, 2 * (c % 2) + b, t0 - b * HT:t0 - b * HT + n], modT[:, 16 + c, g:g + 1],
                    hT[:, c, t0:t0 + n], ALU.mult, ALU.add).then_inc(gemms[1].ev, 1)
            if c + 2 < KD:
                lo(gemms[1], c + 2, (c + 2) // 4, (c + 2) % 4)
            if c >= 2:
                square(c - 1)
        square(KD - 1)
        dve.sem_inc(s_sum, 1)
        dve.wait_ge(norms[1].sd, 1)
        link(nc.vector.reciprocal(rs[:], rs[:]))

        def norm2_lo(k):
            dve.wait_ge(norms[1].hi, 2 * k + 2)
            for g, cols in enumerate((slice(0, TP), slice(TP, T))):
                stt(XL[:, k, cols], scr2[:, k, cols], modT[:, 24 + k, g:g + 1], f(XH[:, k, cols]), ALU.add,
                    ALU.subtract).then_inc(norms[1].lo, 1)

        for k in range(KD):
            for g, cols in enumerate((slice(0, TP), slice(TP, T))):
                stt(scr2[:, k, cols], hT[:, k, cols], coefA[:, 1, k, g:g + 1], rs[:, cols], ALU.mult, ALU.mult
                    ).then_inc(norms[1].tmp, 1)
            if k == 1:
                for c in range(2):
                    lo(gemms[2], c, 0, c)
            if k >= 2:
                norm2_lo(k - 2)
        norm2_lo(KD - 2)
        norm2_lo(KD - 1)
        gemm_lo(gemms[2], 2)

        dve.wait_ge(gemms[2].ev, CREDIT + 16)
        nc.vector.tensor_copy(iotaE[:], bc(iota, 2, OG)).then_inc(s_dch, 1)
        chain[0] += 1
        dve.wait_ge(s_dch, chain[0])

        def choose(n, w, per):
            count = [0]

            def step(*ins):
                for x in ins:
                    count[0] += 1
                    x.then_inc(s_cch, 1)
                dve.wait_ge(s_cch, per * n + count[0])
                if not isinstance(n, int):
                    dve.sem_inc(s_vpass, 1)

            dve.wait_ge(s_scev, 4 * n + 4)
            if not isinstance(n, int):
                dve.sem_inc(s_vpass, 1)
            r = slice(0, w)
            lo8, hi8 = slice(0, 8), slice(8, 16)
            step(*[nc.vector.max(val[r, hp, lo8], S[r, hp, :]) for hp in range(16)])
            step(*[nc.vector.match_replace(S2[r, hp, :], val[r, hp, lo8], S[r, hp, :], -3.0e38) for hp in range(16)])
            step(*[nc.vector.max(val[r, hp, hi8], S2[r, hp, :]) for hp in range(16)])
            step(*[nc.vector.max_index(ind[r, hp, lo8], val[r, hp, lo8], S[r, hp, :]) for hp in range(16)],
                 *[nc.vector.max_index(ind[r, hp, hi8], val[r, hp, hi8], S2[r, hp, :]) for hp in range(16)])
            va = val[r].rearrange("p (h a) k -> p h a k", a=2)
            cv = cand[r].rearrange("p h (a b) -> p h a b", a=TOPK)
            step(nc.vector.tensor_copy(indf[r], ind[r]),
                 *[tt(cv[:, h], bc(va[:, h, 0, :], 2, TOPK), bc(va[:, h, 1, :], 1, TOPK), ALU.add) for h in range(PH)])
            step(*[nc.vector.max(tops[r, h, lo8], cand[r, h, :]) for h in range(PH)])
            step(*[nc.vector.match_replace(cand2[r, h, :], tops[r, h, lo8], cand[r, h, :], -3.0e38) for h in range(PH)])
            step(*[nc.vector.max(tops[r, h, hi8], cand2[r, h, :]) for h in range(PH)])
            step(*[nc.vector.max_index(pos[r, h, lo8], tops[r, h, lo8], cand[r, h, :]) for h in range(PH)],
                 *[nc.vector.max_index(pos[r, h, hi8], tops[r, h, hi8], cand2[r, h, :]) for h in range(PH)])
            step(nc.vector.tensor_copy(sm[r, 0, :], tops[r, :, 0]),
                 ts(posa[r], pos[r], 4, None, ALU.logical_shift_right))
            step(tt(tops[r], tops[r], bc(sm[r, 0, :], 2, TOPK), ALU.subtract),
                 nc.vector.tensor_copy(posf[r, 0], posa[r]))
            dve.sem_inc(s_exd, 1)
            step(ts(posa[r], pos[r], 15, None, ALU.bitwise_and))
            step(nc.vector.tensor_copy(posf[r, 1], posa[r]))
            for side in range(2):
                step(tt(eq[r], bc(posf[r, side].rearrange("p h k -> p (h k)"), 2, TOPK),
                        bc(iota[r, 0:TOPK], 1, PH * TOPK), ALU.is_equal))
                ev = eq[r].rearrange("p (h k) a -> p h k a", h=PH)
                iv = indf[r].rearrange("p (h a) k -> p h a k", a=2)
                step(*[tt(ev[:, h], ev[:, h], bc(iv[:, h, side, :], 1, TOPK), ALU.mult) for h in range(PH)])
                step(nc.vector.tensor_reduce(sel[r, side, :], eq[r], AX_X, ALU.add))
            dve.wait_ge(s_exa, n + 1)
            step(nc.vector.tensor_reduce(sm[r, 1, :], ex[r], AX_X, ALU.add))
            step(nc.vector.reciprocal(sm[r, 0, :], sm[r, 1, :]))
            step(tt(sel[r, 2, :].rearrange("p (h k) -> p h k", h=PH), ex[r], bc(sm[r, 0, :], 2, TOPK), ALU.mult))
            dve.sem_inc(s_sel, 1)
            dve.wait_ge(s_selTe, n + 1)
            step(nc.vector.tensor_copy(keyb[:, :, 0:w], selT[:, 0:2, 0:w]),
                 nc.vector.tensor_copy(gb[:, 0, 0:w], selT[:, 2, 0:w]))
            step(tt(gres[:, 0, 0:w], selT[:, 2, 0:w], gb[:, 0, 0:w], ALU.subtract))
            step(nc.vector.tensor_copy(gb[:, 1, 0:w], gres[:, 0, 0:w]))
            step(tt(gres[:, 1, 0:w], gres[:, 0, 0:w], gb[:, 1, 0:w], ALU.subtract))
            step(nc.vector.tensor_copy(gb[:, 2, 0:w], gres[:, 1, 0:w]))
            for g in range(w // OG):
                gi = NG * n + g
                sl, cols = g % 2, slice(OG * g, OG * (g + 1))
                if g >= 2 or not isinstance(n, int) or n >= 1:
                    dve.wait_ge(s_gmm, 2 * gi - 2)
                tt(ohA[:, sl], iotaE[:], bc(keyb[:, 1, cols], 1, P), ALU.is_equal)
                step(tt(eqb[:], iotaE[:], bc(keyb[:, 0, cols], 1, P), ALU.is_equal))
                for part in range(3):
                    last = tt(ohB[:, part, sl], eqb[:], bc(gb[:, part, cols], 1, P), ALU.mult)
                last.then_inc(s_oh, 1)
                dve.wait_ge(s_oh, gi + 1)
            return count[0]

        per = choose(0, P, 0)
        with dve.Fori(1, 4) as n:
            again = choose(n, P, per)
        assert again == per
        choose(4, TS, per)

        dve.wait_ge(s_gev, CREDIT + 8 * 17)
        dve.wait_ge(s_gout[0], 16 * 9)
        dve.wait_ge(s_gout[1], 16 * 8)
        link(nc.vector.memset(acc[:], 0.0))
        dve.sem_inc(s_add, 4)

        def u_lo(m, par):
            dve.wait_ge(s_uth, m + 1)
            tt(utl[:, par], PS[:, 0:2, :].rearrange("p b (k i) -> p (b k) i", i=P), f(uth[:, par]),
               ALU.subtract).then_inc(s_utl, 1)

        def v_lo(t, r, par):
            dve.wait_ge(s_vh, t + 1)
            tt(vl[:, par, r, :], vrw[:, par, r, :], f(vh[:, par, r, :]), ALU.subtract).then_inc(s_vl, 1)

        def gate(t, r, par, src, blk, j):
            if not isinstance(t, int) or t >= 2:
                dve.wait_ge(s_wh, t - 1)
                dve.wait_ge(s_wl, t - 1)
            tt(wv[:, r, :], src, G[:, blk, :, j], ALU.mult).then_inc(s_wv, 1)

        def w_lo(t, r, par):
            dve.wait_ge(s_wh, t + 1)
            tt(wl[:, par, r, :], wv[:, r, :], f(wh[:, par, r, :]), ALU.subtract).then_inc(s_wl, 1)

        def add(pr_, n):
            dve.wait_ge(s_om, 16 * pr_ + n + 1)
            if not isinstance(pr_, int) or pr_ >= 1:
                dve.wait_ge(s_add, 16 * pr_ + n - 12 + 4)
            a = acc[:, n // 2, (n % 2) * HT:(n % 2 + 1) * HT]
            tt(a, a, PS[:, 4 + n % 4, 0:HT], ALU.add).then_inc(s_add, 1)

        def iteration(i, first, last):
            for q in range(4):
                pr_, par, blk, j = 4 * i + q, q % 2, q // 2, 2 * (q % 2)
                adds = not (first and q == 0)
                if j == 0:
                    dve.wait_ge(s_g[blk], 16 * i + 16)
                dve.wait_ge(s_al[par], 32 * i + 16 * (q // 2) + 16)
                gate(2 * pr_, 0, par, al[:, par, :], blk, j)
                v_lo(2 * pr_, 0, par)
                w_lo(2 * pr_, 0, par)
                dve.wait_ge(s_gel, 2 * (NU + pr_) + 2)
                gate(2 * pr_ + 1, 1, par, gel[:, par, :], blk, j + 1)
                if adds:
                    add(pr_ - 1, 0)
                if not (last and q == 3):
                    u_lo(NU + pr_ + 1, 1 - par)
                for n in range(1, 5) if adds else ():
                    add(pr_ - 1, n)
                w_lo(2 * pr_ + 1, 1, par)
                for n in range(5, 8) if adds else ():
                    add(pr_ - 1, n)
                v_lo(2 * pr_ + 1, 1, par)
                for n in range(8, 16) if adds else ():
                    add(pr_ - 1, n)

        iteration(0, True, False)
        with dve.Fori(1, 15) as i:
            iteration(i, False, False)
        iteration(15, False, True)
        def residual(k):
            dve.wait_ge(s_add, 4 + 16 * 63 + 2 * k + 2)
            for g, cols in enumerate((slice(0, TP), slice(TP, T))):
                stt(hT[:, k, cols], acc[:, k, cols], modT[:, 40 + k, g:g + 1], hT[:, k, cols], ALU.mult, ALU.add
                    ).then_inc(s_h2, 1)

        for n in range(16):
            add(63, n)
            if n >= 2 and n % 2 == 0:
                residual(n // 2 - 1)
        residual(KD - 1)
        dve.wait_ge(norms[2].sd, 1)
        link(nc.vector.reciprocal(rs[:], rs[:]))
        for k in range(KD):
            stt(scr2[:, k, :], hT[:, k, :], rowsT[:, R_FG + k:R_FG + k + 1], rs[:], ALU.mult, ALU.mult
                ).then_inc(norms[2].y, 1)

    ctx.close()


def pcol(kb):
    return sum(TP - P * n for n in range(kb))


_INS = ['x_prompt', 'x_sample', 'c_prompt', 'c_sample', 'state_ret', 'cache_sb_k', 'cache_sb_v', 'w_ada', 'b_ada',
        'norm1_g', 'w_in', 'ret_norm_g', 'w_out', 'norm2_g', 'peer_w_query', 'peer_sub_keys', 'peer_u', 'peer_v',
        'final_norm_g']
_OUTS = [(1, TP, D), (1, TS, D), (1, 1, NH, P, P), (1, 1, TP, NH, P), (1, 1, TP, NH, P), (1, 1, NH, P, P),
         (1, 1, TS, NH, P), (1, 1, TS, NH, P)]


def kernel(**inputs):
    import concourse.bacc as _bacc
    from concourse.bass_utils import run_bass_kernel_spmd as _run

    nc = _bacc.Bacc("TRN2", target_bir_lowering=False, num_devices=1)
    small, mix = shape_constants()
    arrays, args = {}, []
    for name, a in [(n, np.ascontiguousarray(inputs[n])) for n in _INS] + [("small", small), ("mix", mix)]:
        arrays[f"in_{name}_dram"] = a
        args.append(nc.dram_tensor(f"in_{name}_dram", a.shape, mybir.dt.from_np(a.dtype), kind="ExternalInput").ap())
    args.append(nc.dram_tensor("gates_dram", (P, NJB, T, JB), F32, kind="Internal").ap())
    args.append(nc.dram_tensor("acts_dram", (P, NU, T), F32, kind="Internal").ap())
    for i, shape in enumerate(_OUTS):
        args.append(nc.dram_tensor(f"out_{i}_dram", shape, F32, kind="ExternalOutput").ap())
    build(nc, *args)
    r = _run(nc, [arrays], core_ids=[0])
    return tuple(r.results[0][f"out_{i}_dram"] for i in range(len(_OUTS)))
```
